# Optimizing a Trainium2 kernel written in Bass

```python
import math
import jax
import jax.numpy as jnp
from jax import lax
import numpy as np

D_MODEL = 1024
BATCH = 1
SEQ = 128
DEPTH = 2
DEC_BATCH = 1
DEC_SEQ = 512
PAST_LEN = 256

GRID_W = 64
HEAD_DIM = 64
RET_HEADS = 4
RWKV_HEADS = 8
MLSTM_HEADS = 4
RET_W = RET_HEADS * HEAD_DIM
RWKV_W = RWKV_HEADS * HEAD_DIM
MLSTM_W = MLSTM_HEADS * HEAD_DIM
MIX_W = RET_W + RWKV_W + MLSTM_W
RWKV_DECAY_RANK = 64
RWKV_A_RANK = 64
RWKV_GATE_RANK = 128
MLSTM_GATES = 2 * 2 * MLSTM_HEADS
RET_IN = 4 * RET_W
RWKV_IN = 3 * RWKV_W + RWKV_DECAY_RANK + RWKV_A_RANK + RWKV_GATE_RANK
MLSTM_IN = 4 * MLSTM_W + MLSTM_GATES
IN_COLS = RET_IN + RWKV_IN + MLSTM_IN
CHUNK = 128
ROPE_BASE = 10000.0
PEER_HEADS = 8
PEER_NKEYS = 128
PEER_EXPERTS = PEER_NKEYS * PEER_NKEYS
PEER_QDIM = 256
PEER_HALF = PEER_QDIM // 2
PEER_TOPK = 16
PEER_BLOCK = 128
DEEPNORM_ALPHA = (2 * DEPTH) ** 0.25
DEEPNORM_BETA = (8 * DEPTH) ** -0.25
LN_EPS = 1e-5

kernel_name = 'hybrid_ret_rwkv7_mlstm_peer_dit_step'

def split_cols(x, sizes):
    offs = [int(o) for o in np.cumsum(sizes)[:-1]]
    return jnp.split(x, offs, axis=-1)

def layer_norm(x, gain_bias=None):
    xf = x.astype(jnp.float32)
    mu = jnp.mean(xf, -1, keepdims=True)
    var = jnp.mean(jnp.square(xf - mu), -1, keepdims=True)
    y = (xf - mu) * lax.rsqrt(var + LN_EPS)
    if gain_bias is not None:
        y = y * gain_bias[0] + gain_bias[1]
    return y

def head_norm(y, gain_bias):
    B, T, H, d = y.shape
    mu = jnp.mean(y, -1, keepdims=True)
    var = jnp.mean(jnp.square(y - mu), -1, keepdims=True)
    yn = ((y - mu) * lax.rsqrt(var + LN_EPS)).reshape(B, T, H * d)
    return yn * gain_bias[0] + gain_bias[1]

def to_heads(a, n_heads):
    return a.reshape(a.shape[0], a.shape[1], n_heads, HEAD_DIM)

def flip_t(a):
    return jnp.flip(a, axis=1)

def to_chunks(a):
    B, T = a.shape[0], a.shape[1]
    a = a.reshape((B, T // CHUNK, CHUNK) + a.shape[2:])
    return jnp.moveaxis(jnp.moveaxis(a, 1, 0), 2, 3)

def from_chunks(a):
    a = jnp.moveaxis(jnp.moveaxis(a, 3, 2), 0, 1)
    return a.reshape((a.shape[0], a.shape[1] * a.shape[2]) + a.shape[3:])

def centred_conv3(x, w):
    xp = jnp.pad(x, ((0, 0), (1, 1), (0, 0)))
    return w[0] * xp[:, :-2] + w[1] * xp[:, 1:-1] + w[2] * xp[:, 2:]

def centred_shift(x):
    xp = jnp.pad(x, ((0, 0), (1, 1), (0, 0)))
    return 0.5 * (xp[:, :-2] + xp[:, 2:])

def axial_rope(x, rows):
    f32 = jnp.float32
    nf = HEAD_DIM // 4
    inv = ROPE_BASE ** (-jnp.arange(nf, dtype=f32) / nf)
    row_pos = jnp.repeat(jnp.arange(rows, dtype=f32), GRID_W)
    col_pos = jnp.tile(jnp.arange(GRID_W, dtype=f32), rows)
    ang = jnp.concatenate([row_pos[:, None] * inv, col_pos[:, None] * inv], -1)
    cos = jnp.cos(ang)[None, :, None, :]
    sin = jnp.sin(ang)[None, :, None, :]
    x1, x2 = jnp.split(x, 2, axis=-1)
    return jnp.concatenate([x1 * cos - x2 * sin, x1 * sin + x2 * cos], -1)

def retention_chunked(q, k, v, log_gamma, s0):
    pos = jnp.arange(CHUNK, dtype=jnp.float32)
    diff = pos[:, None] - pos[None, :]
    intra = jnp.where(diff >= 0, jnp.exp(log_gamma[:, None, None] * jnp.maximum(diff, 0.0)), 0.0)
    q_dec = jnp.exp(log_gamma[:, None] * (pos + 1.0))[:, :, None]
    k_dec = jnp.exp(log_gamma[:, None] * (CHUNK - 1.0 - pos))[:, :, None]
    c_dec = jnp.exp(log_gamma * CHUNK)[:, None, None]

    def step(s, inp):
        qc, kc, vc = inp
        scores = jnp.einsum('bhld,bhmd->bhlm', qc, kc) * intra
        o = jnp.einsum('bhlm,bhme->bhle', scores, vc) + jnp.einsum('bhld,bhde->bhle', qc * q_dec, s)
        s = s * c_dec + jnp.einsum('bhmd,bhme->bhde', kc * k_dec, vc)
        return s, o

    s, o = lax.scan(step, s0, (to_chunks(q), to_chunks(k), to_chunks(v)))
    return from_chunks(o), s

def rwkv7_scan(r, w, k, v, kk, b, s0):
    def step(S, inp):
        r_t, w_t, k_t, v_t, kk_t, b_t = inp
        sa = -jnp.einsum('bhij,bhj->bhi', S, kk_t)
        S = S * w_t[:, :, None, :] + sa[..., :, None] * b_t[..., None, :] + v_t[..., :, None] * k_t[..., None, :]
        return S, jnp.einsum('bhij,bhj->bhi', S, r_t)

    xs = tuple(jnp.moveaxis(a, 1, 0) for a in (r, w, k, v, kk, b))
    S, y = lax.scan(step, s0, xs)
    return jnp.moveaxis(y, 0, 1), S

def mlstm_chunked(q, k, v, i_pre, log_f, c0, n0, m0):
    tri = jnp.tril(jnp.ones((CHUNK, CHUNK), dtype=bool))

    def step(carry, inp):
        C, n, m = carry
        qc, kc, vc, ic, fc = inp
        b = jnp.cumsum(fc, axis=-1)
        logw = jnp.where(tri, b[..., :, None] - b[..., None, :] + ic[..., None, :], -jnp.inf)
        inter = b + m[..., None]
        m_t = jnp.maximum(inter, jnp.max(logw, axis=-1))
        w = jnp.exp(logw - m_t[..., None])
        sc = jnp.einsum('bhld,bhsd->bhls', qc, kc) * w
        ws = jnp.exp(inter - m_t)
        num = jnp.einsum('bhls,bhse->bhle', sc, vc) + ws[..., None] * jnp.einsum('bhld,bhde->bhle', qc, C)
        den = jnp.sum(sc, -1) + ws * jnp.einsum('bhld,bhd->bhl', qc, n)
        h = num / jnp.maximum(jnp.abs(den), jnp.exp(-m_t))[..., None]
        b_last = b[..., -1]
        logu = b_last[..., None] - b + ic
        m_new = jnp.maximum(b_last + m, jnp.max(logu, axis=-1))
        u = jnp.exp(logu - m_new[..., None])
        carry_scale = jnp.exp(b_last + m - m_new)
        C = carry_scale[..., None, None] * C + jnp.einsum('bhs,bhsd,bhse->bhde', u, kc, vc)
        n = carry_scale[..., None] * n + jnp.einsum('bhs,bhsd->bhd', u, kc)
        return (C, n, m_new), h

    xs = tuple(to_chunks(a) for a in (q, k, v, i_pre, log_f))
    (C, n, m), h = lax.scan(step, (c0, n0, m0), xs)
    return from_chunks(h), C, n, m

def token_mixers(h, p, st, rows):
    f32 = jnp.float32
    B, T, _ = h.shape
    st_ret, st_rwkv, st_c, st_n, st_m = st
    proj = jnp.einsum('btd,dc->btc', h, p['w_in']).astype(f32)
    ret_p, rwkv_p, ml_p = split_cols(proj, [RET_IN, RWKV_IN, MLSTM_IN])

    q, k, v, g = split_cols(ret_p, [RET_W] * 4)
    q, k, v = (to_heads(a, RET_HEADS) for a in (q, k, v))
    if rows is not None:
        q, k = axial_rope(q, rows), axial_rope(k, rows)
    k = k * HEAD_DIM ** -0.5
    log_gamma = -jnp.exp(p['ret_decay'].astype(f32))
    y_f, s_f = retention_chunked(q, k, v, log_gamma[0], st_ret[:, 0])
    y_b, s_b = retention_chunked(flip_t(q), flip_t(k), flip_t(v), log_gamma[1], st_ret[:, 1])
    out_ret = jax.nn.silu(g) * head_norm(y_f + flip_t(y_b), p['ret_gn'])

    rwkv_p = rwkv_p + p['rwkv_mu'] * (centred_shift(rwkv_p) - rwkv_p)
    r, k, v, w_low, a_low, g_low = split_cols(
        rwkv_p, [RWKV_W] * 3 + [RWKV_DECAY_RANK, RWKV_A_RANK, RWKV_GATE_RANK])
    kk = to_heads(k * p['rwkv_kk'], RWKV_HEADS)
    kk = kk / jnp.maximum(jnp.sqrt(jnp.sum(kk * kk, -1, keepdims=True)), 1e-12)
    rh = to_heads(r, RWKV_HEADS)
    vh = to_heads(v, RWKV_HEADS)
    w_lora = jnp.tanh(w_low)
    ys, ss = [], []
    for d in range(2):
        w_log = -jax.nn.softplus(-(p['rwkv_w0'][d] + w_lora @ p['rwkv_w_up'][d])) - 0.5
        decay = to_heads(jnp.exp(-jnp.exp(w_log)), RWKV_HEADS)
        a = jax.nn.sigmoid(p['rwkv_a0'][d] + a_low @ p['rwkv_a_up'][d])
        k_rep = to_heads(k * (1.0 + (a - 1.0) * p['rwkv_ka']), RWKV_HEADS)
        b_rem = kk * to_heads(a, RWKV_HEADS)
        seqs = (rh, decay, k_rep, vh, kk, b_rem)
        if d == 1:
            seqs = tuple(flip_t(s) for s in seqs)
        y_d, s_d = rwkv7_scan(*seqs, st_rwkv[:, d])
        ys.append(y_d if d == 0 else flip_t(y_d))
        ss.append(s_d)
    bonus = jnp.sum(rh * to_heads(k, RWKV_HEADS) * p['rwkv_rk'].reshape(RWKV_HEADS, HEAD_DIM),
                    -1, keepdims=True) * vh
    gate = jax.nn.sigmoid(g_low) @ p['rwkv_g_up']
    out_rwkv = (head_norm(ys[0] + ys[1], p['rwkv_gn']) + bonus.reshape(B, T, RWKV_W)) * gate

    q, k, v, o, gates = split_cols(ml_p, [MLSTM_W] * 4 + [MLSTM_GATES])
    qk = jax.nn.silu(centred_conv3(jnp.concatenate([q, k], -1), p['mlstm_conv']))
    q, k = jnp.split(qk, 2, axis=-1)
    q, k, v = (to_heads(a, MLSTM_HEADS) for a in (q, k, v))
    k = k * HEAD_DIM ** -0.5
    gates = gates.reshape(B, T, 2, 2, MLSTM_HEADS) + p['mlstm_gate_bias']
    i_pre = gates[:, :, :, 0]
    log_f = jax.nn.log_sigmoid(gates[:, :, :, 1])
    h_f, c_f, n_f, m_f = mlstm_chunked(q, k, v, i_pre[:, :, 0], log_f[:, :, 0],
                                       st_c[:, 0], st_n[:, 0], st_m[:, 0])
    h_b, c_b, n_b, m_b = mlstm_chunked(flip_t(q), flip_t(k), flip_t(v), flip_t(i_pre[:, :, 1]),
                                       flip_t(log_f[:, :, 1]), st_c[:, 1], st_n[:, 1], st_m[:, 1])
    out_ml = jax.nn.sigmoid(o) * head_norm(h_f + flip_t(h_b), p['mlstm_gn'])

    mix = jnp.concatenate([out_ret, out_rwkv, out_ml], -1) @ p['w_out']
    new_st = (jnp.stack([s_f, s_b], 1), jnp.stack(ss, 1), jnp.stack([c_f, c_b], 1),
              jnp.stack([n_f, n_b], 1), jnp.stack([m_f, m_b], 1))
    return mix, new_st

def peer_ffn(h, wq, keys, u, v):
    B, T, D = h.shape
    ntok = B * T
    x = h.reshape(ntok, D)
    q = (x @ wq).astype(jnp.float32).reshape(ntok, PEER_HEADS, 2, PEER_HALF)
    scores = jnp.einsum('nhpd,hpkd->nhpk', q, keys.astype(jnp.float32))
    sub_val, sub_idx = lax.top_k(scores, PEER_TOPK)
    cand = (sub_val[:, :, 0, :, None] + sub_val[:, :, 1, None, :]).reshape(
        ntok, PEER_HEADS, PEER_TOPK * PEER_TOPK)
    top_val, top_pos = lax.top_k(cand, PEER_TOPK)
    e1 = jnp.take_along_axis(sub_idx[:, :, 0], top_pos // PEER_TOPK, axis=-1)
    e2 = jnp.take_along_axis(sub_idx[:, :, 1], top_pos % PEER_TOPK, axis=-1)
    expert = e1 * PEER_NKEYS + e2
    g = jax.nn.softmax(top_val, axis=-1)

    def block(args):
        xb, eb, gb = args
        act = jax.nn.gelu(jnp.einsum('nd,nhkd->nhk', xb, u[eb]), approximate=False)
        return jnp.einsum('nhk,nhkd->nd', gb * act, v[eb])

    nblk = ntok // PEER_BLOCK
    out = lax.map(block, (x.reshape(nblk, PEER_BLOCK, D),
                          expert.reshape(nblk, PEER_BLOCK, PEER_HEADS, PEER_TOPK),
                          g.reshape(nblk, PEER_BLOCK, PEER_HEADS, PEER_TOPK)))
    return out.reshape(B, T, D).astype(jnp.float32)

def trunk_layer(x, cond, p, st, rows):
    mod = jax.nn.silu(cond.astype(jnp.float32)) @ p['w_mod'] + p['b_mod']
    sh1, sc1, g1, sh2, sc2, g2 = jnp.split(mod[:, None, :], 6, axis=-1)
    h = layer_norm(x) * (1.0 + sc1) + sh1
    mix, new_st = token_mixers(h, p, st, rows)
    x = layer_norm(DEEPNORM_ALPHA * x + g1 * mix, p['ln1'])
    h = layer_norm(x) * (1.0 + sc2) + sh2
    ffn = peer_ffn(h, p['peer_wq'], p['peer_keys'], p['peer_u'], p['peer_v'])
    x = layer_norm(DEEPNORM_ALPHA * x + g2 * ffn, p['ln2'])
    return x, new_st

def setup_inputs(seed: int = 0) -> dict:
    key = jax.random.key(seed)
    ks = list(jax.random.split(key, 40))
    f32 = jnp.float32
    D = D_MODEL

    def nrm(i, shape, scale=1.0):
        return scale * jax.random.normal(ks[i], shape, f32)

    def gain_bias(i, width):
        return jnp.array([1.0, 0.0], f32)[None, :, None] + nrm(i, (DEPTH, 2, width), 0.02)

    gamma0 = 1.0 - 2.0 ** (-5.0 - jnp.arange(RET_HEADS, dtype=f32))
    ret_base = jnp.log(-jnp.log(gamma0))
    gate_bias = jnp.concatenate(
        [nrm(30, (DEPTH, 2, 1, MLSTM_HEADS), 0.1),
         jnp.linspace(3.0, 6.0, MLSTM_HEADS, dtype=f32) + nrm(31, (DEPTH, 2, 1, MLSTM_HEADS), 0.1)], axis=2)
    return {
        'x_prompt': nrm(0, (BATCH, SEQ, D)),
        'x_sample': nrm(1, (DEC_BATCH, DEC_SEQ, D)),
        'c': nrm(2, (DEC_BATCH, D)),
        'state_ret': nrm(3, (DEC_BATCH, DEPTH, 2, RET_HEADS, HEAD_DIM, HEAD_DIM), 0.3),
        'state_rwkv': nrm(4, (DEC_BATCH, DEPTH, 2, RWKV_HEADS, HEAD_DIM, HEAD_DIM), 0.3),
        'state_mlstm_c': nrm(5, (DEC_BATCH, DEPTH, 2, MLSTM_HEADS, HEAD_DIM, HEAD_DIM), 0.3),
        'state_mlstm_n': nrm(6, (DEC_BATCH, DEPTH, 2, MLSTM_HEADS, HEAD_DIM), 0.3),
        'state_mlstm_m': nrm(7, (DEC_BATCH, DEPTH, 2, MLSTM_HEADS), 0.5),
        'c_ctx': nrm(8, (D,)),
        'w_mod': nrm(9, (DEPTH, D, 6 * D), D ** -0.5),
        'b_mod': nrm(10, (DEPTH, 6 * D), 0.02),
        'w_in': nrm(11, (DEPTH, D, IN_COLS), D ** -0.5),
        'w_out': nrm(12, (DEPTH, MIX_W, D), DEEPNORM_BETA * MIX_W ** -0.5),
        'ret_decay': ret_base + nrm(13, (DEPTH, 2, RET_HEADS), 0.1),
        'ret_gn': gain_bias(14, RET_W),
        'rwkv_mu': jax.random.uniform(ks[15], (DEPTH, RWKV_IN), f32, 0.2, 0.8),
        'rwkv_w0': jax.random.uniform(ks[16], (DEPTH, 2, RWKV_W), f32, -6.0, 0.0),
        'rwkv_w_up': nrm(17, (DEPTH, 2, RWKV_DECAY_RANK, RWKV_W), 0.1 * RWKV_DECAY_RANK ** -0.5),
        'rwkv_a0': nrm(18, (DEPTH, 2, RWKV_W), 0.1),
        'rwkv_a_up': nrm(19, (DEPTH, 2, RWKV_A_RANK, RWKV_W), 0.1 * RWKV_A_RANK ** -0.5),
        'rwkv_g_up': nrm(20, (DEPTH, RWKV_GATE_RANK, RWKV_W), RWKV_GATE_RANK ** -0.5),
        'rwkv_kk': 0.85 + nrm(21, (DEPTH, RWKV_W), 0.02),
        'rwkv_ka': 1.0 + nrm(22, (DEPTH, RWKV_W), 0.02),
        'rwkv_rk': nrm(23, (DEPTH, RWKV_W), 0.1),
        'rwkv_gn': gain_bias(24, RWKV_W),
        'mlstm_conv': nrm(25, (DEPTH, 3, 2 * MLSTM_W), 3 ** -0.5),
        'mlstm_gate_bias': gate_bias,
        'mlstm_gn': gain_bias(26, MLSTM_W),
        'ln1': gain_bias(27, D),
        'ln2': gain_bias(28, D),
        'peer_wq': nrm(29, (DEPTH, D, PEER_HEADS * PEER_QDIM), D ** -0.5),
        'peer_keys': nrm(32, (DEPTH, PEER_HEADS, 2, PEER_NKEYS, PEER_HALF), PEER_HALF ** -0.5),
        'peer_u': nrm(33, (DEPTH, PEER_EXPERTS, D), D ** -0.5),
        'peer_v': nrm(34, (DEPTH, PEER_EXPERTS, D), DEEPNORM_BETA),
    }

def reference(x_prompt, x_sample, c, state_ret, state_rwkv, state_mlstm_c, state_mlstm_n, state_mlstm_m,
              c_ctx, w_mod, b_mod, w_in, w_out, ret_decay, ret_gn, rwkv_mu, rwkv_w0, rwkv_w_up, rwkv_a0,
              rwkv_a_up, rwkv_g_up, rwkv_kk, rwkv_ka, rwkv_rk, rwkv_gn, mlstm_conv, mlstm_gate_bias,
              mlstm_gn, ln1, ln2, peer_wq, peer_keys, peer_u, peer_v):
    f32 = jnp.float32
    rows = x_sample.shape[1] // GRID_W
    bp = x_prompt.shape[0]
    xp = x_prompt.astype(f32)
    xs = x_sample.astype(f32)
    ctx_cond = c_ctx[None, :]
    zero_st = (jnp.zeros((bp, 2, RET_HEADS, HEAD_DIM, HEAD_DIM), f32),
               jnp.zeros((bp, 2, RWKV_HEADS, HEAD_DIM, HEAD_DIM), f32),
               jnp.zeros((bp, 2, MLSTM_HEADS, HEAD_DIM, HEAD_DIM), f32),
               jnp.zeros((bp, 2, MLSTM_HEADS, HEAD_DIM), f32),
               jnp.zeros((bp, 2, MLSTM_HEADS), f32))
    caches = (state_ret, state_rwkv, state_mlstm_c, state_mlstm_n, state_mlstm_m)
    new_lists = ([], [], [], [], [])
    for l in range(DEPTH):
        p = {'w_mod': w_mod[l], 'b_mod': b_mod[l], 'w_in': w_in[l], 'w_out': w_out[l],
             'ret_decay': ret_decay[l], 'ret_gn': ret_gn[l], 'rwkv_mu': rwkv_mu[l],
             'rwkv_w0': rwkv_w0[l], 'rwkv_w_up': rwkv_w_up[l], 'rwkv_a0': rwkv_a0[l],
             'rwkv_a_up': rwkv_a_up[l], 'rwkv_g_up': rwkv_g_up[l], 'rwkv_kk': rwkv_kk[l],
             'rwkv_ka': rwkv_ka[l], 'rwkv_rk': rwkv_rk[l], 'rwkv_gn': rwkv_gn[l],
             'mlstm_conv': mlstm_conv[l], 'mlstm_gate_bias': mlstm_gate_bias[l], 'mlstm_gn': mlstm_gn[l],
             'ln1': ln1[l], 'ln2': ln2[l], 'peer_wq': peer_wq[l], 'peer_keys': peer_keys[l],
             'peer_u': peer_u[l], 'peer_v': peer_v[l]}
        xp, st_new = trunk_layer(xp, ctx_cond, p, zero_st, None)
        for lst, s in zip(new_lists, st_new):
            lst.append(s)
        cache_l = tuple(s[:, l].astype(f32) for s in caches)
        xs, _ = trunk_layer(xs, c, p, cache_l, rows)
    new_ret = jnp.stack(new_lists[0], axis=1).astype(x_prompt.dtype)
    new_rwkv = jnp.stack(new_lists[1], axis=1).astype(x_prompt.dtype)
    new_mc = jnp.stack(new_lists[2], axis=1).astype(x_prompt.dtype)
    new_mn = jnp.stack(new_lists[3], axis=1).astype(x_prompt.dtype)
    new_mm = jnp.stack(new_lists[4], axis=1).astype(x_prompt.dtype)
    return (xp.astype(x_prompt.dtype), xs.astype(x_sample.dtype), new_ret, new_rwkv, new_mc, new_mn, new_mm)


_drawn_inputs = setup_inputs


def setup_inputs(seed=0):
    import zlib

    import numpy as np

    out = dict(_drawn_inputs(seed))
    spreads = {}
    factors = {'state_ret': 3.912,
     'state_rwkv': 3.864,
     'state_mlstm_c': 5.199,
     'state_mlstm_n': 32.941,
     'state_mlstm_m': 22.673,
     'rwkv_w_up': 3.944}
    for name, (base, spread) in spreads.items():
        noise = np.random.default_rng([zlib.crc32(name.encode()), seed]).standard_normal(out[name].shape)
        drawn = base * np.exp(spread * noise) if base else spread * noise
        out[name] = jnp.asarray(drawn.astype(out[name].dtype))
    for name, factor in factors.items():
        out[name] = (out[name] * factor).astype(out[name].dtype)
    return out
```

```python
from contextlib import ExitStack

import concourse.bass as bass
from concourse import mybir

P = 128
D_MODEL = 1024
KC = D_MODEL // P
NT = 5
TOK = NT * P
LAT = TOK - P
HT = TOK // 2
DEPTH = 2
HD = 64
CT_RW = 14
CT = CT_RW + 4
COLS = 1 + P + 1 + LAT + 1
IN = COLS - 2
TM = 1552
ML_V, ML_O, GATES = 1024, 1280, 1536
TOPK = 16
NB = 64
NBATCH = TOK // NB
GRP = 4
NGRP = P // GRP
NPRM = 46
EPS = 1e-5
ALPHA = (2 * DEPTH) ** 0.25

F32 = mybir.dt.float32
U32 = mybir.dt.uint32
F32R = mybir.dt.float32r
ALU = mybir.AluOpType
ACT = mybir.ActivationFunctionType
AX = mybir.AxisListType.X
ds = bass.ds


def tile(nc, ctx, name, shape, dt=F32):
    return ctx.enter_context(nc.sbuf_tensor(f"{name}_{nc.next_id()}", shape, dt))


class Chain:

    def __init__(self, eng, sem):
        self.eng, self.sem, self.n = eng, sem, 0

    def inc(self, ins):
        self.n += 1
        ins.then_inc(self.sem, 1)

    def sync(self):
        self.eng.wait_ge(self.sem, self.n)

    def __call__(self, ins):
        self.inc(ins)
        self.sync()


class Phase:

    def __init__(self, nc, sems):
        self.nc, self.names, self.ctx = nc, sems.split(), ExitStack()

    def __enter__(self):
        self.s = {n: self.ctx.enter_context(self.nc.semaphore(f"{n}_{self.nc.next_id()}")) for n in self.names}
        return self

    def __exit__(self, *a):
        self.ctx.close()

    def sem(self, n):
        return self.s[n]

    def sb(self, name, shape, dt=F32):
        return tile(self.nc, self.ctx, name, shape, dt)

    def meet(self):
        nums = [h.num for h in self.s.values()]
        self.nc.gpsimd.sem_clear(range(min(nums), max(nums) + 1))
        self.nc.all_engine_barrier()


def bc(ap, axis, n):
    v = ap.unsqueeze(axis)
    shape = list(v.shape)
    shape[axis] = n
    return v.to_broadcast(shape)


def of_layer(ap, layer):
    names = " ".join("abcdefg"[:len(ap.shape) - 1])
    rest = names.split()
    return ap[ds(layer, 1)].rearrange(f"l {names} -> (l {rest[0]}) {' '.join(rest[1:])}")


def tile_cols(t):
    return 1 if isinstance(t, int) else t * P + 2


def load_all(nc, loads):
    with Phase(nc, "loaded") as ph:
        with nc.Block() as block:
            @block.sync
            def _(sp):
                for dst, src in loads:
                    sp.dma_start(dst, src).then_inc(ph.sem("loaded"), 16)
                sp.wait_ge(ph.sem("loaded"), 16 * len(loads))
        ph.meet()


def build(nc, D):
    with ExitStack() as ctx:
        def sb(name, shape, dt=F32):
            return tile(nc, ctx, name, shape, dt)

        PS = ctx.enter_context(nc.psum_tensor("PS", [P, 8, 512], F32))
        ident = sb("ident", [P, P])
        ones = sb("ones", [P, P])
        modT = sb("modT", [P, NT, 32])
        grow = sb("grow", [2, 2, D_MODEL])
        selc = sb("selc", [2, 2, P])
        X = D["x_work"]

        load_all(nc, [(ident[:], D["c_ident"]), (ones[:], D["c_ones"]), (selc[:], D["c_selc"]), (X, D["x"])])

        with nc.Fori(0, DEPTH) as layer:
            modulation(nc, D, layer, modT, grow, PS, ident)
            with ExitStack() as mixer:
                def mb(name, shape, dt=F32):
                    return tile(nc, mixer, name, shape, dt)

                B = {"chan": mb("chan", [P, CT, COLS]),
                     "tokm": mb("tokm", [P, NT, TM]),
                     "prm": mb("prm", [P, NPRM])}
                with nc.sbuf_tensor("hT", [P, KC, TOK], F32) as hT:
                    normalise(nc, X, hT, modT, 0, PS, ident)
                    project_in(nc, D, layer, hT, B, PS)
                B["kkn"] = mb("kkn", [P, 4, IN])
                B["gates"] = mb("gates", [P, NT, 16])
                prepare(nc, D, layer, B, PS)
                B["Y"] = mb("Y", [P, NT, D_MODEL])
                rwkv(nc, D, layer, B, PS, ident, ones)
                linear(nc, D, layer, B, PS, ident, ones)
                mix_out(nc, D, layer, B, X, grow, selc, PS, ident)
            with ExitStack() as ex:
                hh, hl = tile(nc, ex, "hh", [P, KC, TOK], F32R), tile(nc, ex, "hl", [P, KC, TOK], F32R)
                with ExitStack() as choice:
                    h2T = tile(nc, choice, "h2T", [P, KC, TOK])
                    normalise(nc, X, h2T, modT, 16, PS, ident)
                    route(nc, D, layer, h2T, PS, ident)
                    split_rows(nc, h2T, hh, hl, PS)
                ffn = tile(nc, ex, "ffn", [P, NT, D_MODEL])
                experts(nc, D, layer, hh, hl, ffn, PS)
                finish(nc, D, layer, ffn, X, grow, selc, PS)
        load_all(nc, [(D["y"], X)])


def modulation(nc, D, layer, modT, grow, PS, ident):
    NW, HALF = 3, 3 * D_MODEL
    with Phase(nc, "cond_loaded bias_loaded w0_loaded w1_loaded w2_loaded silu_ready w_used rows_ready cols_ready mod_ready") as ph:
        S = ph.sem
        cond = ph.sb("cond", [P, KC, 2])
        scond = ph.sb("scond", [P, KC, 2])
        bmod = ph.sb("bmod", [2, 6 * D_MODEL])
        mrow = ph.sb("mrow", [2, 6 * D_MODEL])
        wm = ph.sb("wm", [P, NW, HALF])
        with nc.Block() as block:
            @block.sync
            def _(sp):
                sp.dma_start(cond[:], D["cond"]).then_inc(S("cond_loaded"), 16)
                sp.dma_start(bmod[:], of_layer(D["b_mod"], layer)).then_inc(S("bias_loaded"), 16)
                for i in range(16):
                    hf, kc = divmod(i, 8)
                    if i >= NW:
                        sp.wait_ge(S("w_used"), i - NW + 1)
                    sp.dma_start(wm[:, i % NW, :], of_layer(D["w_mod"], layer)[kc * P:(kc + 1) * P, hf * HALF:(hf + 1) * HALF]).then_inc(S(f"w{i % NW}_loaded"), 16)

            @block.scalar
            def _(act):
                act.wait_ge(S("cond_loaded"), 16)
                act.activation(scond[:], cond[:], ACT.Silu).then_inc(S("silu_ready"), 1)

            @block.tensor
            def _(pe):
                pe.wait_ge(S("silu_ready"), 1)
                for i in range(16):
                    hf, kc = divmod(i, 8)
                    pe.wait_ge(S(f"w{i % NW}_loaded"), 16 * (i // NW + 1))
                    if i == 8:
                        pe.wait_ge(S("rows_ready"), 1)
                    for n in range(6):
                        mm = pe.matmul(PS[0:2, n, :], scond[:, kc, :], wm[:, i % NW, n * 512:(n + 1) * 512],
                                       start=(kc == 0), stop=(kc == 7))
                    mm.then_inc(S("w_used"), 1)
                pe.wait_ge(S("rows_ready"), 2)
                for k, sec in enumerate((0, 1, 3, 4)):
                    for c in range(KC):
                        j = k * KC + c
                        mm = pe.transpose(PS[:, 6, 2 * j:2 * j + 2],
                                          mrow[:, (sec * KC + c) * P:(sec * KC + c + 1) * P], ident[0:2, 0:2])
                mm.then_inc(S("cols_ready"), 1)

            @block.vector
            def _(dve):
                dve.wait_ge(S("bias_loaded"), 16)
                for hf in range(2):
                    dve.wait_ge(S("w_used"), 8 * hf + 8)
                    dve.tensor_tensor(mrow[:, hf * HALF:(hf + 1) * HALF], PS[0:2, 0:6, :].rearrange("p b n -> p (b n)"),
                                      bmod[:, hf * HALF:(hf + 1) * HALF], ALU.add).then_inc(S("rows_ready"), 1)
                dve.wait_ge(S("rows_ready"), 2)
                dve.tensor_copy(grow[:, 0, :], mrow[:, 2 * D_MODEL:3 * D_MODEL]).then_inc(S("mod_ready"), 1)
                dve.tensor_copy(grow[:, 1, :], mrow[:, 5 * D_MODEL:6 * D_MODEL]).then_inc(S("mod_ready"), 1)
                dve.wait_ge(S("cols_ready"), 1)
                cols = PS[:, 6, 0:64].rearrange("p (j c) -> p c j", c=2)
                dve.tensor_copy(modT[:, 0, :], cols[:, 0, :]).then_inc(S("mod_ready"), 1)
                dve.tensor_copy(modT[:, 1:NT, :], bc(cols[:, 1, :], 1, NT - 1)).then_inc(S("mod_ready"), 1)
                dve.wait_ge(S("mod_ready"), 4)
                for c in (8, 24):
                    dve.tensor_scalar(modT[:, :, c:c + 8], modT[:, :, c:c + 8], 1.0, None, ALU.add).then_inc(S("mod_ready"), 1)
                dve.wait_ge(S("mod_ready"), 6)
        ph.meet()


def normalise(nc, X, hT, modT, first, PS, ident):
    with Phase(nc, "x_loaded stats_ready var_ready root_ready inv_ready norm_ready turned columns_ready") as ph:
        S = ph.sem
        x = ph.sb("nx", [P, NT, D_MODEL])
        xn = ph.sb("nxn", [P, 2, D_MODEL])
        st = ph.sb("nst", [P, NT, 2, 6])
        mv = ph.sb("nmv", [P, NT, 2])
        rs = ph.sb("nrs", [P, 2, NT])
        with nc.Block() as block:
            @block.sync
            def _(sp):
                for t in range(NT):
                    sp.dma_start(x[:, t, :], X[t]).then_inc(S("x_loaded"), 16)

            @block.vector
            def _(dve):
                dve.wait_ge(S("x_loaded"), 16 * NT)
                for t in range(NT):
                    for z in range(2):
                        dve.bn_stats(st[:, t, z, :], x[:, t, z * 512:(z + 1) * 512]).then_inc(S("stats_ready"), 1)
                for t in range(NT):
                    dve.wait_ge(S("stats_ready"), 2 * t + 2)
                    dve.bn_aggr(mv[:, t, :], st[:, t, :, :]).then_inc(S("stats_ready"), 1)
                dve.wait_ge(S("stats_ready"), 3 * NT)
                dve.tensor_scalar(rs[:, 0, :], mv[:, :, 1], EPS, None, ALU.add).then_inc(S("var_ready"), 1)
                dve.wait_ge(S("root_ready"), 1)
                dve.reciprocal(rs[:, 1, :], rs[:, 0, :]).then_inc(S("inv_ready"), 1)
                dve.wait_ge(S("inv_ready"), 1)
                for t in range(NT):
                    if t >= 2:
                        dve.wait_ge(S("turned"), t - 1)
                    dve.tensor_scalar(xn[:, t % 2, :], x[:, t, :], mv[:, t, 0:1], rs[:, 1, t:t + 1], ALU.subtract, ALU.mult).then_inc(S("norm_ready"), 1)

            @block.scalar
            def _(act):
                act.wait_ge(S("var_ready"), 1)
                act.activation(rs[:, 0, :], rs[:, 0, :], ACT.Sqrt).then_inc(S("root_ready"), 1)
                for t in range(NT):
                    act.wait_ge(S("turned"), t + 1)
                    for k in range(KC):
                        act.activation(hT[:, k, t * P:(t + 1) * P], PS[:, 2 * (t % 4) + k // 4, (k % 4) * P:(k % 4 + 1) * P], ACT.Identity,
                                       scale=modT[:, t, first + 8 + k:first + 9 + k], bias=modT[:, t, first + k:first + k + 1]).then_inc(S("columns_ready"), 1)
                act.wait_ge(S("columns_ready"), KC * NT)

            @block.tensor
            def _(pe):
                for t in range(NT):
                    if t >= 4:
                        pe.wait_ge(S("columns_ready"), KC * (t - 3))
                    pe.wait_ge(S("norm_ready"), t + 1)
                    for k in range(KC):
                        mm = pe.transpose(PS[:, 2 * (t % 4) + k // 4, (k % 4) * P:(k % 4 + 1) * P], xn[:, t % 2, k * P:(k + 1) * P], ident[:])
                    mm.then_inc(S("turned"), 1)
        ph.meet()


def project_in(nc, D, layer, hT, B, PS):
    chan, tokm, prm = B["chan"], B["tokm"], B["prm"]
    with Phase(nc, "prm_loaded pads_zero wa_loaded wb_loaded acc_ready acc_read ta_loaded tb_loaded tacc_ready tacc_read") as ph:
        S = ph.sem
        wt = ph.sb("wt", [P, 2, KC, P])
        wk = ph.sb("wk", [P, 2, KC, 512])
        WL = ["wa_loaded", "wb_loaded"]
        TL = ["ta_loaded", "tb_loaded"]
        widths = [512, 512, 512, TM - 1536]
        with nc.Block() as block:
            @block.sync
            def _(sp):
                sp.dma_start(prm[:], of_layer(D["prm"], layer)).then_inc(S("prm_loaded"), 16)
                sp.wait_ge(S("prm_loaded"), 16)
                with sp.Fori(0, CT // 2) as i:
                    for b in range(2):
                        sp.wait_ge(S("acc_ready"), i * 2 + b + 1)
                        sp.dma_start(wt[:, b], of_layer(of_layer(D["w_ch"], layer), i * 2 + b)).then_inc(S(WL[b]), 16)
                w_tm = of_layer(D["w_tm"], layer)
                for i, w in enumerate(widths):
                    if i >= 2:
                        sp.wait_ge(S("tacc_ready"), NT * (i - 1))
                    sp.dma_start(wk[:, i % 2, :, 0:w], w_tm[:, :, i * 512:i * 512 + w]).then_inc(S(TL[i % 2]), 16)

            @block.gpsimd
            def _(pool):
                for c in (0, 1 + P, COLS - 1):
                    pool.memset(chan[:, :, c:c + 1], 0.0).then_inc(S("pads_zero"), 1)
                pool.wait_ge(S("pads_zero"), 3)

            @block.tensor
            def _(pe):
                pe.sem_inc(S("acc_ready"), 2)
                with pe.Fori(0, CT // 2) as i:
                    for b in range(2):
                        pe.wait_ge(S(WL[b]), i * 16 + 16)
                        pe.wait_ge(S("acc_read"), i * 4 + 2 * b + 2)
                        for k in range(KC):
                            pe.matmul(PS[:, 2 * b, :], wt[:, b, k, :], hT[:, k, P:TOK], start=(k == 0), stop=(k == KC - 1))
                            mm = pe.matmul(PS[:, 2 * b + 1, 0:P], wt[:, b, k, :], hT[:, k, 0:P], start=(k == 0), stop=(k == KC - 1))
                        mm.then_inc(S("acc_ready"), 1)
                n = 0
                for i, w in enumerate(widths):
                    pe.wait_ge(S(TL[i % 2]), 16 * (i // 2 + 1))
                    for t in range(NT):
                        if n >= 4:
                            pe.wait_ge(S("tacc_read"), n - 3)
                        for k in range(KC):
                            mm = pe.matmul(PS[:, 4 + n % 4, 0:w], hT[:, k, t * P:(t + 1) * P], wk[:, i % 2, k, 0:w],
                                           start=(k == 0), stop=(k == KC - 1))
                        mm.then_inc(S("tacc_ready"), 1)
                        n += 1

            @block.scalar
            def _(act):
                act.sem_inc(S("acc_read"), 4)
                with act.Fori(0, CT // 2) as i:
                    for b in range(2):
                        act.wait_ge(S("acc_ready"), i * 2 + b + 3)
                        act.activation(chan[:, ds(i * 2 + b, 1), P + 2:P + 2 + LAT].rearrange("p a n -> p (a n)"),
                                       PS[:, 2 * b, :], ACT.Copy).then_inc(S("acc_read"), 1)
                        act.activation(chan[:, ds(i * 2 + b, 1), 1:P + 1].rearrange("p a n -> p (a n)"),
                                       PS[:, 2 * b + 1, 0:P], ACT.Copy).then_inc(S("acc_read"), 1)
                act.wait_ge(S("acc_read"), 4 + 2 * CT)

            @block.vector
            def _(dve):
                n = 0
                for i, w in enumerate(widths):
                    for t in range(NT):
                        dve.wait_ge(S("tacc_ready"), n + 1)
                        dve.tensor_copy(tokm[:, t, i * 512:i * 512 + w], PS[:, 4 + n % 4, 0:w]).then_inc(S("tacc_read"), 1)
                        n += 1
                dve.wait_ge(S("tacc_read"), n)
        ph.meet()


def prepare(nc, D, layer, B, PS):
    chan, tokm, prm, kkn, gates = B["chan"], B["tokm"], B["prm"], B["kkn"], B["gates"]
    with Phase(nc, "c_loaded shifted conv_ready silu_done low_done key_ready square_ready sums_ready root_ready z_ready ln_ready dve_step act_step") as ph:
        S = ph.sem
        tmp = ph.sb("tmp", [P, CT_RW, IN])
        blk = ph.sb("blk", [P, P])
        cos = ph.sb("cos", [P, NT - 1, 32])
        sin = ph.sb("sin", [P, NT - 1, 32])
        gbias = ph.sb("gbias", [P, 16])
        lz = ph.sb("lz", [P, NT, 2, 4])
        loads = [(blk[:], D["c_blk"]), (cos[:], D["c_cos"]), (sin[:], D["c_sin"]),
                 (gbias[:], of_layer(D["gbias"], layer))]
        rw, ml = chan[:, 0:CT_RW, :], chan[:, CT_RW:CT, :]
        conv = prm[:, 34:46].rearrange("p (c j) -> p j c", j=3)
        g4 = gates[:].rearrange("p t (d x h) -> p t d x h", d=2, x=2)
        logf = [g4[:, :, d, 1, :] for d in range(2)]
        t2, t3 = tmp[:, 0:4, :], tmp[:, 4:8, :]
        with nc.Block() as block:
            @block.sync
            def _(sp):
                for dst, src in loads:
                    sp.dma_start(dst, src).then_inc(S("c_loaded"), 16)

            @block.vector
            def _(dve):
                ch = Chain(dve, S("dve_step"))
                ch(dve.tensor_tensor(tmp[:], rw[:, :, 0:IN], rw[:, :, 2:IN + 2], ALU.add))
                ch(dve.scalar_tensor_tensor(tmp[:], tmp[:], 0.5, rw[:, :, 1:IN + 1], ALU.mult, ALU.subtract))
                ch(dve.tensor_tensor(tmp[:], tmp[:], bc(prm[:, 0:CT_RW], 2, IN), ALU.mult))
                dve.tensor_tensor(rw[:, :, 1:IN + 1], rw[:, :, 1:IN + 1], tmp[:], ALU.add).then_inc(S("shifted"), 1)
                dve.wait_ge(S("shifted"), 1)
                dve.tensor_tensor(kkn[:], rw[:, 4:8, 1:IN + 1], bc(prm[:, 22:26], 2, IN), ALU.mult).then_inc(S("key_ready"), 1)
                t0, t1 = tmp[:, 4:8, :], tmp[:, 8:12, :]
                ch(dve.tensor_tensor(t0, ml[:, :, 0:IN], bc(conv[:, 0, :], 2, IN), ALU.mult))
                ch(dve.tensor_tensor(t1, ml[:, :, 1:IN + 1], bc(conv[:, 1, :], 2, IN), ALU.mult))
                ch(dve.tensor_tensor(t0, t0, t1, ALU.add))
                ch(dve.tensor_tensor(t1, ml[:, :, 2:IN + 2], bc(conv[:, 2, :], 2, IN), ALU.mult))
                dve.tensor_tensor(t0, t0, t1, ALU.add).then_inc(S("conv_ready"), 1)
                dve.wait_ge(S("c_loaded"), 16 * len(loads))
                dve.tensor_tensor(gates[:], tokm[:, :, GATES:TM], bc(gbias[:], 1, NT), ALU.add).then_inc(S("z_ready"), 1)
                qk = tokm[:, 1:NT, 0:512].rearrange("p t (h z i) -> p t h z i", h=8, z=2)
                x1, x2 = qk[:, :, :, 0, :], qk[:, :, :, 1, :]
                cb, sbb = bc(cos[:], 2, 8), bc(sin[:], 2, 8)
                r = [tmp[:, 8:14, :].rearrange("p a n -> p (a n)")[:, i * 1024:(i + 1) * 1024].rearrange("p (t h i) -> p t h i", t=4, h=8) for i in range(3)]
                dve.wait_ge(S("conv_ready"), 1)
                ch.inc(dve.tensor_tensor(r[0], x1, cb, ALU.mult))
                ch.inc(dve.tensor_tensor(r[1], x2, sbb, ALU.mult))
                ch(dve.tensor_tensor(r[2], x1, sbb, ALU.mult))
                ch(dve.tensor_tensor(x1, r[0], r[1], ALU.subtract))
                ch(dve.tensor_tensor(r[0], x2, cb, ALU.mult))
                ch(dve.tensor_tensor(x2, r[0], r[2], ALU.add))
                ch(dve.tensor_scalar(tokm[:, :, 256:512], tokm[:, :, 256:512], HD ** -0.5, None, ALU.mult))
                dve.wait_ge(S("silu_done"), 1)
                ch(dve.tensor_scalar(ml[:, 2:4, 1:IN + 1], ml[:, 2:4, 1:IN + 1], HD ** -0.5, None, ALU.mult))
                for i in range(8):
                    dve.wait_ge(S("sums_ready"), i + 1)
                    a = (0, 321)[i % 2]
                    n = (321, IN - 321)[i % 2]
                    dve.tensor_scalar(t3[:, i // 2, a:a + n], PS[:, i, 0:n], 1e-24, None, ALU.max).then_inc(S("ln_ready"), 1)
                dve.wait_ge(S("root_ready"), 1)
                ch(dve.tensor_scalar(t3, t3, 1e-12, None, ALU.max))
                ch(dve.reciprocal(t3, t3))
                ch(dve.tensor_tensor(kkn[:], kkn[:], t3, ALU.mult))
                dve.wait_ge(S("act_step"), 4)
                for d in range(2):
                    ch(dve.tensor_scalar(logf[d], logf[d], 0.0, None, ALU.min))
                    ch(dve.tensor_tensor(logf[d], logf[d], lz[:, :, d, :], ALU.subtract))

            @block.scalar
            def _(act):
                act.wait_ge(S("shifted"), 1)
                act.activation(chan[0:64, 12, 1:IN + 1], chan[0:64, 12, 1:IN + 1], ACT.Tanh).then_inc(S("low_done"), 1)
                act.activation(chan[:, 13, 1:IN + 1], chan[:, 13, 1:IN + 1], ACT.Sigmoid).then_inc(S("low_done"), 1)
                act.wait_ge(S("key_ready"), 1)
                act.activation(t2, kkn[:], ACT.Square).then_inc(S("square_ready"), 1)
                act.wait_ge(S("conv_ready"), 1)
                act.activation(ml[:, :, 1:IN + 1], tmp[:, 4:8, :], ACT.Silu).then_inc(S("silu_done"), 1)
                act.wait_ge(S("z_ready"), 1)
                for d in range(2):
                    act.activation(lz[:, :, d, :], logf[d], ACT.Abs).then_inc(S("act_step"), 1)
                act.wait_ge(S("act_step"), 2)
                act.activation(lz[:], lz[:], ACT.Exp, scale=-1.0).then_inc(S("act_step"), 1)
                act.wait_ge(S("act_step"), 3)
                act.activation(lz[:], lz[:], ACT.Ln, bias=1.0).then_inc(S("act_step"), 1)
                act.wait_ge(S("ln_ready"), 8)
                act.activation(t3, t3, ACT.Sqrt).then_inc(S("root_ready"), 1)
                act.wait_ge(S("low_done"), 2)

            @block.tensor
            def _(pe):
                pe.wait_ge(S("square_ready"), 1)
                pe.wait_ge(S("c_loaded"), 16 * len(loads))
                for i in range(8):
                    a = (0, 321)[i % 2]
                    n = (321, IN - 321)[i % 2]
                    pe.matmul(PS[:, i, 0:n], blk[:], t2[:, i // 2, a:a + n], start=True, stop=True).then_inc(S("sums_ready"), 1)
        ph.meet()


def rwkv(nc, D, layer, B, PS, ident, ones):
    with ExitStack() as ctx:
        W = {n: tile(nc, ctx, "r_" + n, s) for n, s in {
            "tri": [P, 2, 257],
            "strict": [P, 2, P], "incl": [P, 2, P], "strictT": [P, 2, P],
            "lvl": [P, 4, P],
            "lora": [P, 2, 512],
            "w0": [1, 2, 512],
            "state": [P, 2, 4, HD]}.items()}
        for n, s in {"s0": [P, 4, HD], "low": [P, P], "vt": [P, 512], "eM": [P, 4], "ePC": [P, 4],
                     "bt": [P, 4, P], "kt": [P, 4, P], "KR": [P, 4, 2, P], "btk": [P, 512], "ktk": [P, 512],
                     "G": [P, 4, 3, P], "L": [P, 4, P], "E": [P, 4, P], "ET": [P, 4, P], "Z": [P, 4, P], "ZT": [P, 4, P]}.items():
            W[n] = [tile(nc, ctx, f"r_{n}{d}", s) for d in range(2)]
        W["sg"], W["a"], W["eN"], W["v"] = W["E"], W["Z"], W["ET"], W["ZT"]
        load_all(nc, [(W["tri"][:], D["c_tri"]), (W["strict"][:], D["c_strict"]), (W["incl"][:], D["c_incl"]),
                      (W["strictT"][:], D["c_strictT"]), (W["lvl"][:], D["c_lvl"]),
                      (W["lora"][:], of_layer(D["lora"], layer)), (W["w0"][:], of_layer(D["w0"], layer))])
        with Phase(nc, "zeroed") as ph:
            with nc.Block() as block:
                @block.gpsimd
                def _(pool):
                    pool.memset(W["state"][:], 0.0).then_inc(ph.sem("zeroed"), 1)
                    pool.memset(B["Y"][:], 0.0).then_inc(ph.sem("zeroed"), 1)
                    pool.wait_ge(ph.sem("zeroed"), 2)
            ph.meet()
        rwkv_tiles(nc, B, W, PS, ident, ones, (0, 0))
        load_all(nc, [(of_layer(D["o_rwkv"], layer), W["state"][:])])
        load_all(nc, [(W["state"][:], of_layer(D["s_rwkv"], layer))])
        with nc.Fori(0, NT - 1) as j:
            rwkv_tiles(nc, B, W, PS, ident, ones, (j + 1, 4 - j))


def rwkv_tiles(nc, B, W, PS, ident, ones, tiles):
    chan, prm, kkn, Y, state = B["chan"], B["prm"], B["kkn"], B["Y"], W["state"]
    names = ("cur_ready z_ready a_ready vt_turned sg_ready rate_ready vt_ready cum_ready exp_ready feat_ready tok_turned tok_ready "
             "g_ready g_read l_ready inv_start pow_ready pow_dve pow_act lm_ready merge_ready merge_act merge_dve "
             "rh_ready rhn_ready sa_ready sas_ready y_ready half_done")
    HEADS = [(h, h // 2, slice(64 * (h % 2), 64 * (h % 2) + 64), 2 * (h % 2) + h // 2) for h in range(4)]

    with Phase(nc, "dve_step " + " ".join(f"{n}{d}" for n in names.split() for d in range(2))) as ph:
        def S(name, d):
            return ph.sem(f"{name}{d}")

        def four(d, b, n=P):
            return PS[:, 4 * d + b, 0:4 * n].rearrange("p (h n) -> p h n", n=n)

        def parity(d, b, n):
            return PS[:, 4 * d + b:4 * d + b + 2, 0:2 * n].rearrange("p x (j n) -> p x j n", n=n)

        with nc.Block() as block:
            @block.scalar
            def _(act):
                for d in range(2):
                    c0 = tile_cols(tiles[d])
                    act.activation(W["low"][d][:], chan[:, 12, ds(c0, P)], ACT.Copy).then_inc(S("cur_ready", d), 1)
                    act.activation(W["v"][d][:], chan[:, 8:12, ds(c0, P)], ACT.Copy).then_inc(S("cur_ready", d), 1)
                for d in range(2):
                    act.wait_ge(S("z_ready", d), 1)
                    act.activation(W["sg"][d][:].rearrange("p h n -> p (h n)"), PS[:, 4 * d, :], ACT.Sigmoid).then_inc(S("sg_ready", d), 1)
                    act.wait_ge(S("a_ready", d), 1)
                    for c in range(4):
                        act.activation(W["a"][d][:, c, :], four(d, 1)[:, c, :], ACT.Sigmoid,
                                       bias=prm[:, 14 + 4 * d + c:15 + 4 * d + c]).then_inc(S("rate_ready", d), 1)
                    act.wait_ge(S("vt_turned", d), 1)
                    act.activation(W["vt"][d][:], PS[:, 4 * d + 2, :], ACT.Copy).then_inc(S("vt_ready", d), 1)
                for d in range(2):
                    act.wait_ge(S("cum_ready", d), 1)
                    act.activation(W["eN"][d][:], four(d, 3), ACT.Exp, scale=-1.0).then_inc(S("exp_ready", d), 1)
                    act.activation(W["KR"][d][:, :, 1, :], four(d, 3), ACT.Exp).then_inc(S("exp_ready", d), 1)
                    act.activation(W["KR"][d][:, :, 0, :], four(d, 0), ACT.Exp).then_inc(S("exp_ready", d), 1)
                    act.activation(W["eM"][d][:], PS[:, 4 * d + 1, 0:4], ACT.Exp).then_inc(S("exp_ready", d), 1)
                for d in range(2):
                    act.wait_ge(S("tok_turned", d), 1)
                    act.activation(W["btk"][d][:], PS[:, 4 * d + 2, :], ACT.Copy).then_inc(S("tok_ready", d), 1)
                    act.activation(W["ktk"][d][:], PS[:, 4 * d + 1, :], ACT.Copy).then_inc(S("tok_ready", d), 1)
                for half in range(2):
                    for k in range(3):
                        for d in range(2):
                            act.wait_ge(S("pow_ready", d), 4 * half + k + 1)
                            act.activation(W["E"][d][:], four(d, 0), ACT.Copy).then_inc(S("pow_act", d), 1)
                            act.activation(W["ET"][d][:], four(d, 1), ACT.Copy).then_inc(S("pow_act", d), 1)
                    for k in range(3):
                        for d in range(2):
                            act.wait_ge(S("merge_ready", d), 6 * half + 2 * k + 1)
                            act.activation(W["E"][d][:], four(d, 0), ACT.Copy).then_inc(S("merge_act", d), 1)
                    for d in range(2):
                        act.wait_ge(S("rh_ready", d), half + 1)
                        act.activation(W["L"][d][:, 0:2, :].rearrange("p j (x n) -> p x j n", x=2), parity(d, 0, HD), ACT.Copy,
                                       scale=-1.0).then_inc(S("rhn_ready", d), 1)
                    for d in range(2):
                        act.wait_ge(S("sa_ready", d), half + 1)
                        act.activation(W["L"][d][:, 2:4, :].rearrange("p j n -> p (j n)"), PS[:, 4 * d + 2, 0:4 * HD], ACT.Copy).then_inc(S("sas_ready", d), 1)

            @block.vector
            def _(dve):
                ch = Chain(dve, ph.sem("dve_step"))
                for d in range(2):
                    c0 = tile_cols(tiles[d])
                    r, k = chan[:, 0:4, ds(c0, P)], chan[:, 4:8, ds(c0, P)]
                    kk = kkn[:, :, ds(c0 - 1, P)]
                    kt, bt, KR, a, eN = (W[n][d] for n in ("kt", "bt", "KR", "a", "eN"))
                    dve.wait_ge(S("rate_ready", d), 4)
                    for c in range(4):
                        ch.inc(dve.tensor_scalar(kt[:, c, :], a[:, c, :], 1.0, prm[:, 26 + c:27 + c], ALU.subtract, ALU.mult))
                    ch(dve.tensor_tensor(bt[:], kk, a[:], ALU.mult))
                    ch(dve.scalar_tensor_tensor(kt[:], kt[:], 1.0, k, ALU.add, ALU.mult))
                    dve.wait_ge(S("exp_ready", d), 4)
                    ch.inc(dve.tensor_copy(W["ePC"][d][:], KR[:, :, 1, P - 1 if d == 0 else 0]))
                    ch.sync()
                    dve.tensor_tensor(bt[:], bt[:], eN[:], ALU.mult).then_inc(S("feat_ready", d), 1)
                    dve.tensor_tensor(kt[:], kt[:], eN[:], ALU.mult).then_inc(S("feat_ready", d), 1)
                    dve.tensor_tensor(KR[:, :, 0, :], KR[:, :, 0, :], kk, ALU.mult).then_inc(S("feat_ready", d), 1)
                    dve.tensor_tensor(KR[:, :, 1, :], KR[:, :, 1, :], r, ALU.mult).then_inc(S("feat_ready", d), 1)
                    dve.tensor_tensor(W["s0"][d][:], state[:, d], bc(W["eM"][d][:], 2, HD), ALU.mult).then_inc(S("feat_ready", d), 1)
                for half in range(2):
                    for d in range(2):
                        E, G = W["E"][d], W["G"][d]
                        for h, j, q, s in HEADS:
                            dve.wait_ge(S("g_ready", d), 4 * half + h + 1)
                            g = PS[:, 4 * d + h, :].rearrange("p (x y n) -> p x y n", x=2, y=2)
                            dve.tensor_tensor(E[:, s, :], g[:, 0, 0, :], W["strict"][:, d, :], ALU.mult).then_inc(S("g_read", d), 1)
                            dve.tensor_tensor(G[:, h, 0, :], g[:, 1, 0, :], W["strict"][:, d, :], ALU.mult).then_inc(S("g_read", d), 1)
                            dve.tensor_tensor(G[:, h, 1:3, :], g[:, :, 1, :], bc(W["incl"][:, d, :], 1, 2), ALU.mult).then_inc(S("g_read", d), 1)
                    for d in range(2):
                        L, E, ET = W["L"][d], W["E"][d], W["ET"][d]
                        dve.wait_ge(S("l_ready", d), half + 1)
                        Lp = L[:].rearrange("p (x j) n -> p x j n", x=2)
                        strictT = bc(bc(W["strictT"][:, d, :], 1, 2), 1, 2)
                        ch.inc(dve.tensor_tensor(Lp, parity(d, 0, P), strictT, ALU.mult))
                        dve.wait_ge(S("g_read", d), 12 * half + 12)
                        ch(dve.tensor_tensor(E[:], E[:], bc(W["lvl"][:, 0, :], 1, 4), ALU.mult))
                        ch.inc(dve.tensor_tensor(ET[:], L[:], bc(W["lvl"][:, 0, :], 1, 4), ALU.mult))
                        dve.tensor_tensor(W["Z"][d][:], bc(ident[:], 1, 4), E[:], ALU.subtract).then_inc(S("inv_start", d), 1)
                        ch.sync()
                        dve.tensor_tensor(W["ZT"][d][:], bc(ident[:], 1, 4), ET[:], ALU.subtract).then_inc(S("inv_start", d), 1)
                    for k in range(1, 4):
                        for d in range(2):
                            Z, ZT = W["Z"][d], W["ZT"][d]
                            dve.wait_ge(S("pow_ready", d), 4 * half + k + 1)
                            if k > 1:
                                dve.wait_ge(S("pow_dve", d), 6 * half + 2 * k - 2)
                            else:
                                dve.wait_ge(S("inv_start", d), 2 * half + 2)
                            dve.tensor_tensor(Z[:], Z[:], four(d, 2), ALU.add).then_inc(S("pow_dve", d), 1)
                            dve.tensor_tensor(ZT[:], ZT[:], four(d, 3), ALU.add).then_inc(S("pow_dve", d), 1)
                            if k == 3:
                                dve.tensor_tensor(W["ET"][d][:], W["L"][d][:], bc(W["lvl"][:, 1, :], 1, 4), ALU.mult).then_inc(S("lm_ready", d), 1)
                    for k in range(3):
                        for d in range(2):
                            Z, ZT = W["Z"][d], W["ZT"][d]
                            dve.wait_ge(S("merge_ready", d), 6 * half + 2 * k + 2)
                            if k:
                                dve.wait_ge(S("merge_dve", d), 5 * half + 2 * k)
                            else:
                                dve.wait_ge(S("pow_dve", d), 6 * half + 6)
                            dve.tensor_tensor(Z[:], Z[:], four(d, 2), ALU.subtract).then_inc(S("merge_dve", d), 1)
                            if k < 2:
                                dve.tensor_tensor(ZT[:], ZT[:], four(d, 3), ALU.subtract).then_inc(S("merge_dve", d), 1)
                                dve.tensor_tensor(W["ET"][d][:], W["L"][d][:], bc(W["lvl"][:, k + 2, :], 1, 4), ALU.mult).then_inc(S("lm_ready", d), 1)
                    for d in range(2):
                        dve.wait_ge(S("y_ready", d), 2 * half + 1)
                        yt = Y[:, ds(tiles[d], 1), 256 + 256 * half:512 + 256 * half].rearrange("p a (j x n) -> p (a x) j n", x=2, n=HD)
                        ch.inc(dve.tensor_tensor(yt, yt, parity(d, 0, HD), ALU.add))
                        dve.wait_ge(S("y_ready", d), 2 * half + 2)
                        pairs = PS[:, 4 * d + 3, 0:256].rearrange("p (j x n) -> p j x n", j=2, x=2)
                        js = slice(2 * half, 2 * half + 2)
                        for x in range(2):
                            q = slice(64 * x, 64 * x + 64)
                            ch.inc(dve.tensor_tensor(state[q, d, js, :], W["s0"][d][q, js, :], pairs[q, :, x, :], ALU.add))
                        ch.sync()
                        dve.tensor_tensor(state[:, d, js, :], state[:, d, js, :], bc(W["ePC"][d][:, js], 2, HD), ALU.mult).then_inc(S("half_done", d), 1)
                for d in range(2):
                    dve.wait_ge(S("half_done", d), 2)

            @block.tensor
            def _(pe):
                for d in range(2):
                    b, low = 4 * d, W["low"][d]
                    pe.wait_ge(S("cur_ready", d), 2)
                    pe.matmul(PS[:, b, :], low[0:64, :], W["lora"][0:64, d, :], start=True, stop=False)
                    pe.matmul(PS[:, b, :], ones[0:1, :], W["w0"][0:1, d, :], start=False, stop=True).then_inc(S("z_ready", d), 1)
                    for c in range(4):
                        mm = pe.matmul(PS[:, b + 1, c * P:(c + 1) * P], W["lora"][64:128, d, c * P:(c + 1) * P], low[64:128, :], start=True, stop=True)
                    mm.then_inc(S("a_ready", d), 1)
                    for c in range(4):
                        mm = pe.transpose(PS[:, b + 2, c * P:(c + 1) * P], W["v"][d][:, c, :], ident[:])
                    mm.then_inc(S("vt_turned", d), 1)
                for d in range(2):
                    b = 4 * d
                    pe.wait_ge(S("sg_ready", d), 1)
                    pe.wait_ge(S("rate_ready", d), 4)
                    for c in range(4):
                        w = W["sg"][d][:, c, :]
                        pe.matmul(PS[:, b + 3, c * P:(c + 1) * P], w, W["tri"][:, d, 0:P], start=True, stop=True)
                        pe.matmul(PS[:, b, c * P:(c + 1) * P], w, W["tri"][:, d, P:2 * P], start=True, stop=True)
                        mm = pe.matmul(PS[:, b + 1, c:c + 1], w, W["tri"][:, d, 2 * P:2 * P + 1], start=True, stop=True)
                    mm.then_inc(S("cum_ready", d), 1)
                for d in range(2):
                    b = 4 * d
                    pe.wait_ge(S("vt_ready", d), 1)
                    pe.wait_ge(S("feat_ready", d), 2)
                    for c in range(4):
                        pe.transpose(PS[:, b + 2, c * P:(c + 1) * P], W["bt"][d][:, c, :], ident[:])
                        mm = pe.transpose(PS[:, b + 1, c * P:(c + 1) * P], W["kt"][d][:, c, :], ident[:])
                    mm.then_inc(S("tok_turned", d), 1)
                for half in range(2):
                    for d in range(2):
                        bt, kt, KR = W["bt"][d], W["kt"][d], W["KR"][d]
                        if half:
                            pe.wait_ge(S("half_done", d), 1)
                        else:
                            pe.wait_ge(S("feat_ready", d), 5)
                            pe.wait_ge(S("tok_ready", d), 2)
                        for h, j, q, s in HEADS:
                            kr = KR[q, 2 * half + j].rearrange("p x n -> p (x n)")
                            pe.matmul(PS[:, 4 * d + h, 0:256], bt[q, 2 * half + j, :], kr, start=True, stop=True)
                            pe.matmul(PS[:, 4 * d + h, 256:512], kt[q, 2 * half + j, :], kr, start=True, stop=True).then_inc(S("g_ready", d), 1)
                    for d in range(2):
                        pe.wait_ge(S("g_read", d), 12 * half + 6)
                        for h, j, q, s in HEADS:
                            mm = pe.matmul(PS[:, 4 * d + h % 2, j * P:(j + 1) * P], W["KR"][d][q, 2 * half + j, 0, :],
                                           W["bt"][d][q, 2 * half + j, :], start=True, stop=True)
                        mm.then_inc(S("l_ready", d), 1)
                    for k in range(4):
                        for d in range(2):
                            E, ET, Z, ZT = (W[n][d] for n in ("E", "ET", "Z", "ZT"))
                            if k:
                                pe.wait_ge(S("pow_act", d), 6 * half + 2 * k)
                            else:
                                pe.wait_ge(S("inv_start", d), 2 * half + 2)
                            if k > 1:
                                pe.wait_ge(S("pow_dve", d), 6 * half + 2 * k - 2)
                            for s in range(4):
                                o = slice(s * P, s * P + P)
                                if k < 3:
                                    pe.matmul(PS[:, 4 * d, o], ET[:, s, :], E[:, s, :], start=True, stop=True)
                                    mm = pe.matmul(PS[:, 4 * d + 1, o], E[:, s, :], ET[:, s, :], start=True, stop=True)
                                if k:
                                    pe.matmul(PS[:, 4 * d + 2, o], ET[:, s, :], Z[:, s, :], start=True, stop=True)
                                    mm = pe.matmul(PS[:, 4 * d + 3, o], E[:, s, :], ZT[:, s, :], start=True, stop=True)
                            mm.then_inc(S("pow_ready", d), 1)
                    for k in range(3):
                        for d in range(2):
                            pe.wait_ge(S("lm_ready", d), 3 * half + k + 1)
                            if k:
                                pe.wait_ge(S("merge_dve", d), 5 * half + 2 * k)
                            else:
                                pe.wait_ge(S("pow_dve", d), 6 * half + 6)
                            for s in range(4):
                                mm = pe.matmul(PS[:, 4 * d, s * P:s * P + P], W["ET"][d][:, s, :], W["Z"][d][:, s, :], start=True, stop=True)
                            mm.then_inc(S("merge_ready", d), 1)
                        for d in range(2):
                            E, ZT = W["E"][d], W["ZT"][d]
                            pe.wait_ge(S("merge_act", d), 3 * half + k + 1)
                            for s in range(4):
                                o = slice(s * P, s * P + P)
                                mm = pe.matmul(PS[:, 4 * d + 2, o], ZT[:, s, :], E[:, s, :], start=True, stop=True)
                                if k < 2:
                                    mm = pe.matmul(PS[:, 4 * d + 3, o], E[:, s, :], ZT[:, s, :], start=True, stop=True)
                            mm.then_inc(S("merge_ready", d), 1)
                    for d in range(2):
                        KR, G, s0, vt = (W[n][d] for n in ("KR", "G", "s0", "vt"))
                        for h, j, q, s in HEADS:
                            o, J = slice(j * HD, (j + 1) * HD), 2 * half + j
                            pe.matmul(PS[:, 4 * d + h % 2, o], KR[q, J, 0, :], s0[q, J, :], start=True, stop=False)
                            mm = pe.matmul(PS[:, 4 * d + h % 2, o], G[:, h, 0, :], vt[:, (4 * half + h) * HD:(4 * half + h + 1) * HD], start=False, stop=True)
                        mm.then_inc(S("rh_ready", d), 1)
                    for d in range(2):
                        pe.wait_ge(S("rhn_ready", d), half + 1)
                        pe.wait_ge(S("merge_dve", d), 5 * half + 5)
                        for h, j, q, s in HEADS:
                            mm = pe.matmul(PS[:, 4 * d + 2, h * HD:(h + 1) * HD], W["Z"][d][:, s, :], W["L"][d][:, j, (h % 2) * HD:(h % 2 + 1) * HD],
                                           start=True, stop=True)
                        mm.then_inc(S("sa_ready", d), 1)
                    for d in range(2):
                        KR, G, s0, vt, L = (W[n][d] for n in ("KR", "G", "s0", "vt", "L"))
                        pe.wait_ge(S("sas_ready", d), half + 1)
                        for h, j, q, s in HEADS:
                            o, J, vc = slice(j * HD, (j + 1) * HD), 2 * half + j, slice((4 * half + h) * HD, (4 * half + h + 1) * HD)
                            sa = L[:, 2 + j, (h % 2) * HD:(h % 2 + 1) * HD]
                            pe.matmul(PS[:, 4 * d + h % 2, o], KR[q, J, 1, :], s0[q, J, :], start=True, stop=False)
                            pe.matmul(PS[:, 4 * d + h % 2, o], G[:, h, 1, :], sa, start=False, stop=False)
                            mm = pe.matmul(PS[:, 4 * d + h % 2, o], G[:, h, 2, :], vt[:, vc], start=False, stop=True)
                        mm.then_inc(S("y_ready", d), 1)
                        for j in range(2):
                            o, c = slice(j * P, (j + 1) * P), slice((2 * half + j) * P, (2 * half + j + 1) * P)
                            pe.matmul(PS[:, 4 * d + 3, o], W["btk"][d][:, c], L[:, 2 + j, :], start=True, stop=False)
                            mm = pe.matmul(PS[:, 4 * d + 3, o], W["ktk"][d][:, c], vt[:, c], start=False, stop=True)
                        mm.then_inc(S("y_ready", d), 1)
        ph.meet()


def row_bc(ap, layer):
    v = ap[ds(layer, 1)].partition_broadcast(P)
    names = " ".join("bcdefg"[:len(v.shape) - 2])
    return v.rearrange(f"p a {names} -> p (a {names.split()[0]}) {' '.join(names.split()[1:])}")


def linear(nc, D, layer, B, PS, ident, ones):
    with ExitStack() as ctx:
        def sb(name, shape, dt=F32):
            return tile(nc, ctx, name, shape, dt)

        W = {n: sb("l_" + n, s) for n, s in {
            "cum": [P, 2, P], "negm": [P, 2, P], "dist": [P, 2, P], "pos": [P, 2, 3],
            "rdec": [P, 8], "wret": [P, 2, 4, P], "fret": [P, 2, 3, 4],
            "state": [P, 2, 4, HD + 1],
            "m": [P, 2, 4],
            "qk": [P, 512], "qT": [P, 4, P], "kT": [P, 4, P], "va": [P, 8, HD + 1], "gc": [P, 16],
            "b": [P, 8], "c": [P, 4], "diag": [P, 4, P], "Dm": [P, 4, P], "gl": [P, 4], "g": [P, 4], "mn": [P, 4],
            "sm": [P, 4, 4], "f": [P, 3, 8], "cs": [P, 4], "SC": [P, 8, P], "SCT": [P, 8, P], "ku": [P, 8, HD],
            "num": [P, 8, HD + 1], "den": [P, 4]}.items()}
        load_all(nc, [(W["cum"][:], D["c_cum"]), (W["negm"][:], D["c_negm"]), (W["dist"][:], D["c_dist"]),
                      (W["pos"][:], D["c_pos"]), (W["rdec"][:], row_bc(D["ret_decay"], layer))])
        with Phase(nc, "zeroed lg_ready dist_ready w_ready dve_step") as ph:
            S = ph.sem
            with nc.Block() as block:
                @block.gpsimd
                def _(pool):
                    pool.memset(W["state"][:], 0.0).then_inc(S("zeroed"), 1)
                    pool.memset(W["m"][:], 0.0).then_inc(S("zeroed"), 1)
                    pool.memset(W["va"][:], 1.0).then_inc(S("zeroed"), 1)
                    pool.wait_ge(S("zeroed"), 3)

                @block.scalar
                def _(act):
                    act.activation(W["rdec"][:], W["rdec"][:], ACT.Exp).then_inc(S("lg_ready"), 1)
                    act.wait_ge(S("dist_ready"), 1)
                    act.activation(W["wret"][:], W["wret"][:], ACT.Exp).then_inc(S("w_ready"), 1)
                    act.activation(W["fret"][:], W["fret"][:], ACT.Exp).then_inc(S("w_ready"), 1)
                    act.wait_ge(S("w_ready"), 2)

                @block.vector
                def _(dve):
                    ch = Chain(dve, S("dve_step"))
                    dve.wait_ge(S("lg_ready"), 1)
                    ch(dve.tensor_scalar(W["rdec"][:], W["rdec"][:], -1.0, None, ALU.mult))
                    for d in range(2):
                        for h in range(4):
                            lg = W["rdec"][:, 4 * d + h:4 * d + h + 1]
                            ch.inc(dve.scalar_tensor_tensor(W["wret"][:, d, h, :], W["dist"][:, d, :], lg, W["negm"][:, d, :], ALU.mult, ALU.add))
                            ch.inc(dve.tensor_scalar(W["fret"][:, d, :, h], W["pos"][:, d, :], lg, None, ALU.mult))
                    ch.sync()
                    dve.engine_nop().then_inc(S("dist_ready"), 1)
            ph.meet()
        linear_tiles(nc, B, W, PS, ident, ones, (0, 0))
        load_all(nc, [(of_layer(D["o_la"], layer), W["state"][:]), (D["o_m"][ds(layer, 1), :], W["m"][0:1].rearrange("p d h -> p (d h)"))])
        load_all(nc, [(W["state"][:], of_layer(D["s_la"], layer)), (W["m"][:].rearrange("p d h -> p (d h)"), row_bc(D["s_m"], layer))])
        with nc.Fori(0, NT - 1) as j:
            linear_tiles(nc, B, W, PS, ident, ones, (j + 1, 4 - j))


def linear_tiles(nc, B, W, PS, ident, ones, tiles):
    chan, tokm, gates, Y = B["chan"], B["tokm"], B["gates"], B["Y"]
    state, m, qk, qT, kT, va, gc, b, c, diag, Dm = (W[n] for n in "state m qk qT kT va gc b c diag Dm".split())
    gl, g, mn, sm, f, cs, SC, SCT, ku, num, den = (W[n] for n in "gl g mn sm f cs SC SCT ku num den".split())

    def by_parity(ap):
        return ap.rearrange("p (j x) n -> p x j n", x=2)

    def halves(b, n):
        return PS[:, b:b + 2, 0:4 * n].rearrange("p x (j n) -> p x j n", n=n)

    def heads(bank, n, k=4):
        return PS[:, bank, 0:k * n].rearrange("p (h n) -> p h n", n=n)

    with Phase(nc, "cur_ready v_ready qk_turned qk_ready b_ready diag_ready cb_ready logs_ready w_ready s_ready sc_ready "
                   "sct_turned sct_ready o_ready u_ready chunk_done dve_step") as ph:
        S = ph.sem
        with nc.Block() as block:
            @block.gpsimd
            def _(pool):
                for d in range(2):
                    if d:
                        pool.wait_ge(S("chunk_done"), d)
                    for i, c0 in enumerate((512, ML_V)):
                        pool.tensor_copy(va[:, 4 * i:4 * i + 4, 0:HD], tokm[:, ds(tiles[d], 1), c0:c0 + 256].rearrange("p a (h n) -> p (a h) n", h=4)).then_inc(S("v_ready"), 1)

            @block.scalar
            def _(act):
                for d in range(2):
                    t, c0 = tiles[d], tile_cols(tiles[d])
                    if d:
                        act.wait_ge(S("chunk_done"), d)
                    act.activation(qk[:], tokm[:, ds(t, 1), 0:512].rearrange("p a n -> p (a n)"), ACT.Copy).then_inc(S("cur_ready"), 1)
                    act.activation(gc[:], gates[:, ds(t, 1), :].rearrange("p a n -> p (a n)"), ACT.Copy).then_inc(S("cur_ready"), 1)
                    act.activation(qT[:, 2:4, :], chan[:, 14:16, ds(c0, P)], ACT.Copy).then_inc(S("cur_ready"), 1)
                    act.activation(kT[:, 2:4, :], chan[:, 16:18, ds(c0, P)], ACT.Copy).then_inc(S("cur_ready"), 1)
                    act.wait_ge(S("qk_turned"), d + 1)
                    act.activation(qT[:, 0:2, :], heads(4, P)[:, 0:2, :], ACT.Copy).then_inc(S("qk_ready"), 1)
                    act.activation(kT[:, 0:2, :], heads(4, P)[:, 2:4, :], ACT.Copy).then_inc(S("qk_ready"), 1)
                    act.wait_ge(S("logs_ready"), d + 1)
                    act.activation(Dm[:], Dm[:], ACT.Exp).then_inc(S("w_ready"), 1)
                    act.activation(sm[:], sm[:], ACT.Exp).then_inc(S("w_ready"), 1)
                    act.wait_ge(S("sct_turned"), d + 1)
                    act.activation(SCT[:], PS[:, 4:6, :].rearrange("p b (h n) -> p (b h) n", n=P), ACT.Copy).then_inc(S("sct_ready"), 1)

            @block.vector
            def _(dve):
                ch = Chain(dve, S("dve_step"))
                for d in range(2):
                    dve.wait_ge(S("b_ready"), d + 1)
                    ch(dve.tensor_copy(b[:], PS[:, 0, 0:8]))
                    ch(dve.tensor_tensor(c[:], gc[:, 8 * d:8 * d + 4], b[:, 0:4], ALU.subtract))
                    dve.tensor_tensor(diag[:], bc(ident[:], 1, 4), bc(c[:], 2, P), ALU.mult).then_inc(S("diag_ready"), 1)
                    dve.wait_ge(S("cb_ready"), d + 1)
                    ch.inc(dve.tensor_reduce(gl[:], heads(1, P), AX, ALU.max))
                    ch(dve.tensor_tensor(Dm[:], heads(1, P), bc(W["negm"][:, d, :], 1, 4), ALU.add))
                    ch(dve.tensor_reduce(g[:], Dm[:], AX, ALU.max))
                    ch.inc(dve.tensor_tensor(g[:], g[:], m[:, d, :], ALU.max))
                    ch(dve.tensor_tensor(gl[:], gl[:], m[:, d, :], ALU.max))
                    ch.inc(dve.tensor_tensor(Dm[:], Dm[:], bc(g[:], 2, P), ALU.subtract))
                    ch.inc(dve.tensor_tensor(sm[:, 0, :], m[:, d, :], g[:], ALU.subtract))
                    ch.inc(dve.scalar_tensor_tensor(sm[:, 1, :], b[:, 0:4], -1.0, g[:], ALU.mult, ALU.subtract))
                    ch.inc(dve.tensor_tensor(sm[:, 2, :], c[:], gl[:], ALU.subtract))
                    ch.inc(dve.tensor_tensor(sm[:, 3, :], m[:, d, :], gl[:], ALU.subtract))
                    ch(dve.tensor_tensor(mn[:], b[:, 4:8], gl[:], ALU.add))
                    dve.tensor_copy(m[:, d, :], mn[:]).then_inc(S("logs_ready"), 1)
                    dve.wait_ge(S("w_ready"), 2 * d + 2)
                    ch.inc(dve.tensor_copy(f[:, :, 0:4], W["fret"][:, d]))
                    ch.inc(dve.tensor_copy(f[:, 0, 4:8], sm[:, 0, :]))
                    ch(dve.tensor_copy(f[:, 1:3, 4:8], sm[:, 2:4, :]))
                    ch.inc(dve.tensor_tensor(ku[:, 0:4, :], qk[:, 256:512].rearrange("p (h n) -> p h n", h=4), bc(f[:, 1, 0:4], 2, HD), ALU.mult))
                    ch.inc(dve.tensor_tensor(ku[:, 4:8, :], heads(5, HD), bc(f[:, 1, 4:8], 2, HD), ALU.mult))
                    for x in range(2):
                        q = slice(64 * x, 64 * x + 64)
                        ch.inc(dve.tensor_copy(cs[q, :], f[q, 2, x:8:2]))
                    dve.wait_ge(S("s_ready"), d + 1)
                    ch.inc(dve.tensor_tensor(by_parity(SC[:, 0:4, :]), halves(2, P)[:, :, 0:2, :], by_parity(W["wret"][:, d]), ALU.mult))
                    ch(dve.tensor_tensor(by_parity(SC[:, 4:8, :]), halves(2, P)[:, :, 2:4, :], by_parity(Dm[:]), ALU.mult))
                    dve.engine_nop().then_inc(S("sc_ready"), 1)
                    dve.wait_ge(S("o_ready"), d + 1)
                    ws = bc(f[:, 0, :].rearrange("p (j x) -> p x j", x=2), 3, HD + 1)
                    ch(dve.tensor_tensor(by_parity(num[:]), halves(0, HD + 1), ws, ALU.mult))
                    ch(dve.tensor_tensor(by_parity(num[:]), by_parity(num[:]), halves(6, HD + 1), ALU.add))
                    ch(dve.scalar_tensor_tensor(den[:], num[:, 4:8, HD], -1.0, num[:, 4:8, HD], ALU.mult, ALU.max))
                    ch(dve.tensor_tensor(den[:], den[:], sm[:, 1, :], ALU.max))
                    ch(dve.reciprocal(den[:], den[:]))
                    ch(dve.tensor_tensor(num[:, 4:8, 0:HD], num[:, 4:8, 0:HD], bc(den[:], 2, HD), ALU.mult))
                    for i, o in enumerate((0, 768)):
                        yt = Y[:, ds(tiles[d], 1), o:o + 256].rearrange("p a (h n) -> p (a h) n", h=4)
                        ch.inc(dve.tensor_tensor(yt, yt, num[:, 4 * i:4 * i + 4, 0:HD], ALU.add))
                    dve.wait_ge(S("u_ready"), d + 1)
                    ch(dve.tensor_tensor(state[:, d], state[:, d], bc(cs[:], 2, HD + 1), ALU.mult))
                    for j in range(4):
                        for x in range(2):
                            q = slice(64 * x, 64 * x + 64)
                            o = (j % 3) * 130 + 65 * x
                            ch.inc(dve.tensor_tensor(state[q, d, j, :], state[q, d, j, :], PS[q, 2 + j // 3, o:o + 65], ALU.add))
                    ch.sync()
                    dve.engine_nop().then_inc(S("chunk_done"), 1)
                    dve.wait_ge(S("chunk_done"), d + 1)

            @block.tensor
            def _(pe):
                for d in range(2):
                    pe.wait_ge(S("cur_ready"), 4 * d + 4)
                    pe.matmul(PS[:, 0, 0:4], W["cum"][:, d, :], gc[:, 8 * d + 4:8 * d + 8], start=True, stop=True)
                    pe.matmul(PS[:, 0, 4:8], ones[:], gc[:, 8 * d + 4:8 * d + 8], start=True, stop=True).then_inc(S("b_ready"), 1)
                    for i in range(4):
                        pe.transpose(PS[:, 4, i * P:(i + 1) * P], qk[:, i * P:(i + 1) * P], ident[:])
                    for i in range(2):
                        mm = pe.transpose(PS[:, 5, i * P:(i + 1) * P], kT[:, 2 + i, :], ident[:])
                    mm.then_inc(S("qk_turned"), 1)
                    pe.wait_ge(S("diag_ready"), d + 1)
                    pe.matmul(PS[:, 1, :], ones[:], diag[:].rearrange("p h n -> p (h n)"), start=True, stop=True).then_inc(S("cb_ready"), 1)
                    pe.wait_ge(S("qk_ready"), 2 * d + 2)
                    for h in range(8):
                        j, q = h // 2, slice(64 * (h % 2), 64 * (h % 2) + 64)
                        mm = pe.matmul(PS[:, 2 + h % 2, j * P:(j + 1) * P], qT[q, j, :], kT[q, j, :], start=True, stop=True)
                    mm.then_inc(S("s_ready"), 1)
                    pe.wait_ge(S("sc_ready"), d + 1)
                    for h in range(8):
                        mm = pe.transpose(PS[:, 4 + h // 4, (h % 4) * P:(h % 4 + 1) * P], SC[:, h, :], ident[:])
                    mm.then_inc(S("sct_turned"), 1)
                    for h in range(8):
                        j, q, o = h // 2, slice(64 * (h % 2), 64 * (h % 2) + 64), (h // 2) * 65
                        pe.matmul(PS[:, h % 2, o:o + 65], qT[q, j, :], state[q, d, j, :], start=True, stop=True)
                    pe.wait_ge(S("sct_ready"), d + 1)
                    pe.wait_ge(S("v_ready"), 2 * d + 2)
                    for h in range(8):
                        o = (h // 2) * 65
                        mm = pe.matmul(PS[:, 6 + h % 2, o:o + 65], SCT[:, h, :], va[:, h, :], start=True, stop=True)
                    mm.then_inc(S("o_ready"), 1)
                    for j in range(4):
                        o = (j % 3) * 130
                        mm = pe.matmul(PS[:, 2 + j // 3, o:o + 130], ku[:, 2 * j:2 * j + 2, :].rearrange("p h n -> p (h n)"),
                                       va[:, 2 * j:2 * j + 2, :].rearrange("p h n -> p (h n)"), start=True, stop=True)
                    mm.then_inc(S("u_ready"), 1)
                    pe.wait_ge(S("chunk_done"), d + 1)
        ph.meet()


def post_norm_dve(dve, S, ch, t, x, st, mv, lnr):
    ch.inc(dve.bn_stats(st[:, 0, :], t[:, 0:512]))
    ch.inc(dve.bn_stats(st[:, 1, :], t[:, 512:1024]))
    ch.sync()
    ch(dve.bn_aggr(mv[:, 0:2], st[:, :, :]))
    dve.tensor_scalar(mv[:, 2:3], mv[:, 1:2], EPS, None, ALU.add).then_inc(S("var_ready"), 1)
    dve.wait_ge(S("root_ready"), 1)
    ch(dve.reciprocal(mv[:, 3:4], mv[:, 2:3]))
    ch(dve.tensor_scalar(t[:], t[:], mv[:, 0:1], mv[:, 3:4], ALU.subtract, ALU.mult))
    ch(dve.tensor_tensor(t[:], t[:], lnr[:, 0, :], ALU.mult))
    dve.tensor_tensor(t[:], t[:], lnr[:, 1, :], ALU.add).then_inc(S("row_ready"), 1)


def mix_out(nc, D, layer, B, X, grow, selc, PS, ident):
    with ExitStack() as ctx:
        def sb(name, shape, dt=F32):
            return tile(nc, ctx, name, shape, dt)

        W = {n: sb("m_" + n, s) for n, s in {
            "wo": [P, KC, D_MODEL], "gup": [P, 512], "gn": [P, 2, D_MODEL], "ln": [P, 2, D_MODEL], "hsel": [P, 2],
            "x": [P, D_MODEL], "gb": [P, D_MODEL], "y": [P, D_MODEL], "sq": [P, D_MODEL], "T": [P, KC, P],
            "glow": [P, P], "v": [P, 4, P], "rk": [P, 4, P], "sil": [P, 256], "og": [P, 256], "bon": [P, 8],
            "mean": [P, 16], "var": [P, 16], "st": [P, 2, 6], "mv": [P, 4]}.items()}
        load_all(nc, [(W["wo"][:], of_layer(D["w_out"], layer).rearrange("(k p) n -> p k n", p=P)), (W["gup"][:], of_layer(D["g_up"], layer)),
                      (W["gn"][:], row_bc(D["gn"], layer)), (W["ln"][:], row_bc(D["ln1"], layer)), (W["hsel"][:], D["c_hsel"])])
        mix_tile(nc, B, W, X, grow, selc, PS, ident, 0, 0)
        with nc.Fori(1, NT) as t:
            mix_tile(nc, B, W, X, grow, selc, PS, ident, t, 1)


def mix_tile(nc, B, W, X, grow, selc, PS, ident, t, cond):
    chan, tokm, prm, Y = B["chan"], B["tokm"], B["prm"], B["Y"]
    x, gb, y, sq, T, v, rk = (W[n] for n in "x gb y sq T v rk".split())
    c0 = tile_cols(t)
    with Phase(nc, "x_loaded stored cur_ready rk_ready heads_ready gate_ready gb_ready gbs_ready hvar_ready hroot_ready mix_ready "
                   "turned T_ready out_ready var_ready root_ready row_ready dve_step") as ph:
        S = ph.sem
        with nc.Block() as block:
            @block.sync
            def _(sp):
                sp.dma_start(x[:], of_layer(X, t)).then_inc(S("x_loaded"), 16)
                sp.wait_ge(S("row_ready"), 1)
                sp.dma_start(of_layer(X, t), y[:]).then_inc(S("stored"), 16)
                sp.wait_ge(S("stored"), 16)

            @block.scalar
            def _(act):
                act.activation(W["glow"][:], chan[:, 13, ds(c0, P)], ACT.Copy).then_inc(S("cur_ready"), 1)
                act.activation(v[:], chan[:, 8:12, ds(c0, P)], ACT.Copy).then_inc(S("cur_ready"), 1)
                tr = tokm[:, ds(t, 1), :].rearrange("p a n -> p (a n)")
                act.activation(W["sil"][:], tr[:, 768:1024], ACT.Silu).then_inc(S("gate_ready"), 1)
                act.activation(W["og"][:], tr[:, ML_O:ML_O + 256], ACT.Sigmoid).then_inc(S("gate_ready"), 1)
                act.wait_ge(S("gb_ready"), 1)
                act.activation(gb[:], PS[:, 4:6, :].rearrange("p b n -> p (b n)"), ACT.Copy).then_inc(S("gbs_ready"), 1)
                act.wait_ge(S("hvar_ready"), 1)
                act.activation(W["var"][:], W["var"][:], ACT.Sqrt).then_inc(S("hroot_ready"), 1)
                act.wait_ge(S("turned"), 1)
                act.activation(T[:], PS[:, 6:8, :].rearrange("p b (k n) -> p (b k) n", n=P), ACT.Copy).then_inc(S("T_ready"), 1)
                act.wait_ge(S("var_ready"), 1)
                act.activation(W["mv"][:, 2:3], W["mv"][:, 2:3], ACT.Sqrt).then_inc(S("root_ready"), 1)

            @block.tensor
            def _(pe):
                pe.wait_ge(S("cur_ready"), 2)
                pe.matmul(PS[:, 1, :], W["glow"][:], W["gup"][:], start=True, stop=True)
                for c in range(4):
                    pe.transpose(PS[:, 2, c * P:(c + 1) * P], v[:, c, :], ident[:])
                for i in range(2):
                    mm = pe.matmul(PS[:, 4 + i, :], selc[:, cond, :], grow[:, 0, i * 512:(i + 1) * 512], start=True, stop=True)
                mm.then_inc(S("gb_ready"), 1)
                pe.wait_ge(S("rk_ready"), 1)
                for c in range(4):
                    mm = pe.matmul(PS[:, 0, 2 * c:2 * c + 2], rk[:, c, :], W["hsel"][:], start=True, stop=True)
                mm.then_inc(S("heads_ready"), 1)
                pe.wait_ge(S("mix_ready"), 1)
                for k in range(KC):
                    mm = pe.transpose(PS[:, 6 + k // 4, (k % 4) * P:(k % 4 + 1) * P], y[:, k * P:(k + 1) * P], ident[:])
                mm.then_inc(S("turned"), 1)
                pe.wait_ge(S("T_ready"), 1)
                for i in range(2):
                    for k in range(KC):
                        mm = pe.matmul(PS[:, i, :], T[:, k, :], W["wo"][:, k, i * 512:(i + 1) * 512], start=(k == 0), stop=(k == KC - 1))
                mm.then_inc(S("out_ready"), 1)

            @block.vector
            def _(dve):
                ch = Chain(dve, S("dve_step"))
                ch(dve.tensor_tensor(rk[:], chan[:, 0:4, ds(c0, P)], chan[:, 4:8, ds(c0, P)], ALU.mult))
                dve.tensor_tensor(rk[:], rk[:], bc(prm[:, 30:34], 2, P), ALU.mult).then_inc(S("rk_ready"), 1)
                yt = Y[:, ds(t, 1), :].rearrange("p a (h n) -> p (a h) n", n=HD)
                y3, s3 = (z[:].rearrange("p (h n) -> p h n", n=HD) for z in (y, sq))
                ch(dve.tensor_reduce(W["mean"][:], yt, AX, ALU.add))
                ch(dve.tensor_scalar(W["mean"][:], W["mean"][:], 1.0 / HD, None, ALU.mult))
                ch(dve.tensor_tensor(y3, yt, bc(W["mean"][:], 2, HD), ALU.subtract))
                ch(dve.tensor_tensor(sq[:], y[:], y[:], ALU.mult))
                ch(dve.tensor_reduce(W["var"][:], s3, AX, ALU.add))
                dve.tensor_scalar(W["var"][:], W["var"][:], 1.0 / HD, EPS, ALU.mult, ALU.add).then_inc(S("hvar_ready"), 1)
                dve.wait_ge(S("hroot_ready"), 1)
                ch(dve.reciprocal(W["mean"][:], W["var"][:]))
                ch(dve.tensor_tensor(y3, y3, bc(W["mean"][:], 2, HD), ALU.mult))
                ch(dve.tensor_tensor(y[:], y[:], W["gn"][:, 0, :], ALU.mult))
                ch(dve.tensor_tensor(y[:], y[:], W["gn"][:, 1, :], ALU.add))
                dve.wait_ge(S("gate_ready"), 2)
                ch.inc(dve.tensor_tensor(y[:, 0:256], y[:, 0:256], W["sil"][:], ALU.mult))
                ch.inc(dve.tensor_tensor(y[:, 768:1024], y[:, 768:1024], W["og"][:], ALU.mult))
                dve.wait_ge(S("heads_ready"), 1)
                ch(dve.tensor_copy(W["bon"][:], PS[:, 0, 0:8]))
                ch(dve.tensor_tensor(s3[:, 0:8, :], PS[:, 2, :].rearrange("p (h n) -> p h n", n=HD), bc(W["bon"][:], 2, HD), ALU.mult))
                ch(dve.tensor_tensor(y[:, 256:768], y[:, 256:768], sq[:, 0:512], ALU.add))
                dve.tensor_tensor(y[:, 256:768], y[:, 256:768], PS[:, 1, :], ALU.mult).then_inc(S("mix_ready"), 1)
                dve.wait_ge(S("out_ready"), 1)
                dve.wait_ge(S("gbs_ready"), 1)
                dve.wait_ge(S("x_loaded"), 16)
                ch(dve.tensor_tensor(y[:], PS[:, 0:2, :].rearrange("p b n -> p (b n)"), gb[:], ALU.mult))
                ch(dve.scalar_tensor_tensor(y[:], x[:], ALPHA, y[:], ALU.mult, ALU.add))
                post_norm_dve(dve, S, ch, y, x, W["st"], W["mv"], W["ln"])
        ph.meet()


def route(nc, D, layer, h2T, PS, ident):
    with ExitStack() as ctx:
        def sb(name, shape, dt=F32):
            return tile(nc, ctx, name, shape, dt)

        slots = sb("slots", [P, 3, TOK])
        iota = sb("iota", [P, P])
        with ExitStack() as c2:
            scores = c2.enter_context(nc.sbuf_tensor("scores", [P, NT, 16, P], F32))
            queries(nc, D, layer, h2T, scores, iota, PS)
            with Phase(nc, "cur_ready e_ready exp_ready slots_ready turned done dve_step") as ph:
                bufs = {n: ph.sb("k_" + n, s, dt) for n, s, dt in (
                    ("s", [P, 16, P], F32), ("s2", [P, 16, P], F32), ("v", [P, 16, TOPK], F32), ("i", [P, 16, TOPK], U32), ("if", [P, 16, TOPK], F32),
                    ("cand", [P, 8, 256], F32), ("cand2", [P, 8, 256], F32), ("tv", [P, 8, TOPK], F32), ("ti", [P, 8, TOPK], U32), ("hi", [P, 8, TOPK], U32),
                    ("lo", [P, 8, TOPK], U32), ("hl", [P, 2, 8, TOPK], F32), ("one", [P, P, TOPK], F32), ("sl", [P, 3, P], F32), ("sum", [P, 8], F32))}
                with nc.Fori(0, NT) as t:
                    top_tile(nc, ph, bufs, scores, slots, iota, PS, ident, t)
        spread(nc, D, slots, iota, PS)


def queries(nc, D, layer, h2T, scores, iota, PS):
    with Phase(nc, "k_loaded wa_loaded wb_loaded acc_ready q_ready s_ready s_read") as ph:
        S = ph.sem
        wt = ph.sb("wt", [P, 2, KC, P])
        keys = ph.sb("keys", [P, 16, P])
        qT = ph.sb("pqT", [P, 2, TOK])
        WL = ["wa_loaded", "wb_loaded"]
        with nc.Block() as block:
            @block.sync
            def _(sp):
                sp.dma_start(keys[:], of_layer(D["keys"], layer)).then_inc(S("k_loaded"), 16)
                sp.dma_start(iota[:], D["c_iota"]).then_inc(S("k_loaded"), 16)
                with sp.Fori(0, 8) as i:
                    for b in range(2):
                        sp.wait_ge(S("acc_ready"), i * 2 + b + 1)
                        sp.dma_start(wt[:, b], of_layer(of_layer(D["wq"], layer), i * 2 + b)).then_inc(S(WL[b]), 16)

            @block.tensor
            def _(pe):
                pe.sem_inc(S("acc_ready"), 2)
                pe.wait_ge(S("k_loaded"), 32)
                with pe.Fori(0, 8) as i:
                    for b in range(2):
                        pe.wait_ge(S(WL[b]), i * 16 + 16)
                        pe.wait_ge(S("q_ready"), i * 4 + 2 * b + 2)
                        for k in range(KC):
                            for z in range(2):
                                mm = pe.matmul(PS[:, 2 * b + z, 0:HT], wt[:, b, k, :], h2T[:, k, z * HT:(z + 1) * HT],
                                               start=(k == 0), stop=(k == KC - 1))
                        mm.then_inc(S("acc_ready"), 1)
                        pe.wait_ge(S("q_ready"), i * 4 + 2 * b + 6)
                        pe.wait_ge(S("s_read"), i * 4 + 2 * b + 2)
                        for t in range(NT):
                            mm = pe.matmul(PS[:, 4 + 2 * b + t // 4, (t % 4) * P:(t % 4 + 1) * P], qT[:, b, t * P:(t + 1) * P],
                                           keys[:, ds(i * 2 + b, 1), :].rearrange("p a n -> p (a n)"), start=True, stop=True)
                        mm.then_inc(S("s_ready"), 1)

            @block.scalar
            def _(act):
                act.sem_inc(S("q_ready"), 4)
                with act.Fori(0, 8) as i:
                    for b in range(2):
                        act.wait_ge(S("acc_ready"), i * 2 + b + 3)
                        act.wait_ge(S("s_ready"), i * 2 + b + 1)
                        for z in range(2):
                            act.activation(qT[:, b, z * HT:(z + 1) * HT], PS[:, 2 * b + z, 0:HT], ACT.Copy).then_inc(S("q_ready"), 1)

            @block.vector
            def _(dve):
                dve.sem_inc(S("s_read"), 4)
                dve.sem_inc(S("s_ready"), 2)
                with dve.Fori(0, 8) as i:
                    for b in range(2):
                        dve.wait_ge(S("s_ready"), i * 2 + b + 3)
                        dst = scores[:, :, ds(i * 2 + b, 1), :].rearrange("p t a n -> p t (a n)")
                        dve.tensor_copy(dst[:, 0:4, :], PS[:, 4 + 2 * b, :].rearrange("p (t n) -> p t n", t=4)).then_inc(S("s_read"), 1)
                        dve.tensor_copy(dst[:, 4, :], PS[:, 5 + 2 * b, 0:P]).then_inc(S("s_read"), 1)
                dve.wait_ge(S("s_read"), 4 + 32)
        ph.meet()


def top_tile(nc, ph, K, scores, slots, iota, PS, ident, t):
    S = ph.sem
    NEG = -3.0e38
    with nc.Block() as block:
        @block.scalar
        def _(act):
            act.activation(K["s"][:], scores[:, ds(t, 1), :, :].rearrange("p a g n -> p (a g) n"), ACT.Copy).then_inc(S("cur_ready"), 1)
            act.wait_ge(S("e_ready"), 1)
            act.activation(K["tv"][:], K["tv"][:], ACT.Exp).then_inc(S("exp_ready"), 1)
            act.wait_ge(S("turned"), 1)
            act.activation(slots[:, :, ds(t * P, P)], PS[:, 0, 0:3 * P].rearrange("p (a n) -> p a n", a=3), ACT.Copy).then_inc(S("done"), 1)
            act.wait_ge(S("done"), 1)

        @block.vector
        def _(dve):
            ch = Chain(dve, S("dve_step"))

            def top16(src, work, val, idx, n):
                for g in range(n):
                    ch.inc(dve.max(val[:, g, 0:8], src[:, g, :]))
                ch.sync()
                for g in range(n):
                    ch.inc(dve.max_index(idx[:, g, 0:8], val[:, g, 0:8], src[:, g, :]))
                for g in range(n):
                    ch.inc(dve.match_replace(work[:, g, :], val[:, g, 0:8], src[:, g, :], NEG))
                ch.sync()
                for g in range(n):
                    ch.inc(dve.max(val[:, g, 8:16], work[:, g, :]))
                ch.sync()
                for g in range(n):
                    ch.inc(dve.max_index(idx[:, g, 8:16], val[:, g, 8:16], work[:, g, :]))
                ch.sync()

            dve.wait_ge(S("cur_ready"), 1)
            top16(K["s"], K["s2"], K["v"], K["i"], 16)
            ch.inc(dve.tensor_copy(K["if"][:], K["i"][:]))
            v2 = K["v"][:].rearrange("p (h x) k -> p h x k", x=2)
            ch(dve.tensor_tensor(K["cand"][:].rearrange("p h (i j) -> p h i j", i=TOPK),
                                 bc(v2[:, :, 0, :], 3, TOPK), bc(v2[:, :, 1, :], 2, TOPK), ALU.add))
            top16(K["cand"], K["cand2"], K["tv"], K["ti"], 8)
            ch.inc(dve.tensor_copy(K["sum"][:], K["tv"][:, :, 0]))
            ch.inc(dve.tensor_scalar(K["hi"][:], K["ti"][:], 4, None, ALU.logical_shift_right))
            ch(dve.tensor_scalar(K["lo"][:], K["ti"][:], 15, None, ALU.bitwise_and))
            dve.tensor_tensor(K["tv"][:], K["tv"][:], bc(K["sum"][:], 2, TOPK), ALU.subtract).then_inc(S("e_ready"), 1)
            ch.inc(dve.tensor_copy(K["hl"][:, 0], K["hi"][:]))
            ch(dve.tensor_copy(K["hl"][:, 1], K["lo"][:]))
            i2 = K["if"][:].rearrange("p (h x) k -> p h x k", x=2)
            one4 = K["one"][:].rearrange("p (h k) r -> p h k r", h=8)
            for x in range(2):
                ch(dve.tensor_tensor(K["one"][:], bc(K["hl"][:, x].rearrange("p h k -> p (h k)"), 2, TOPK), bc(iota[:, 0:TOPK], 1, P), ALU.is_equal))
                ch(dve.tensor_tensor(one4, one4, bc(i2[:, :, x, :], 2, TOPK), ALU.mult))
                ch(dve.tensor_reduce(K["sl"][:, x, :], K["one"][:], AX, ALU.add))
            dve.wait_ge(S("exp_ready"), 1)
            ch(dve.tensor_reduce(K["sum"][:], K["tv"][:], AX, ALU.add))
            ch(dve.reciprocal(K["sum"][:], K["sum"][:]))
            dve.tensor_tensor(K["sl"][:, 2, :].rearrange("p (h k) -> p h k", h=8), K["tv"][:], bc(K["sum"][:], 2, TOPK), ALU.mult).then_inc(S("slots_ready"), 1)

        @block.tensor
        def _(pe):
            pe.wait_ge(S("slots_ready"), 1)
            for i in range(3):
                mm = pe.transpose(PS[:, 0, i * P:(i + 1) * P], K["sl"][:, i, :], ident[:])
            mm.then_inc(S("turned"), 1)
    ph.meet()


def spread(nc, D, slots, iota, PS):
    RING = 16
    with Phase(nc, "cur_ready a_ready b_ready w_ready w_read s0_stored s1_stored") as ph:
        S = ph.sem
        cur = ph.sb("cur", [P, 2, 3, NB])
        A, Bh = ph.sb("A", [P, RING, P]), ph.sb("Bh", [P, RING, P])
        Wt = ph.sb("Wt", [P, 2, P, NB])
        QB = NB // 4
        with nc.Block() as block:
            @block.gpsimd
            def _(pool):
                pool.sem_inc(S("w_ready"), 4)
                pool.sem_inc(S("w_read"), 8)
                for b in range(2):
                    pool.sem_inc(S(f"s{b}_stored"), 16)

            @block.scalar
            def _(act):
                with act.Fori(0, NBATCH // 2) as i:
                    for b in range(2):
                        act.activation(cur[:, b], slots[:, :, ds(i * 2 * NB + b * NB, NB)], ACT.Copy).then_inc(S("cur_ready"), 1)
                        act.wait_ge(S(f"s{b}_stored"), i * 16 + 16)
                        for q in range(QB):
                            act.wait_ge(S("w_ready"), i * 2 * QB + b * QB + q + 5)
                            act.activation(Wt[:, b, :, 4 * q:4 * q + 4], PS[:, q % 8, :].rearrange("p (t e) -> p e t", t=4), ACT.Copy).then_inc(S("w_read"), 1)

            @block.vector
            def _(dve):
                with dve.Fori(0, NBATCH // 2) as i:
                    for b in range(2):
                        dve.wait_ge(S("cur_ready"), i * 2 + b + 1)
                        for t in range(NB):
                            if t % 4 == 0:
                                dve.wait_ge(S("w_ready"), i * 2 * QB + b * QB + t // 4 + 1)
                            dve.tensor_scalar(A[:, t % RING, :], iota[:], cur[:, b, 0, t:t + 1], cur[:, b, 2, t:t + 1], ALU.is_equal, ALU.mult).then_inc(S("a_ready"), 1)
                            dve.tensor_scalar(Bh[:, t % RING, :], iota[:], cur[:, b, 1, t:t + 1], None, ALU.is_equal).then_inc(S("b_ready"), 1)

            @block.tensor
            def _(pe):
                with pe.Fori(0, NBATCH // 2) as i:
                    for b in range(2):
                        for t in range(NB):
                            n = b * NB + t
                            if t % 4 == 0:
                                pe.wait_ge(S("w_read"), i * 2 * QB + n // 4 + 1)
                            pe.wait_ge(S("b_ready"), i * 2 * NB + n + 1)
                            mm = pe.matmul(PS[:, (t // 4) % 8, (t % 4) * P:(t % 4 + 1) * P], A[:, t % RING, :], Bh[:, t % RING, :], start=True, stop=True)
                            if t % 4 == 3:
                                mm.then_inc(S("w_ready"), 1)

            @block.sync
            def _(sp):
                with sp.Fori(0, NBATCH // 2) as i:
                    for b in range(2):
                        sp.wait_ge(S("w_read"), i * 2 * QB + (b + 1) * QB + 8)
                        sp.dma_start(of_layer(D["wts"], i * 2 + b), Wt[:, b]).then_inc(S(f"s{b}_stored"), 16)
                for b in range(2):
                    sp.wait_ge(S(f"s{b}_stored"), 16 * (NBATCH // 2) + 16)
        ph.meet()


def split_rows(nc, src, hi, lo, PS):
    with Phase(nc, "hi_ready lo_ready") as ph:
        with nc.Block() as block:
            @block.scalar
            def _(act):
                for k in range(KC):
                    act.activation(hi[:, k, :], src[:, k, :], ACT.Copy).then_inc(ph.sem("hi_ready"), 1)

            @block.vector
            def _(dve):
                for k in range(KC):
                    dve.wait_ge(ph.sem("hi_ready"), k + 1)
                    dve.tensor_tensor(lo[:, k, :], src[:, k, :], hi[:, k, :].bitcast(F32), ALU.subtract).then_inc(ph.sem("lo_ready"), 1)
                dve.wait_ge(ph.sem("lo_ready"), KC)
        ph.meet()


def experts(nc, D, layer, hh, hl, ffn, PS):
    SEMS = ("u0_loaded u1_loaded v0_loaded v1_loaded g_loaded uhi_ready u_split vhi_ready v_split h_ready gelu_ready "
            "wf_ready whi_ready w_split o_ready o_read")
    with Phase(nc, SEMS) as ph:
        S = ph.sem
        u = ph.sb("u", [P, 2, KC * P])
        uh, ul = ph.sb("uh", [P, 2, KC, P], F32R), ph.sb("ul", [P, 2, KC, P], F32R)
        v = ph.sb("v", [P, 2, D_MODEL])
        vh, vl = ph.sb("vh", [P, GRP, D_MODEL], F32R), ph.sb("vl", [P, GRP, D_MODEL], F32R)
        g = ph.sb("g", [P, NBATCH, GRP, NB])
        ge, wf = ph.sb("ge", [P, 2, TOK]), ph.sb("wf", [P, 2, TOK])
        wh, wl = ph.sb("wh", [P, GRP, TOK], F32R), ph.sb("wl", [P, GRP, TOK], F32R)
        ut, pv, wts = of_layer(D["ut"], layer), of_layer(D["pv"], layer), D["wts"]
        OT = 2 * NT

        with nc.Block() as block:
            @block.sync
            def _(sp):
                with sp.Fori(0, NGRP) as i:
                    for e in range(GRP):
                        sp.wait_ge(S("u_split"), i * GRP + e + 1)
                        sp.dma_start(u[:, e % 2, :], of_layer(ut, i)[:, e, :]).then_inc(S(f"u{e % 2}_loaded"), 16)
                        sp.wait_ge(S("v_split"), i * GRP + e + 1)
                        sp.dma_start(v[:, e % 2, :], pv[:, ds(i * GRP + e, 1), :].rearrange("p a n -> p (a n)")).then_inc(S(f"v{e % 2}_loaded"), 16)
                        if e == 0:
                            sp.wait_ge(S("wf_ready"), i * GRP + 2)
                            sp.dma_start(g[:], wts[:, :, ds(i * GRP, GRP), :].rearrange("n p e t -> p n e t")).then_inc(S("g_loaded"), 16)

            @block.tensor
            def _(pe):
                def hidden(i, e):
                    pe.wait_ge(S("u_split"), i * GRP + e + 3)
                    pe.wait_ge(S("gelu_ready"), i * GRP + e + 1)
                    b, n = e % 2, 0
                    for k in range(KC):
                        for wt, x in ((uh, hh), (uh, hl), (ul, hh)):
                            for z in range(2):
                                mm = pe.matmul(PS[:, 2 * b + z, 0:HT], wt[:, b, k, :], x[:, k, z * HT:(z + 1) * HT],
                                               start=(n == 0), stop=(n == 3 * KC - 1))
                            n += 1
                    mm.then_inc(S("h_ready"), 1)

                def outputs(i):
                    pe.wait_ge(S("w_split"), i * GRP + GRP + 2)
                    pe.wait_ge(S("v_split"), i * GRP + GRP + 2)
                    for o in range(OT):
                        pe.wait_ge(S("o_read"), i * OT + 1 + (o - 3 if o >= 4 else 0))
                        n, cols = 0, slice((o % 2) * 512, (o % 2 + 1) * 512)
                        for e in range(GRP):
                            toks = slice((o // 2) * P, (o // 2 + 1) * P)
                            for wt, x in ((wh, vh), (wh, vl), (wl, vh)):
                                mm = pe.matmul(PS[:, 4 + o % 4, :], wt[:, e, toks], x[:, e, cols], start=(n == 0), stop=(n == 3 * GRP - 1))
                                n += 1
                        mm.then_inc(S("o_ready"), 1)

                hidden(0, 0)
                with pe.Fori(0, NGRP - 1) as i:
                    for e in range(1, GRP):
                        hidden(i, e)
                    hidden(i + 1, 0)
                    outputs(i)
                for e in range(1, GRP):
                    hidden(NGRP - 1, e)
                outputs(NGRP - 1)

            @block.scalar
            def _(act):
                def u_hi(i, e):
                    act.wait_ge(S(f"u{e % 2}_loaded"), i * 32 + 16 * (e // 2) + 16)
                    act.wait_ge(S("h_ready"), i * GRP + e + 1)
                    act.activation(uh[:, e % 2].rearrange("p k n -> p (k n)"), u[:, e % 2, :], ACT.Copy).then_inc(S("uhi_ready"), 1)

                def step(i, e, last=False):
                    if not last:
                        u_hi(i + (e + 1) // GRP, (e + 1) % GRP)
                    act.wait_ge(S("h_ready"), i * GRP + e + 3)
                    act.wait_ge(S("wf_ready"), i * GRP + e + 1)
                    b = e % 2
                    act.activation(ge[:, b, :].rearrange("p (z n) -> p z n", z=2), PS[:, 2 * b:2 * b + 2, 0:HT], ACT.Gelu).then_inc(S("gelu_ready"), 1)
                    act.wait_ge(S(f"v{b}_loaded"), i * 32 + 16 * (e // 2) + 16)
                    act.wait_ge(S("o_ready"), i * OT + 1)
                    act.activation(vh[:, e, :], v[:, b, :], ACT.Copy).then_inc(S("vhi_ready"), 1)
                    act.wait_ge(S("wf_ready"), i * GRP + e + 3)
                    act.activation(wh[:, e, :], wf[:, b, :], ACT.Copy).then_inc(S("whi_ready"), 1)

                act.sem_inc(S("gelu_ready"), 2)
                u_hi(0, 0)
                step(0, 0)
                with act.Fori(0, NGRP - 1) as i:
                    for e in range(1, GRP):
                        step(i, e)
                    step(i + 1, 0)
                for e in range(1, GRP):
                    step(NGRP - 1, e, last=(e == GRP - 1))

            @block.gpsimd
            def _(pool):
                pool.memset(ffn[:], 0.0).then_inc(S("o_read"), 1)
                pool.sem_inc(S("h_ready"), 2)
                pool.sem_inc(S("o_ready"), 1)

            @block.vector
            def _(dve):
                def u_lo(i, e):
                    dve.wait_ge(S("uhi_ready"), i * GRP + e + 1)
                    b = e % 2
                    dve.tensor_tensor(ul[:, b].rearrange("p k n -> p (k n)"), u[:, b, :], uh[:, b].rearrange("p k n -> p (k n)").bitcast(F32),
                                      ALU.subtract).then_inc(S("u_split"), 1)

                def add_outputs(i):
                    dve.wait_ge(S("o_read"), i * OT + 1)
                    for o in range(OT):
                        dve.wait_ge(S("o_ready"), i * OT + o + 2)
                        acc = ffn[:, o // 2, (o % 2) * 512:(o % 2 + 1) * 512]
                        dve.tensor_tensor(acc, acc, PS[:, 4 + o % 4, :], ALU.add).then_inc(S("o_read"), 1)

                def step(i, e, last=False):
                    b = e % 2
                    if not last:
                        u_lo(i + (e + 1) // GRP, (e + 1) % GRP)
                    if e == 0 and not isinstance(i, int):
                        add_outputs(i - 1)
                    dve.wait_ge(S("gelu_ready"), i * GRP + e + 3)
                    dve.wait_ge(S("g_loaded"), i * 16 + 16)
                    dve.wait_ge(S("w_split"), i * GRP + e + 1)
                    dve.tensor_tensor(wf[:, b, :].rearrange("p (n t) -> p n t", t=NB), ge[:, b, :].rearrange("p (n t) -> p n t", t=NB),
                                      g[:, :, e, :], ALU.mult).then_inc(S("wf_ready"), 1)
                    dve.wait_ge(S("vhi_ready"), i * GRP + e + 1)
                    dve.tensor_tensor(vl[:, e, :], v[:, b, :], vh[:, e, :].bitcast(F32), ALU.subtract).then_inc(S("v_split"), 1)
                    dve.wait_ge(S("whi_ready"), i * GRP + e + 1)
                    dve.tensor_tensor(wl[:, e, :], wf[:, b, :], wh[:, e, :].bitcast(F32), ALU.subtract).then_inc(S("w_split"), 1)

                for name in ("u_split", "v_split", "wf_ready", "w_split"):
                    dve.sem_inc(S(name), 2)
                u_lo(0, 0)
                step(0, 0)
                with dve.Fori(0, NGRP - 1) as i:
                    for e in range(1, GRP):
                        step(i, e)
                    step(i + 1, 0)
                for e in range(1, GRP):
                    step(NGRP - 1, e, last=(e == GRP - 1))
                add_outputs(NGRP - 1)
                dve.wait_ge(S("o_read"), NGRP * OT + 1)
        ph.meet()


def finish(nc, D, layer, ffn, X, grow, selc, PS):
    with ExitStack() as ctx:
        def sb(name, shape, dt=F32):
            return tile(nc, ctx, name, shape, dt)

        W = {n: sb("f_" + n, s) for n, s in {"x": [P, D_MODEL], "y": [P, D_MODEL], "ln": [P, 2, D_MODEL], "st": [P, 2, 6], "mv": [P, 4]}.items()}
        load_all(nc, [(W["ln"][:], row_bc(D["ln2"], layer))])
        finish_tile(nc, W, ffn, X, grow, selc, PS, 0, 0)
        with nc.Fori(1, NT) as t:
            finish_tile(nc, W, ffn, X, grow, selc, PS, t, 1)


def finish_tile(nc, W, ffn, X, grow, selc, PS, t, cond):
    x, y = W["x"], W["y"]
    with Phase(nc, "x_loaded gb_ready var_ready root_ready row_ready stored dve_step") as ph:
        S = ph.sem
        with nc.Block() as block:
            @block.sync
            def _(sp):
                sp.dma_start(x[:], of_layer(X, t)).then_inc(S("x_loaded"), 16)
                sp.wait_ge(S("row_ready"), 1)
                sp.dma_start(of_layer(X, t), y[:]).then_inc(S("stored"), 16)
                sp.wait_ge(S("stored"), 16)

            @block.tensor
            def _(pe):
                for i in range(2):
                    mm = pe.matmul(PS[:, i, :], selc[:, cond, :], grow[:, 1, i * 512:(i + 1) * 512], start=True, stop=True)
                mm.then_inc(S("gb_ready"), 1)

            @block.scalar
            def _(act):
                act.wait_ge(S("var_ready"), 1)
                act.activation(W["mv"][:, 2:3], W["mv"][:, 2:3], ACT.Sqrt).then_inc(S("root_ready"), 1)

            @block.vector
            def _(dve):
                ch = Chain(dve, S("dve_step"))
                dve.wait_ge(S("gb_ready"), 1)
                f = ffn[:, ds(t, 1), :].rearrange("p a n -> p (a n)")
                ch(dve.tensor_tensor(y[:], f, PS[:, 0:2, :].rearrange("p b n -> p (b n)"), ALU.mult))
                dve.wait_ge(S("x_loaded"), 16)
                ch(dve.scalar_tensor_tensor(y[:], x[:], ALPHA, y[:], ALU.mult, ALU.add))
                post_norm_dve(dve, S, ch, y, x, W["st"], W["mv"], W["ln"])
        ph.meet()


def constants(np):
    i = np.arange(P)
    s, t = i[:, None], i[None, :]
    C = {"c_ident": np.eye(P), "c_ones": np.ones((P, P)), "c_iota": np.tile(i, (P, 1))}
    C["c_selc"] = np.stack([np.stack([np.full(P, float(r == c)) for c in range(2)]) for r in range(2)])
    C["c_blk"] = (s // HD == t // HD)
    C["c_hsel"] = (s // HD == np.arange(2)[None, :])
    r = np.exp(-0.5)
    mid = [(i < HD).astype(float), (i >= HD).astype(float)]
    inc = [(s <= t).astype(float), (s >= t).astype(float)]
    exc = [(s < t).astype(float), (s > t).astype(float)]
    C["c_tri"] = np.stack([-r * np.concatenate([inc[d] - mid[d][:, None], exc[d] - mid[d][:, None], mid[d][:, None]], 1) for d in range(2)], 1)
    C["c_strict"] = np.stack(exc, 1)
    C["c_incl"] = np.stack(inc, 1)
    C["c_strictT"] = np.stack([e.T for e in exc], 1)
    same = [(s // n == t // n).astype(float) for n in (16, 32, 64, 128)]
    C["c_lvl"] = np.stack([same[0]] + [same[k] - same[k - 1] for k in (1, 2, 3)], 1)
    C["c_cum"] = np.stack(inc, 1)
    C["c_negm"] = np.stack([(1 - e.T) * -1e30 for e in inc], 1)
    C["c_dist"] = np.stack([np.maximum(s - t, 0), np.maximum(t - s, 0)], 1)
    C["c_pos"] = np.stack([np.stack([i + 1, P - 1 - i, np.full(P, P)], 1), np.stack([P - i, i, np.full(P, P)], 1)], 1)
    nf = HD // 4
    inv = np.float32(10000.0) ** (-np.arange(nf, dtype=np.float32) / np.float32(nf))
    pos = np.arange(LAT, dtype=np.float32)
    ang = np.concatenate([(pos // 64)[:, None] * inv, (pos % 64)[:, None] * inv], -1).astype(np.float32)
    C["c_cos"] = np.cos(ang).reshape(NT - 1, P, 32).transpose(1, 0, 2)
    C["c_sin"] = np.sin(ang).reshape(NT - 1, P, 32).transpose(1, 0, 2)
    return {n: np.ascontiguousarray(a, dtype=np.float32) for n, a in C.items()}


def layouts(np, I):
    L = DEPTH

    def cols(a, n):
        return a.reshape(L, n, P).transpose(0, 2, 1)

    A = {}
    A["x"] = np.concatenate([I["x_prompt"].reshape(1, P, D_MODEL), I["x_sample"].reshape(NT - 1, P, D_MODEL)])
    A["cond"] = np.stack([I["c_ctx"].reshape(KC, P), I["c"].reshape(KC, P)], -1).transpose(1, 0, 2)
    A["b_mod"] = np.stack([I["b_mod"], I["b_mod"]], 1)
    A["w_mod"] = I["w_mod"]
    w = I["w_in"].reshape(L, KC, P, -1)
    ch = np.concatenate([w[..., 1024:2816], w[..., 2816:3328]], -1).reshape(L, KC, P, CT, P)
    A["w_ch"] = ch.transpose(0, 3, 2, 1, 4)
    A["w_tm"] = np.concatenate([w[..., 0:1024], w[..., 3328:3856]], -1).transpose(0, 2, 1, 3)
    A["prm"] = np.concatenate([
        cols(I["rwkv_mu"], 14), I["rwkv_a0"].reshape(L, 2, 4, P).transpose(0, 3, 1, 2).reshape(L, P, 8),
        cols(I["rwkv_kk"], 4), cols(I["rwkv_ka"], 4), cols(I["rwkv_rk"], 4),
        I["mlstm_conv"].reshape(L, 3, 4, P).transpose(0, 3, 2, 1).reshape(L, P, 12)], -1)
    A["gbias"] = np.repeat(I["mlstm_gate_bias"].reshape(L, 1, 16), P, 1)
    A["lora"] = np.concatenate([I["rwkv_w_up"], I["rwkv_a_up"]], 2).transpose(0, 2, 1, 3)
    A["w0"] = I["rwkv_w0"].reshape(L, 1, 2, 512)
    A["s_rwkv"] = I["state_rwkv"][0].reshape(L, 2, 4, 2, HD, HD).transpose(0, 3, 5, 1, 2, 4).reshape(L, P, 2, 4, HD)
    ret, mc, mn = I["state_ret"][0], I["state_mlstm_c"][0], I["state_mlstm_n"][0]
    c65 = np.concatenate([np.concatenate([ret, np.zeros_like(ret[..., :1])], -1), np.concatenate([mc, mn[..., None]], -1)], 2)
    A["s_la"] = c65.reshape(L, 2, 4, 2, HD, HD + 1).transpose(0, 3, 4, 1, 2, 5).reshape(L, P, 2, 4, HD + 1)
    A["s_m"] = I["state_mlstm_m"][0].reshape(L, 8)
    A["ret_decay"] = I["ret_decay"].reshape(L, 8)
    A["w_out"] = I["w_out"]
    A["g_up"] = I["rwkv_g_up"]
    A["gn"] = np.concatenate([I["ret_gn"], I["rwkv_gn"], I["mlstm_gn"]], -1)
    A["ln1"], A["ln2"] = I["ln1"], I["ln2"]
    A["wq"] = I["peer_wq"].reshape(L, KC, P, 16, P).transpose(0, 3, 2, 1, 4)
    A["keys"] = I["peer_keys"].reshape(L, 16, P, P).transpose(0, 3, 1, 2)
    A["ut"] = I["peer_u"].reshape(L, P, NGRP, GRP, KC, P).transpose(0, 2, 5, 3, 4, 1)
    A["pv"] = I["peer_v"].reshape(L, P, P, D_MODEL)
    return {n: np.ascontiguousarray(a) for n, a in A.items()}


OUTS = {"y": (NT, P, D_MODEL), "o_rwkv": (DEPTH, P, 2, 4, HD), "o_la": (DEPTH, P, 2, 4, HD + 1), "o_m": (DEPTH, 8)}
SCRATCH = {"x_work": (NT, P, D_MODEL), "wts": (NBATCH, P, P, NB)}


def kernel(**inputs):
    import numpy as np
    import concourse.bacc as bacc
    from concourse.bass_utils import run_bass_kernel_spmd as run

    I = {n: np.asarray(a) for n, a in inputs.items()}
    arrays = {**layouts(np, I), **constants(np)}
    nc = bacc.Bacc("TRN2", target_bir_lowering=False, num_devices=1)
    D = {n: nc.dram_tensor(n, a.shape, F32, kind="ExternalInput").ap() for n, a in arrays.items()}
    D |= {n: nc.dram_tensor(n, s, F32).ap() for n, s in SCRATCH.items()}
    D |= {n: nc.dram_tensor(n, s, F32, kind="ExternalOutput").ap() for n, s in OUTS.items()}
    build(nc, D)
    out = run(nc, [arrays], core_ids=[0]).results[0]
    y = out["y"]
    rwkv_s = out["o_rwkv"].reshape(DEPTH, 2, HD, 2, 4, HD).transpose(0, 3, 4, 1, 5, 2).reshape(1, DEPTH, 2, 8, HD, HD)
    la = out["o_la"].reshape(DEPTH, 2, HD, 2, 4, HD + 1).transpose(0, 3, 4, 1, 2, 5).reshape(1, DEPTH, 2, 8, HD, HD + 1)
    c = np.ascontiguousarray
    return (c(y[0:1]), c(y[1:].reshape(1, LAT, D_MODEL)), c(la[:, :, :, 0:4, :, 0:HD]), c(rwkv_s),
            c(la[:, :, :, 4:8, :, 0:HD]), c(la[:, :, :, 4:8, :, HD]), c(out["o_m"].reshape(1, DEPTH, 2, 4)))
```

```python
from contextlib import ExitStack

import concourse.bass as bass
from concourse import mybir

P = 128
D_MODEL = 1024
KC = D_MODEL // P
NT = 5
TOK = NT * P
LAT = TOK - P
HT = TOK // 2
DEPTH = 2
HD = 64
CT_RW = 14
CT = CT_RW + 4
COLS = 1 + P + 1 + LAT + 1
IN = COLS - 2
TM = 1552
ML_V, ML_O, GATES = 1024, 1280, 1536
TOPK = 16
NB = 64
NBATCH = TOK // NB
GRP = 4
NGRP = P // GRP
NPRM = 46
EPS = 1e-5
ALPHA = (2 * DEPTH) ** 0.25

F32 = mybir.dt.float32
U32 = mybir.dt.uint32
F32R = mybir.dt.float32r
ALU = mybir.AluOpType
ACT = mybir.ActivationFunctionType
AX = mybir.AxisListType.X
ds = bass.ds


def tile(nc, ctx, name, shape, dt=F32):
    return ctx.enter_context(nc.sbuf_tensor(f"{name}_{nc.next_id()}", shape, dt))


class Chain:

    def __init__(self, eng, sem):
        self.eng, self.sem, self.n = eng, sem, 0

    def inc(self, ins):
        self.n += 1
        ins.then_inc(self.sem, 1)

    def sync(self):
        self.eng.wait_ge(self.sem, self.n)

    def __call__(self, ins):
        self.inc(ins)
        self.sync()


class Phase:

    def __init__(self, nc, sems):
        self.nc, self.names, self.ctx = nc, sems.split(), ExitStack()

    def __enter__(self):
        self.s = {n: self.ctx.enter_context(self.nc.semaphore(f"{n}_{self.nc.next_id()}")) for n in self.names}
        return self

    def __exit__(self, *a):
        self.ctx.close()

    def sem(self, n):
        return self.s[n]

    def sb(self, name, shape, dt=F32):
        return tile(self.nc, self.ctx, name, shape, dt)

    def meet(self):
        nums = [h.num for h in self.s.values()]
        self.nc.gpsimd.sem_clear(range(min(nums), max(nums) + 1))
        self.nc.all_engine_barrier()


def bc(ap, axis, n):
    v = ap.unsqueeze(axis)
    shape = list(v.shape)
    shape[axis] = n
    return v.to_broadcast(shape)


def of_layer(ap, layer):
    names = " ".join("abcdefg"[:len(ap.shape) - 1])
    rest = names.split()
    return ap[ds(layer, 1)].rearrange(f"l {names} -> (l {rest[0]}) {' '.join(rest[1:])}")


def tile_cols(t):
    return 1 if isinstance(t, int) and t == 0 else t * P + 2


def load_all(nc, loads):
    with Phase(nc, "loaded") as ph:
        with nc.Block() as block:
            @block.sync
            def _(sp):
                for dst, src in loads:
                    sp.dma_start(dst, src).then_inc(ph.sem("loaded"), 16)
                sp.wait_ge(ph.sem("loaded"), 16 * len(loads))
        ph.meet()


def build(nc, D):
    with ExitStack() as ctx:
        def sb(name, shape, dt=F32):
            return tile(nc, ctx, name, shape, dt)

        PS = ctx.enter_context(nc.psum_tensor("PS", [P, 8, 512], F32))
        ident = sb("ident", [P, P])
        ones = sb("ones", [P, P])
        modT = sb("modT", [P, NT, 32])
        grow = sb("grow", [2, 2, D_MODEL])
        selc = sb("selc", [2, 2, P])
        X = D["x_work"]

        load_all(nc, [(ident[:], D["c_ident"]), (ones[:], D["c_ones"]), (selc[:], D["c_selc"]), (X, D["x"])])

        with nc.Fori(0, DEPTH) as layer:
            modulation(nc, D, layer, modT, grow, PS, ident)
            with ExitStack() as mixer:
                def mb(name, shape, dt=F32):
                    return tile(nc, mixer, name, shape, dt)

                B = {"chan": mb("chan", [P, CT, COLS]),
                     "tokm": mb("tokm", [P, NT, TM]),
                     "prm": mb("prm", [P, NPRM])}
                with nc.sbuf_tensor("hT", [P, KC, TOK], F32) as hT:
                    normalise(nc, X, hT, modT, 0, PS, ident)
                    project_in(nc, D, layer, hT, B, PS)
                B["kkn"] = mb("kkn", [P, 4, IN])
                B["gates"] = mb("gates", [P, NT, 16])
                prepare(nc, D, layer, B, PS)
                B["Y"] = mb("Y", [P, NT, D_MODEL])
                rwkv(nc, D, layer, B, PS, ident, ones)
                linear(nc, D, layer, B, PS, ident, ones)
                mix_out(nc, D, layer, B, X, grow, selc, PS, ident)
            with ExitStack() as ex:
                hh, hl = tile(nc, ex, "hh", [P, KC, TOK], F32R), tile(nc, ex, "hl", [P, KC, TOK], F32R)
                with ExitStack() as choice:
                    h2T = tile(nc, choice, "h2T", [P, KC, TOK])
                    normalise(nc, X, h2T, modT, 16, PS, ident)
                    route(nc, D, layer, h2T, PS, ident)
                    split_rows(nc, h2T, hh, hl, PS)
                ffn = tile(nc, ex, "ffn", [P, NT, D_MODEL])
                experts(nc, D, layer, hh, hl, ffn, PS)
                finish(nc, D, layer, ffn, X, grow, selc, PS)
        load_all(nc, [(D["y"], X)])


def modulation(nc, D, layer, modT, grow, PS, ident):
    NW, HALF = 3, 3 * D_MODEL
    with Phase(nc, "cond_loaded bias_loaded w0_loaded w1_loaded w2_loaded silu_ready w_used rows_ready cols_ready mod_ready") as ph:
        S = ph.sem
        cond = ph.sb("cond", [P, KC, 2])
        scond = ph.sb("scond", [P, KC, 2])
        bmod = ph.sb("bmod", [2, 6 * D_MODEL])
        mrow = ph.sb("mrow", [2, 6 * D_MODEL])
        wm = ph.sb("wm", [P, NW, HALF])
        with nc.Block() as block:
            @block.sync
            def _(sp):
                sp.dma_start(cond[:], D["cond"]).then_inc(S("cond_loaded"), 16)
                sp.dma_start(bmod[:], of_layer(D["b_mod"], layer)).then_inc(S("bias_loaded"), 16)
                for i in range(16):
                    hf, kc = divmod(i, 8)
                    if i >= NW:
                        sp.wait_ge(S("w_used"), i - NW + 1)
                    sp.dma_start(wm[:, i % NW, :], of_layer(D["w_mod"], layer)[kc * P:(kc + 1) * P, hf * HALF:(hf + 1) * HALF]).then_inc(S(f"w{i % NW}_loaded"), 16)

            @block.scalar
            def _(act):
                act.wait_ge(S("cond_loaded"), 16)
                act.activation(scond[:], cond[:], ACT.Silu).then_inc(S("silu_ready"), 1)

            @block.tensor
            def _(pe):
                pe.wait_ge(S("silu_ready"), 1)
                for i in range(16):
                    hf, kc = divmod(i, 8)
                    pe.wait_ge(S(f"w{i % NW}_loaded"), 16 * (i // NW + 1))
                    if i == 8:
                        pe.wait_ge(S("rows_ready"), 1)
                    for n in range(6):
                        mm = pe.matmul(PS[0:2, n, :], scond[:, kc, :], wm[:, i % NW, n * 512:(n + 1) * 512],
                                       start=(kc == 0), stop=(kc == 7))
                    mm.then_inc(S("w_used"), 1)
                pe.wait_ge(S("rows_ready"), 2)
                for k, sec in enumerate((0, 1, 3, 4)):
                    for c in range(KC):
                        j = k * KC + c
                        mm = pe.transpose(PS[:, 6, 2 * j:2 * j + 2],
                                          mrow[:, (sec * KC + c) * P:(sec * KC + c + 1) * P], ident[0:2, 0:2])
                mm.then_inc(S("cols_ready"), 1)

            @block.vector
            def _(dve):
                dve.wait_ge(S("bias_loaded"), 16)
                for hf in range(2):
                    dve.wait_ge(S("w_used"), 8 * hf + 8)
                    dve.tensor_tensor(mrow[:, hf * HALF:(hf + 1) * HALF], PS[0:2, 0:6, :].rearrange("p b n -> p (b n)"),
                                      bmod[:, hf * HALF:(hf + 1) * HALF], ALU.add).then_inc(S("rows_ready"), 1)
                dve.wait_ge(S("rows_ready"), 2)
                dve.tensor_copy(grow[:, 0, :], mrow[:, 2 * D_MODEL:3 * D_MODEL]).then_inc(S("mod_ready"), 1)
                dve.tensor_copy(grow[:, 1, :], mrow[:, 5 * D_MODEL:6 * D_MODEL]).then_inc(S("mod_ready"), 1)
                dve.wait_ge(S("cols_ready"), 1)
                cols = PS[:, 6, 0:64].rearrange("p (j c) -> p c j", c=2)
                dve.tensor_copy(modT[:, 0, :], cols[:, 0, :]).then_inc(S("mod_ready"), 1)
                dve.tensor_copy(modT[:, 1:NT, :], bc(cols[:, 1, :], 1, NT - 1)).then_inc(S("mod_ready"), 1)
                dve.wait_ge(S("mod_ready"), 4)
                for c in (8, 24):
                    dve.tensor_scalar(modT[:, :, c:c + 8], modT[:, :, c:c + 8], 1.0, None, ALU.add).then_inc(S("mod_ready"), 1)
                dve.wait_ge(S("mod_ready"), 6)
        ph.meet()


def normalise(nc, X, hT, modT, first, PS, ident):
    with Phase(nc, "x_loaded stats_ready var_ready root_ready inv_ready norm_ready turned columns_ready") as ph:
        S = ph.sem
        x = ph.sb("nx", [P, NT, D_MODEL])
        xn = ph.sb("nxn", [P, 2, D_MODEL])
        st = ph.sb("nst", [P, NT, 2, 6])
        mv = ph.sb("nmv", [P, NT, 2])
        rs = ph.sb("nrs", [P, 2, NT])
        with nc.Block() as block:
            @block.sync
            def _(sp):
                for t in range(NT):
                    sp.dma_start(x[:, t, :], X[t]).then_inc(S("x_loaded"), 16)

            @block.vector
            def _(dve):
                dve.wait_ge(S("x_loaded"), 16 * NT)
                for t in range(NT):
                    for z in range(2):
                        dve.bn_stats(st[:, t, z, :], x[:, t, z * 512:(z + 1) * 512]).then_inc(S("stats_ready"), 1)
                for t in range(NT):
                    dve.wait_ge(S("stats_ready"), 2 * t + 2)
                    dve.bn_aggr(mv[:, t, :], st[:, t, :, :]).then_inc(S("stats_ready"), 1)
                dve.wait_ge(S("stats_ready"), 3 * NT)
                dve.tensor_scalar(rs[:, 0, :], mv[:, :, 1], EPS, None, ALU.add).then_inc(S("var_ready"), 1)
                dve.wait_ge(S("root_ready"), 1)
                dve.reciprocal(rs[:, 1, :], rs[:, 0, :]).then_inc(S("inv_ready"), 1)
                dve.wait_ge(S("inv_ready"), 1)
                for t in range(NT):
                    if t >= 2:
                        dve.wait_ge(S("turned"), t - 1)
                    dve.tensor_scalar(xn[:, t % 2, :], x[:, t, :], mv[:, t, 0:1], rs[:, 1, t:t + 1], ALU.subtract, ALU.mult).then_inc(S("norm_ready"), 1)

            @block.scalar
            def _(act):
                act.wait_ge(S("var_ready"), 1)
                act.activation(rs[:, 0, :], rs[:, 0, :], ACT.Sqrt).then_inc(S("root_ready"), 1)
                for t in range(NT):
                    act.wait_ge(S("turned"), t + 1)
                    for k in range(KC):
                        act.activation(hT[:, k, t * P:(t + 1) * P], PS[:, 2 * (t % 4) + k // 4, (k % 4) * P:(k % 4 + 1) * P], ACT.Identity,
                                       scale=modT[:, t, first + 8 + k:first + 9 + k], bias=modT[:, t, first + k:first + k + 1]).then_inc(S("columns_ready"), 1)
                act.wait_ge(S("columns_ready"), KC * NT)

            @block.tensor
            def _(pe):
                for t in range(NT):
                    if t >= 4:
                        pe.wait_ge(S("columns_ready"), KC * (t - 3))
                    pe.wait_ge(S("norm_ready"), t + 1)
                    for k in range(KC):
                        mm = pe.transpose(PS[:, 2 * (t % 4) + k // 4, (k % 4) * P:(k % 4 + 1) * P], xn[:, t % 2, k * P:(k + 1) * P], ident[:])
                    mm.then_inc(S("turned"), 1)
        ph.meet()


def project_in(nc, D, layer, hT, B, PS):
    chan, tokm, prm = B["chan"], B["tokm"], B["prm"]
    with Phase(nc, "prm_loaded pads_zero wa_loaded wb_loaded acc_ready acc_read ta_loaded tb_loaded tacc_ready tacc_read") as ph:
        S = ph.sem
        wt = ph.sb("wt", [P, 2, KC, P])
        wk = ph.sb("wk", [P, 2, KC, 512])
        WL = ["wa_loaded", "wb_loaded"]
        TL = ["ta_loaded", "tb_loaded"]
        widths = [512, 512, 512, TM - 1536]
        with nc.Block() as block:
            @block.sync
            def _(sp):
                sp.dma_start(prm[:], of_layer(D["prm"], layer)).then_inc(S("prm_loaded"), 16)
                sp.wait_ge(S("prm_loaded"), 16)
                with sp.Fori(0, CT // 2) as i:
                    for b in range(2):
                        sp.wait_ge(S("acc_ready"), i * 2 + b + 1)
                        sp.dma_start(wt[:, b], of_layer(of_layer(D["w_ch"], layer), i * 2 + b)).then_inc(S(WL[b]), 16)
                w_tm = of_layer(D["w_tm"], layer)
                for i, w in enumerate(widths):
                    if i >= 2:
                        sp.wait_ge(S("tacc_ready"), NT * (i - 1))
                    sp.dma_start(wk[:, i % 2, :, 0:w], w_tm[:, :, i * 512:i * 512 + w]).then_inc(S(TL[i % 2]), 16)

            @block.gpsimd
            def _(pool):
                for c in (0, 1 + P, COLS - 1):
                    pool.memset(chan[:, :, c:c + 1], 0.0).then_inc(S("pads_zero"), 1)
                pool.wait_ge(S("pads_zero"), 3)

            @block.tensor
            def _(pe):
                pe.sem_inc(S("acc_ready"), 2)
                with pe.Fori(0, CT // 2) as i:
                    for b in range(2):
                        pe.wait_ge(S(WL[b]), i * 16 + 16)
                        pe.wait_ge(S("acc_read"), i * 4 + 2 * b + 2)
                        for k in range(KC):
                            pe.matmul(PS[:, 2 * b, :], wt[:, b, k, :], hT[:, k, P:TOK], start=(k == 0), stop=(k == KC - 1))
                            mm = pe.matmul(PS[:, 2 * b + 1, 0:P], wt[:, b, k, :], hT[:, k, 0:P], start=(k == 0), stop=(k == KC - 1))
                        mm.then_inc(S("acc_ready"), 1)
                n = 0
                for i, w in enumerate(widths):
                    pe.wait_ge(S(TL[i % 2]), 16 * (i // 2 + 1))
                    for t in range(NT):
                        if n >= 4:
                            pe.wait_ge(S("tacc_read"), n - 3)
                        for k in range(KC):
                            mm = pe.matmul(PS[:, 4 + n % 4, 0:w], hT[:, k, t * P:(t + 1) * P], wk[:, i % 2, k, 0:w],
                                           start=(k == 0), stop=(k == KC - 1))
                        mm.then_inc(S("tacc_ready"), 1)
                        n += 1

            @block.scalar
            def _(act):
                act.sem_inc(S("acc_read"), 4)
                with act.Fori(0, CT // 2) as i:
                    for b in range(2):
                        act.wait_ge(S("acc_ready"), i * 2 + b + 3)
                        act.activation(chan[:, ds(i * 2 + b, 1), P + 2:P + 2 + LAT].rearrange("p a n -> p (a n)"),
                                       PS[:, 2 * b, :], ACT.Copy).then_inc(S("acc_read"), 1)
                        act.activation(chan[:, ds(i * 2 + b, 1), 1:P + 1].rearrange("p a n -> p (a n)"),
                                       PS[:, 2 * b + 1, 0:P], ACT.Copy).then_inc(S("acc_read"), 1)
                act.wait_ge(S("acc_read"), 4 + 2 * CT)

            @block.vector
            def _(dve):
                n = 0
                for i, w in enumerate(widths):
                    for t in range(NT):
                        dve.wait_ge(S("tacc_ready"), n + 1)
                        dve.tensor_copy(tokm[:, t, i * 512:i * 512 + w], PS[:, 4 + n % 4, 0:w]).then_inc(S("tacc_read"), 1)
                        n += 1
                dve.wait_ge(S("tacc_read"), n)
        ph.meet()


def prepare(nc, D, layer, B, PS):
    chan, tokm, prm, kkn, gates = B["chan"], B["tokm"], B["prm"], B["kkn"], B["gates"]
    with Phase(nc, "c_loaded shifted conv_ready silu_done low_done key_ready square_ready sums_ready root_ready z_ready ln_ready dve_step act_step") as ph:
        S = ph.sem
        tmp = ph.sb("tmp", [P, CT_RW, IN])
        blk = ph.sb("blk", [P, P])
        cos = ph.sb("cos", [P, NT - 1, 32])
        sin = ph.sb("sin", [P, NT - 1, 32])
        gbias = ph.sb("gbias", [P, 16])
        lz = ph.sb("lz", [P, NT, 2, 4])
        loads = [(blk[:], D["c_blk"]), (cos[:], D["c_cos"]), (sin[:], D["c_sin"]),
                 (gbias[:], of_layer(D["gbias"], layer))]
        rw, ml = chan[:, 0:CT_RW, :], chan[:, CT_RW:CT, :]
        conv = prm[:, 34:46].rearrange("p (c j) -> p j c", j=3)
        g4 = gates[:].rearrange("p t (d x h) -> p t d x h", d=2, x=2)
        logf = [g4[:, :, d, 1, :] for d in range(2)]
        t2, t3 = tmp[:, 0:4, :], tmp[:, 4:8, :]
        with nc.Block() as block:
            @block.sync
            def _(sp):
                for dst, src in loads:
                    sp.dma_start(dst, src).then_inc(S("c_loaded"), 16)

            @block.vector
            def _(dve):
                ch = Chain(dve, S("dve_step"))
                ch(dve.tensor_tensor(tmp[:], rw[:, :, 0:IN], rw[:, :, 2:IN + 2], ALU.add))
                ch(dve.scalar_tensor_tensor(tmp[:], tmp[:], 0.5, rw[:, :, 1:IN + 1], ALU.mult, ALU.subtract))
                ch(dve.tensor_tensor(tmp[:], tmp[:], bc(prm[:, 0:CT_RW], 2, IN), ALU.mult))
                dve.tensor_tensor(rw[:, :, 1:IN + 1], rw[:, :, 1:IN + 1], tmp[:], ALU.add).then_inc(S("shifted"), 1)
                dve.wait_ge(S("shifted"), 1)
                dve.tensor_tensor(kkn[:], rw[:, 4:8, 1:IN + 1], bc(prm[:, 22:26], 2, IN), ALU.mult).then_inc(S("key_ready"), 1)
                t0, t1 = tmp[:, 4:8, :], tmp[:, 8:12, :]
                ch(dve.tensor_tensor(t0, ml[:, :, 0:IN], bc(conv[:, 0, :], 2, IN), ALU.mult))
                ch(dve.tensor_tensor(t1, ml[:, :, 1:IN + 1], bc(conv[:, 1, :], 2, IN), ALU.mult))
                ch(dve.tensor_tensor(t0, t0, t1, ALU.add))
                ch(dve.tensor_tensor(t1, ml[:, :, 2:IN + 2], bc(conv[:, 2, :], 2, IN), ALU.mult))
                dve.tensor_tensor(t0, t0, t1, ALU.add).then_inc(S("conv_ready"), 1)
                dve.wait_ge(S("c_loaded"), 16 * len(loads))
                dve.tensor_tensor(gates[:], tokm[:, :, GATES:TM], bc(gbias[:], 1, NT), ALU.add).then_inc(S("z_ready"), 1)
                qk = tokm[:, 1:NT, 0:512].rearrange("p t (h z i) -> p t h z i", h=8, z=2)
                x1, x2 = qk[:, :, :, 0, :], qk[:, :, :, 1, :]
                cb, sbb = bc(cos[:], 2, 8), bc(sin[:], 2, 8)
                r = [tmp[:, 8:14, :].rearrange("p a n -> p (a n)")[:, i * 1024:(i + 1) * 1024].rearrange("p (t h i) -> p t h i", t=4, h=8) for i in range(3)]
                dve.wait_ge(S("conv_ready"), 1)
                ch.inc(dve.tensor_tensor(r[0], x1, cb, ALU.mult))
                ch.inc(dve.tensor_tensor(r[1], x2, sbb, ALU.mult))
                ch(dve.tensor_tensor(r[2], x1, sbb, ALU.mult))
                ch(dve.tensor_tensor(x1, r[0], r[1], ALU.subtract))
                ch(dve.tensor_tensor(r[0], x2, cb, ALU.mult))
                ch(dve.tensor_tensor(x2, r[0], r[2], ALU.add))
                ch(dve.tensor_scalar(tokm[:, :, 256:512], tokm[:, :, 256:512], HD ** -0.5, None, ALU.mult))
                dve.wait_ge(S("silu_done"), 1)
                ch(dve.tensor_scalar(ml[:, 2:4, 1:IN + 1], ml[:, 2:4, 1:IN + 1], HD ** -0.5, None, ALU.mult))
                for i in range(8):
                    dve.wait_ge(S("sums_ready"), i + 1)
                    a = (0, 321)[i % 2]
                    n = (321, IN - 321)[i % 2]
                    dve.tensor_scalar(t3[:, i // 2, a:a + n], PS[:, i, 0:n], 1e-24, None, ALU.max).then_inc(S("ln_ready"), 1)
                dve.wait_ge(S("root_ready"), 1)
                ch(dve.tensor_scalar(t3, t3, 1e-12, None, ALU.max))
                ch(dve.reciprocal(t3, t3))
                ch(dve.tensor_tensor(kkn[:], kkn[:], t3, ALU.mult))
                dve.wait_ge(S("act_step"), 4)
                for d in range(2):
                    ch(dve.tensor_scalar(logf[d], logf[d], 0.0, None, ALU.min))
                    ch(dve.tensor_tensor(logf[d], logf[d], lz[:, :, d, :], ALU.subtract))

            @block.scalar
            def _(act):
                act.wait_ge(S("shifted"), 1)
                act.activation(chan[0:64, 12, 1:IN + 1], chan[0:64, 12, 1:IN + 1], ACT.Tanh).then_inc(S("low_done"), 1)
                act.activation(chan[:, 13, 1:IN + 1], chan[:, 13, 1:IN + 1], ACT.Sigmoid).then_inc(S("low_done"), 1)
                act.wait_ge(S("key_ready"), 1)
                act.activation(t2, kkn[:], ACT.Square).then_inc(S("square_ready"), 1)
                act.wait_ge(S("conv_ready"), 1)
                act.activation(ml[:, :, 1:IN + 1], tmp[:, 4:8, :], ACT.Silu).then_inc(S("silu_done"), 1)
                act.wait_ge(S("z_ready"), 1)
                for d in range(2):
                    act.activation(lz[:, :, d, :], logf[d], ACT.Abs).then_inc(S("act_step"), 1)
                act.wait_ge(S("act_step"), 2)
                act.activation(lz[:], lz[:], ACT.Exp, scale=-1.0).then_inc(S("act_step"), 1)
                act.wait_ge(S("act_step"), 3)
                act.activation(lz[:], lz[:], ACT.Ln, bias=1.0).then_inc(S("act_step"), 1)
                act.wait_ge(S("ln_ready"), 8)
                act.activation(t3, t3, ACT.Sqrt).then_inc(S("root_ready"), 1)
                act.wait_ge(S("low_done"), 2)

            @block.tensor
            def _(pe):
                pe.wait_ge(S("square_ready"), 1)
                pe.wait_ge(S("c_loaded"), 16 * len(loads))
                for i in range(8):
                    a = (0, 321)[i % 2]
                    n = (321, IN - 321)[i % 2]
                    pe.matmul(PS[:, i, 0:n], blk[:], t2[:, i // 2, a:a + n], start=True, stop=True).then_inc(S("sums_ready"), 1)
        ph.meet()


def rwkv(nc, D, layer, B, PS, ident, ones):
    with ExitStack() as ctx:
        W = {n: tile(nc, ctx, "r_" + n, s) for n, s in {
            "tri": [P, 2, 257],
            "strict": [P, 2, P], "incl": [P, 2, P], "strictT": [P, 2, P],
            "lvl": [P, 4, P],
            "lora": [P, 2, 512],
            "w0": [1, 2, 512],
            "state": [P, 2, 4, HD]}.items()}
        for n, s in {"s0": [P, 4, HD], "low": [P, P], "vt": [P, 512], "eM": [P, 4], "ePC": [P, 4],
                     "bt": [P, 4, P], "kt": [P, 4, P], "KR": [P, 4, 2, P], "btk": [P, 512], "ktk": [P, 512],
                     "G": [P, 4, 3, P], "L": [P, 4, P], "E": [P, 4, P], "ET": [P, 4, P], "Z": [P, 4, P], "ZT": [P, 4, P]}.items():
            W[n] = [tile(nc, ctx, f"r_{n}{d}", s) for d in range(2)]
        W["sg"], W["a"], W["eN"], W["v"] = W["E"], W["Z"], W["ET"], W["ZT"]
        load_all(nc, [(W["tri"][:], D["c_tri"]), (W["strict"][:], D["c_strict"]), (W["incl"][:], D["c_incl"]),
                      (W["strictT"][:], D["c_strictT"]), (W["lvl"][:], D["c_lvl"]),
                      (W["lora"][:], of_layer(D["lora"], layer)), (W["w0"][:], of_layer(D["w0"], layer))])
        with Phase(nc, "zeroed") as ph:
            with nc.Block() as block:
                @block.gpsimd
                def _(pool):
                    pool.memset(W["state"][:], 0.0).then_inc(ph.sem("zeroed"), 1)
                    pool.memset(B["Y"][:], 0.0).then_inc(ph.sem("zeroed"), 1)
                    pool.wait_ge(ph.sem("zeroed"), 2)
            ph.meet()
        rwkv_tiles(nc, B, W, PS, ident, ones, (0, 0))
        load_all(nc, [(of_layer(D["o_rwkv"], layer), W["state"][:])])
        load_all(nc, [(W["state"][:], of_layer(D["s_rwkv"], layer))])
        with nc.Fori(0, NT - 1) as j:
            rwkv_tiles(nc, B, W, PS, ident, ones, (j + 1, 4 - j))


def rwkv_tiles(nc, B, W, PS, ident, ones, tiles):
    chan, prm, kkn, Y, state = B["chan"], B["prm"], B["kkn"], B["Y"], W["state"]
    names = ("cur_ready z_ready a_ready vt_turned sg_ready rate_ready vt_ready cum_ready exp_ready feat_ready tok_turned tok_ready "
             "g_ready g_read l_ready inv_start pow_ready pow_dve pow_act lm_ready merge_ready merge_act merge_dve "
             "rh_ready rhn_ready sa_ready sas_ready y_ready half_done")
    HEADS = [(h, h // 2, slice(64 * (h % 2), 64 * (h % 2) + 64), 2 * (h % 2) + h // 2) for h in range(4)]

    with Phase(nc, "dve_step " + " ".join(f"{n}{d}" for n in names.split() for d in range(2))) as ph:
        def S(name, d):
            return ph.sem(f"{name}{d}")

        def four(d, b, n=P):
            return PS[:, 4 * d + b, 0:4 * n].rearrange("p (h n) -> p h n", n=n)

        def parity(d, b, n):
            return PS[:, 4 * d + b:4 * d + b + 2, 0:2 * n].rearrange("p x (j n) -> p x j n", n=n)

        with nc.Block() as block:
            @block.scalar
            def _(act):
                for d in range(2):
                    c0 = tile_cols(tiles[d])
                    act.activation(W["low"][d][:], chan[:, 12, ds(c0, P)], ACT.Copy).then_inc(S("cur_ready", d), 1)
                    act.activation(W["v"][d][:], chan[:, 8:12, ds(c0, P)], ACT.Copy).then_inc(S("cur_ready", d), 1)
                for d in range(2):
                    act.wait_ge(S("z_ready", d), 1)
                    act.activation(W["sg"][d][:].rearrange("p h n -> p (h n)"), PS[:, 4 * d, :], ACT.Sigmoid).then_inc(S("sg_ready", d), 1)
                    act.wait_ge(S("a_ready", d), 1)
                    for c in range(4):
                        act.activation(W["a"][d][:, c, :], four(d, 1)[:, c, :], ACT.Sigmoid,
                                       bias=prm[:, 14 + 4 * d + c:15 + 4 * d + c]).then_inc(S("rate_ready", d), 1)
                    act.wait_ge(S("vt_turned", d), 1)
                    act.activation(W["vt"][d][:], PS[:, 4 * d + 2, :], ACT.Copy).then_inc(S("vt_ready", d), 1)
                for d in range(2):
                    act.wait_ge(S("cum_ready", d), 1)
                    act.activation(W["eN"][d][:], four(d, 3), ACT.Exp, scale=-1.0).then_inc(S("exp_ready", d), 1)
                    act.activation(W["KR"][d][:, :, 1, :], four(d, 3), ACT.Exp).then_inc(S("exp_ready", d), 1)
                    act.activation(W["KR"][d][:, :, 0, :], four(d, 0), ACT.Exp).then_inc(S("exp_ready", d), 1)
                    act.activation(W["eM"][d][:], PS[:, 4 * d + 1, 0:4], ACT.Exp).then_inc(S("exp_ready", d), 1)
                for d in range(2):
                    act.wait_ge(S("tok_turned", d), 1)
                    act.activation(W["btk"][d][:], PS[:, 4 * d + 2, :], ACT.Copy).then_inc(S("tok_ready", d), 1)
                    act.activation(W["ktk"][d][:], PS[:, 4 * d + 1, :], ACT.Copy).then_inc(S("tok_ready", d), 1)
                for half in range(2):
                    for k in range(3):
                        for d in range(2):
                            act.wait_ge(S("pow_ready", d), 4 * half + k + 1)
                            act.activation(W["E"][d][:], four(d, 0), ACT.Copy).then_inc(S("pow_act", d), 1)
                            act.activation(W["ET"][d][:], four(d, 1), ACT.Copy).then_inc(S("pow_act", d), 1)
                    for k in range(3):
                        for d in range(2):
                            act.wait_ge(S("merge_ready", d), 6 * half + 2 * k + 1)
                            act.activation(W["E"][d][:], four(d, 0), ACT.Copy).then_inc(S("merge_act", d), 1)
                    for d in range(2):
                        act.wait_ge(S("rh_ready", d), half + 1)
                        act.activation(W["L"][d][:, 0:2, :].rearrange("p j (x n) -> p x j n", x=2), parity(d, 0, HD), ACT.Copy,
                                       scale=-1.0).then_inc(S("rhn_ready", d), 1)
                    for d in range(2):
                        act.wait_ge(S("sa_ready", d), half + 1)
                        act.activation(W["L"][d][:, 2:4, :].rearrange("p j n -> p (j n)"), PS[:, 4 * d + 2, 0:4 * HD], ACT.Copy).then_inc(S("sas_ready", d), 1)

            @block.vector
            def _(dve):
                ch = Chain(dve, ph.sem("dve_step"))
                for d in range(2):
                    c0 = tile_cols(tiles[d])
                    r, k = chan[:, 0:4, ds(c0, P)], chan[:, 4:8, ds(c0, P)]
                    kk = kkn[:, :, ds(c0 - 1, P)]
                    kt, bt, KR, a, eN = (W[n][d] for n in ("kt", "bt", "KR", "a", "eN"))
                    dve.wait_ge(S("rate_ready", d), 4)
                    for c in range(4):
                        ch.inc(dve.tensor_scalar(kt[:, c, :], a[:, c, :], 1.0, prm[:, 26 + c:27 + c], ALU.subtract, ALU.mult))
                    ch(dve.tensor_tensor(bt[:], kk, a[:], ALU.mult))
                    ch(dve.scalar_tensor_tensor(kt[:], kt[:], 1.0, k, ALU.add, ALU.mult))
                    dve.wait_ge(S("exp_ready", d), 4)
                    ch.inc(dve.tensor_copy(W["ePC"][d][:], KR[:, :, 1, P - 1 if d == 0 else 0]))
                    ch.sync()
                    dve.tensor_tensor(bt[:], bt[:], eN[:], ALU.mult).then_inc(S("feat_ready", d), 1)
                    dve.tensor_tensor(kt[:], kt[:], eN[:], ALU.mult).then_inc(S("feat_ready", d), 1)
                    dve.tensor_tensor(KR[:, :, 0, :], KR[:, :, 0, :], kk, ALU.mult).then_inc(S("feat_ready", d), 1)
                    dve.tensor_tensor(KR[:, :, 1, :], KR[:, :, 1, :], r, ALU.mult).then_inc(S("feat_ready", d), 1)
                    dve.tensor_tensor(W["s0"][d][:], state[:, d], bc(W["eM"][d][:], 2, HD), ALU.mult).then_inc(S("feat_ready", d), 1)
                for half in range(2):
                    for d in range(2):
                        E, G = W["E"][d], W["G"][d]
                        for h, j, q, s in HEADS:
                            dve.wait_ge(S("g_ready", d), 4 * half + h + 1)
                            g = PS[:, 4 * d + h, :].rearrange("p (x y n) -> p x y n", x=2, y=2)
                            dve.tensor_tensor(E[:, s, :], g[:, 0, 0, :], W["strict"][:, d, :], ALU.mult).then_inc(S("g_read", d), 1)
                            dve.tensor_tensor(G[:, h, 0, :], g[:, 1, 0, :], W["strict"][:, d, :], ALU.mult).then_inc(S("g_read", d), 1)
                            dve.tensor_tensor(G[:, h, 1:3, :], g[:, :, 1, :], bc(W["incl"][:, d, :], 1, 2), ALU.mult).then_inc(S("g_read", d), 1)
                    for d in range(2):
                        L, E, ET = W["L"][d], W["E"][d], W["ET"][d]
                        dve.wait_ge(S("l_ready", d), half + 1)
                        Lp = L[:].rearrange("p (x j) n -> p x j n", x=2)
                        strictT = bc(bc(W["strictT"][:, d, :], 1, 2), 1, 2)
                        ch.inc(dve.tensor_tensor(Lp, parity(d, 0, P), strictT, ALU.mult))
                        dve.wait_ge(S("g_read", d), 12 * half + 12)
                        ch(dve.tensor_tensor(E[:], E[:], bc(W["lvl"][:, 0, :], 1, 4), ALU.mult))
                        ch.inc(dve.tensor_tensor(ET[:], L[:], bc(W["lvl"][:, 0, :], 1, 4), ALU.mult))
                        dve.tensor_tensor(W["Z"][d][:], bc(ident[:], 1, 4), E[:], ALU.subtract).then_inc(S("inv_start", d), 1)
                        ch.sync()
                        dve.tensor_tensor(W["ZT"][d][:], bc(ident[:], 1, 4), ET[:], ALU.subtract).then_inc(S("inv_start", d), 1)
                    for k in range(1, 4):
                        for d in range(2):
                            Z, ZT = W["Z"][d], W["ZT"][d]
                            dve.wait_ge(S("pow_ready", d), 4 * half + k + 1)
                            if k > 1:
                                dve.wait_ge(S("pow_dve", d), 6 * half + 2 * k - 2)
                            else:
                                dve.wait_ge(S("inv_start", d), 2 * half + 2)
                            dve.tensor_tensor(Z[:], Z[:], four(d, 2), ALU.add).then_inc(S("pow_dve", d), 1)
                            dve.tensor_tensor(ZT[:], ZT[:], four(d, 3), ALU.add).then_inc(S("pow_dve", d), 1)
                            if k == 3:
                                dve.tensor_tensor(W["ET"][d][:], W["L"][d][:], bc(W["lvl"][:, 1, :], 1, 4), ALU.mult).then_inc(S("lm_ready", d), 1)
                    for k in range(3):
                        for d in range(2):
                            Z, ZT = W["Z"][d], W["ZT"][d]
                            dve.wait_ge(S("merge_ready", d), 6 * half + 2 * k + 2)
                            if k:
                                dve.wait_ge(S("merge_dve", d), 5 * half + 2 * k)
                            else:
                                dve.wait_ge(S("pow_dve", d), 6 * half + 6)
                            dve.tensor_tensor(Z[:], Z[:], four(d, 2), ALU.subtract).then_inc(S("merge_dve", d), 1)
                            if k < 2:
                                dve.tensor_tensor(ZT[:], ZT[:], four(d, 3), ALU.subtract).then_inc(S("merge_dve", d), 1)
                                dve.tensor_tensor(W["ET"][d][:], W["L"][d][:], bc(W["lvl"][:, k + 2, :], 1, 4), ALU.mult).then_inc(S("lm_ready", d), 1)
                    for d in range(2):
                        dve.wait_ge(S("y_ready", d), 2 * half + 1)
                        yt = Y[:, ds(tiles[d], 1), 256 + 256 * half:512 + 256 * half].rearrange("p a (j x n) -> p (a x) j n", x=2, n=HD)
                        ch.inc(dve.tensor_tensor(yt, yt, parity(d, 0, HD), ALU.add))
                        dve.wait_ge(S("y_ready", d), 2 * half + 2)
                        pairs = PS[:, 4 * d + 3, 0:256].rearrange("p (j x n) -> p j x n", j=2, x=2)
                        js = slice(2 * half, 2 * half + 2)
                        for x in range(2):
                            q = slice(64 * x, 64 * x + 64)
                            ch.inc(dve.tensor_tensor(state[q, d, js, :], W["s0"][d][q, js, :], pairs[q, :, x, :], ALU.add))
                        ch.sync()
                        dve.tensor_tensor(state[:, d, js, :], state[:, d, js, :], bc(W["ePC"][d][:, js], 2, HD), ALU.mult).then_inc(S("half_done", d), 1)
                for d in range(2):
                    dve.wait_ge(S("half_done", d), 2)

            @block.tensor
            def _(pe):
                for d in range(2):
                    b, low = 4 * d, W["low"][d]
                    pe.wait_ge(S("cur_ready", d), 2)
                    pe.matmul(PS[:, b, :], low[0:64, :], W["lora"][0:64, d, :], start=True, stop=False)
                    pe.matmul(PS[:, b, :], ones[0:1, :], W["w0"][0:1, d, :], start=False, stop=True).then_inc(S("z_ready", d), 1)
                    for c in range(4):
                        mm = pe.matmul(PS[:, b + 1, c * P:(c + 1) * P], W["lora"][64:128, d, c * P:(c + 1) * P], low[64:128, :], start=True, stop=True)
                    mm.then_inc(S("a_ready", d), 1)
                    for c in range(4):
                        mm = pe.transpose(PS[:, b + 2, c * P:(c + 1) * P], W["v"][d][:, c, :], ident[:])
                    mm.then_inc(S("vt_turned", d), 1)
                for d in range(2):
                    b = 4 * d
                    pe.wait_ge(S("sg_ready", d), 1)
                    pe.wait_ge(S("rate_ready", d), 4)
                    for c in range(4):
                        w = W["sg"][d][:, c, :]
                        pe.matmul(PS[:, b + 3, c * P:(c + 1) * P], w, W["tri"][:, d, 0:P], start=True, stop=True)
                        pe.matmul(PS[:, b, c * P:(c + 1) * P], w, W["tri"][:, d, P:2 * P], start=True, stop=True)
                        mm = pe.matmul(PS[:, b + 1, c:c + 1], w, W["tri"][:, d, 2 * P:2 * P + 1], start=True, stop=True)
                    mm.then_inc(S("cum_ready", d), 1)
                for d in range(2):
                    b = 4 * d
                    pe.wait_ge(S("vt_ready", d), 1)
                    pe.wait_ge(S("feat_ready", d), 2)
                    for c in range(4):
                        pe.transpose(PS[:, b + 2, c * P:(c + 1) * P], W["bt"][d][:, c, :], ident[:])
                        mm = pe.transpose(PS[:, b + 1, c * P:(c + 1) * P], W["kt"][d][:, c, :], ident[:])
                    mm.then_inc(S("tok_turned", d), 1)
                for half in range(2):
                    for d in range(2):
                        bt, kt, KR = W["bt"][d], W["kt"][d], W["KR"][d]
                        if half:
                            pe.wait_ge(S("half_done", d), 1)
                        else:
                            pe.wait_ge(S("feat_ready", d), 5)
                            pe.wait_ge(S("tok_ready", d), 2)
                        for h, j, q, s in HEADS:
                            kr = KR[q, 2 * half + j].rearrange("p x n -> p (x n)")
                            pe.matmul(PS[:, 4 * d + h, 0:256], bt[q, 2 * half + j, :], kr, start=True, stop=True)
                            pe.matmul(PS[:, 4 * d + h, 256:512], kt[q, 2 * half + j, :], kr, start=True, stop=True).then_inc(S("g_ready", d), 1)
                    for d in range(2):
                        pe.wait_ge(S("g_read", d), 12 * half + 6)
                        for h, j, q, s in HEADS:
                            mm = pe.matmul(PS[:, 4 * d + h % 2, j * P:(j + 1) * P], W["KR"][d][q, 2 * half + j, 0, :],
                                           W["bt"][d][q, 2 * half + j, :], start=True, stop=True)
                        mm.then_inc(S("l_ready", d), 1)
                    for k in range(4):
                        for d in range(2):
                            E, ET, Z, ZT = (W[n][d] for n in ("E", "ET", "Z", "ZT"))
                            if k:
                                pe.wait_ge(S("pow_act", d), 6 * half + 2 * k)
                            else:
                                pe.wait_ge(S("inv_start", d), 2 * half + 2)
                            if k > 1:
                                pe.wait_ge(S("pow_dve", d), 6 * half + 2 * k - 2)
                            for s in range(4):
                                o = slice(s * P, s * P + P)
                                if k < 3:
                                    pe.matmul(PS[:, 4 * d, o], ET[:, s, :], E[:, s, :], start=True, stop=True)
                                    mm = pe.matmul(PS[:, 4 * d + 1, o], E[:, s, :], ET[:, s, :], start=True, stop=True)
                                if k:
                                    pe.matmul(PS[:, 4 * d + 2, o], ET[:, s, :], Z[:, s, :], start=True, stop=True)
                                    mm = pe.matmul(PS[:, 4 * d + 3, o], E[:, s, :], ZT[:, s, :], start=True, stop=True)
                            mm.then_inc(S("pow_ready", d), 1)
                    for k in range(3):
                        for d in range(2):
                            pe.wait_ge(S("lm_ready", d), 3 * half + k + 1)
                            if k:
                                pe.wait_ge(S("merge_dve", d), 5 * half + 2 * k)
                            else:
                                pe.wait_ge(S("pow_dve", d), 6 * half + 6)
                            for s in range(4):
                                mm = pe.matmul(PS[:, 4 * d, s * P:s * P + P], W["ET"][d][:, s, :], W["Z"][d][:, s, :], start=True, stop=True)
                            mm.then_inc(S("merge_ready", d), 1)
                        for d in range(2):
                            E, ZT = W["E"][d], W["ZT"][d]
                            pe.wait_ge(S("merge_act", d), 3 * half + k + 1)
                            for s in range(4):
                                o = slice(s * P, s * P + P)
                                mm = pe.matmul(PS[:, 4 * d + 2, o], ZT[:, s, :], E[:, s, :], start=True, stop=True)
                                if k < 2:
                                    mm = pe.matmul(PS[:, 4 * d + 3, o], E[:, s, :], ZT[:, s, :], start=True, stop=True)
                            mm.then_inc(S("merge_ready", d), 1)
                    for d in range(2):
                        KR, G, s0, vt = (W[n][d] for n in ("KR", "G", "s0", "vt"))
                        for h, j, q, s in HEADS:
                            o, J = slice(j * HD, (j + 1) * HD), 2 * half + j
                            pe.matmul(PS[:, 4 * d + h % 2, o], KR[q, J, 0, :], s0[q, J, :], start=True, stop=False)
                            mm = pe.matmul(PS[:, 4 * d + h % 2, o], G[:, h, 0, :], vt[:, (4 * half + h) * HD:(4 * half + h + 1) * HD], start=False, stop=True)
                        mm.then_inc(S("rh_ready", d), 1)
                    for d in range(2):
                        pe.wait_ge(S("rhn_ready", d), half + 1)
                        pe.wait_ge(S("merge_dve", d), 5 * half + 5)
                        for h, j, q, s in HEADS:
                            mm = pe.matmul(PS[:, 4 * d + 2, h * HD:(h + 1) * HD], W["Z"][d][:, s, :], W["L"][d][:, j, (h % 2) * HD:(h % 2 + 1) * HD],
                                           start=True, stop=True)
                        mm.then_inc(S("sa_ready", d), 1)
                    for d in range(2):
                        KR, G, s0, vt, L = (W[n][d] for n in ("KR", "G", "s0", "vt", "L"))
                        pe.wait_ge(S("sas_ready", d), half + 1)
                        for h, j, q, s in HEADS:
                            o, J, vc = slice(j * HD, (j + 1) * HD), 2 * half + j, slice((4 * half + h) * HD, (4 * half + h + 1) * HD)
                            sa = L[:, 2 + j, (h % 2) * HD:(h % 2 + 1) * HD]
                            pe.matmul(PS[:, 4 * d + h % 2, o], KR[q, J, 1, :], s0[q, J, :], start=True, stop=False)
                            pe.matmul(PS[:, 4 * d + h % 2, o], G[:, h, 1, :], sa, start=False, stop=False)
                            mm = pe.matmul(PS[:, 4 * d + h % 2, o], G[:, h, 2, :], vt[:, vc], start=False, stop=True)
                        mm.then_inc(S("y_ready", d), 1)
                        for j in range(2):
                            o, c = slice(j * P, (j + 1) * P), slice((2 * half + j) * P, (2 * half + j + 1) * P)
                            pe.matmul(PS[:, 4 * d + 3, o], W["btk"][d][:, c], L[:, 2 + j, :], start=True, stop=False)
                            mm = pe.matmul(PS[:, 4 * d + 3, o], W["ktk"][d][:, c], vt[:, c], start=False, stop=True)
                        mm.then_inc(S("y_ready", d), 1)
        ph.meet()


def row_bc(ap, layer):
    v = ap[ds(layer, 1)].partition_broadcast(P)
    names = " ".join("bcdefg"[:len(v.shape) - 2])
    return v.rearrange(f"p a {names} -> p (a {names.split()[0]}) {' '.join(names.split()[1:])}")


def linear(nc, D, layer, B, PS, ident, ones):
    with ExitStack() as ctx:
        def sb(name, shape, dt=F32):
            return tile(nc, ctx, name, shape, dt)

        W = {n: sb("l_" + n, s) for n, s in {
            "cum": [P, 2, P], "negm": [P, 2, P], "dist": [P, 2, P], "pos": [P, 2, 3],
            "rdec": [P, 8], "wret": [P, 2, 4, P], "fret": [P, 2, 3, 4],
            "state": [P, 2, 4, HD + 1],
            "m": [P, 2, 4],
            "qk": [P, 512], "qT": [P, 4, P], "kT": [P, 4, P], "va": [P, 8, HD + 1], "gc": [P, 16],
            "b": [P, 8], "c": [P, 4], "diag": [P, 4, P], "Dm": [P, 4, P], "gl": [P, 4], "g": [P, 4], "mn": [P, 4],
            "sm": [P, 4, 4], "f": [P, 3, 8], "cs": [P, 4], "SC": [P, 8, P], "SCT": [P, 8, P], "ku": [P, 8, HD],
            "num": [P, 8, HD + 1], "den": [P, 4]}.items()}
        load_all(nc, [(W["cum"][:], D["c_cum"]), (W["negm"][:], D["c_negm"]), (W["dist"][:], D["c_dist"]),
                      (W["pos"][:], D["c_pos"]), (W["rdec"][:], row_bc(D["ret_decay"], layer))])
        with Phase(nc, "zeroed lg_ready dist_ready w_ready dve_step") as ph:
            S = ph.sem
            with nc.Block() as block:
                @block.gpsimd
                def _(pool):
                    pool.memset(W["state"][:], 0.0).then_inc(S("zeroed"), 1)
                    pool.memset(W["m"][:], 0.0).then_inc(S("zeroed"), 1)
                    pool.memset(W["va"][:], 1.0).then_inc(S("zeroed"), 1)
                    pool.wait_ge(S("zeroed"), 3)

                @block.scalar
                def _(act):
                    act.activation(W["rdec"][:], W["rdec"][:], ACT.Exp).then_inc(S("lg_ready"), 1)
                    act.wait_ge(S("dist_ready"), 1)
                    act.activation(W["wret"][:], W["wret"][:], ACT.Exp).then_inc(S("w_ready"), 1)
                    act.activation(W["fret"][:], W["fret"][:], ACT.Exp).then_inc(S("w_ready"), 1)
                    act.wait_ge(S("w_ready"), 2)

                @block.vector
                def _(dve):
                    ch = Chain(dve, S("dve_step"))
                    dve.wait_ge(S("lg_ready"), 1)
                    ch(dve.tensor_scalar(W["rdec"][:], W["rdec"][:], -1.0, None, ALU.mult))
                    for d in range(2):
                        for h in range(4):
                            lg = W["rdec"][:, 4 * d + h:4 * d + h + 1]
                            ch.inc(dve.scalar_tensor_tensor(W["wret"][:, d, h, :], W["dist"][:, d, :], lg, W["negm"][:, d, :], ALU.mult, ALU.add))
                            ch.inc(dve.tensor_scalar(W["fret"][:, d, :, h], W["pos"][:, d, :], lg, None, ALU.mult))
                    ch.sync()
                    dve.engine_nop().then_inc(S("dist_ready"), 1)
            ph.meet()
        linear_tiles(nc, B, W, PS, ident, ones, (0, 0))
        load_all(nc, [(of_layer(D["o_la"], layer), W["state"][:]), (D["o_m"][ds(layer, 1), :], W["m"][0:1].rearrange("p d h -> p (d h)"))])
        load_all(nc, [(W["state"][:], of_layer(D["s_la"], layer)), (W["m"][:].rearrange("p d h -> p (d h)"), row_bc(D["s_m"], layer))])
        with nc.Fori(0, NT - 1) as j:
            linear_tiles(nc, B, W, PS, ident, ones, (j + 1, 4 - j))


def linear_tiles(nc, B, W, PS, ident, ones, tiles):
    chan, tokm, gates, Y = B["chan"], B["tokm"], B["gates"], B["Y"]
    state, m, qk, qT, kT, va, gc, b, c, diag, Dm = (W[n] for n in "state m qk qT kT va gc b c diag Dm".split())
    gl, g, mn, sm, f, cs, SC, SCT, ku, num, den = (W[n] for n in "gl g mn sm f cs SC SCT ku num den".split())

    def by_parity(ap):
        return ap.rearrange("p (j x) n -> p x j n", x=2)

    def halves(b, n):
        return PS[:, b:b + 2, 0:4 * n].rearrange("p x (j n) -> p x j n", n=n)

    def heads(bank, n, k=4):
        return PS[:, bank, 0:k * n].rearrange("p (h n) -> p h n", n=n)

    with Phase(nc, "cur_ready v_ready qk_turned qk_ready b_ready diag_ready cb_ready logs_ready w_ready s_ready sc_ready "
                   "sct_turned sct_ready o_ready u_ready chunk_done dve_step") as ph:
        S = ph.sem
        with nc.Block() as block:
            @block.gpsimd
            def _(pool):
                for d in range(2):
                    if d:
                        pool.wait_ge(S("chunk_done"), d)
                    for i, c0 in enumerate((512, ML_V)):
                        pool.tensor_copy(va[:, 4 * i:4 * i + 4, 0:HD], tokm[:, ds(tiles[d], 1), c0:c0 + 256].rearrange("p a (h n) -> p (a h) n", h=4)).then_inc(S("v_ready"), 1)

            @block.scalar
            def _(act):
                for d in range(2):
                    t, c0 = tiles[d], tile_cols(tiles[d])
                    if d:
                        act.wait_ge(S("chunk_done"), d)
                    act.activation(qk[:], tokm[:, ds(t, 1), 0:512].rearrange("p a n -> p (a n)"), ACT.Copy).then_inc(S("cur_ready"), 1)
                    act.activation(gc[:], gates[:, ds(t, 1), :].rearrange("p a n -> p (a n)"), ACT.Copy).then_inc(S("cur_ready"), 1)
                    act.activation(qT[:, 2:4, :], chan[:, 14:16, ds(c0, P)], ACT.Copy).then_inc(S("cur_ready"), 1)
                    act.activation(kT[:, 2:4, :], chan[:, 16:18, ds(c0, P)], ACT.Copy).then_inc(S("cur_ready"), 1)
                    act.wait_ge(S("qk_turned"), d + 1)
                    act.activation(qT[:, 0:2, :], heads(4, P)[:, 0:2, :], ACT.Copy).then_inc(S("qk_ready"), 1)
                    act.activation(kT[:, 0:2, :], heads(4, P)[:, 2:4, :], ACT.Copy).then_inc(S("qk_ready"), 1)
                    act.wait_ge(S("logs_ready"), d + 1)
                    act.activation(Dm[:], Dm[:], ACT.Exp).then_inc(S("w_ready"), 1)
                    act.activation(sm[:], sm[:], ACT.Exp).then_inc(S("w_ready"), 1)
                    act.wait_ge(S("sct_turned"), d + 1)
                    act.activation(SCT[:], PS[:, 4:6, :].rearrange("p b (h n) -> p (b h) n", n=P), ACT.Copy).then_inc(S("sct_ready"), 1)

            @block.vector
            def _(dve):
                ch = Chain(dve, S("dve_step"))
                for d in range(2):
                    dve.wait_ge(S("b_ready"), d + 1)
                    ch(dve.tensor_copy(b[:], PS[:, 0, 0:8]))
                    ch(dve.tensor_tensor(c[:], gc[:, 8 * d:8 * d + 4], b[:, 0:4], ALU.subtract))
                    dve.tensor_tensor(diag[:], bc(ident[:], 1, 4), bc(c[:], 2, P), ALU.mult).then_inc(S("diag_ready"), 1)
                    dve.wait_ge(S("cb_ready"), d + 1)
                    ch.inc(dve.tensor_reduce(gl[:], heads(1, P), AX, ALU.max))
                    ch(dve.tensor_tensor(Dm[:], heads(1, P), bc(W["negm"][:, d, :], 1, 4), ALU.add))
                    ch(dve.tensor_reduce(g[:], Dm[:], AX, ALU.max))
                    ch.inc(dve.tensor_tensor(g[:], g[:], m[:, d, :], ALU.max))
                    ch(dve.tensor_tensor(gl[:], gl[:], m[:, d, :], ALU.max))
                    ch.inc(dve.tensor_tensor(Dm[:], Dm[:], bc(g[:], 2, P), ALU.subtract))
                    ch.inc(dve.tensor_tensor(sm[:, 0, :], m[:, d, :], g[:], ALU.subtract))
                    ch.inc(dve.scalar_tensor_tensor(sm[:, 1, :], b[:, 0:4], -1.0, g[:], ALU.mult, ALU.subtract))
                    ch.inc(dve.tensor_tensor(sm[:, 2, :], c[:], gl[:], ALU.subtract))
                    ch.inc(dve.tensor_tensor(sm[:, 3, :], m[:, d, :], gl[:], ALU.subtract))
                    ch(dve.tensor_tensor(mn[:], b[:, 4:8], gl[:], ALU.add))
                    dve.tensor_copy(m[:, d, :], mn[:]).then_inc(S("logs_ready"), 1)
                    dve.wait_ge(S("w_ready"), 2 * d + 2)
                    ch.inc(dve.tensor_copy(f[:, :, 0:4], W["fret"][:, d]))
                    ch.inc(dve.tensor_copy(f[:, 0, 4:8], sm[:, 0, :]))
                    ch(dve.tensor_copy(f[:, 1:3, 4:8], sm[:, 2:4, :]))
                    ch.inc(dve.tensor_tensor(ku[:, 0:4, :], qk[:, 256:512].rearrange("p (h n) -> p h n", h=4), bc(f[:, 1, 0:4], 2, HD), ALU.mult))
                    ch.inc(dve.tensor_tensor(ku[:, 4:8, :], heads(5, HD), bc(f[:, 1, 4:8], 2, HD), ALU.mult))
                    for x in range(2):
                        q = slice(64 * x, 64 * x + 64)
                        ch.inc(dve.tensor_copy(cs[q, :], f[q, 2, x:8:2]))
                    dve.wait_ge(S("s_ready"), d + 1)
                    ch.inc(dve.tensor_tensor(by_parity(SC[:, 0:4, :]), halves(2, P)[:, :, 0:2, :], by_parity(W["wret"][:, d]), ALU.mult))
                    ch(dve.tensor_tensor(by_parity(SC[:, 4:8, :]), halves(2, P)[:, :, 2:4, :], by_parity(Dm[:]), ALU.mult))
                    dve.engine_nop().then_inc(S("sc_ready"), 1)
                    dve.wait_ge(S("o_ready"), d + 1)
                    ws = bc(f[:, 0, :].rearrange("p (j x) -> p x j", x=2), 3, HD + 1)
                    ch(dve.tensor_tensor(by_parity(num[:]), halves(0, HD + 1), ws, ALU.mult))
                    ch(dve.tensor_tensor(by_parity(num[:]), by_parity(num[:]), halves(6, HD + 1), ALU.add))
                    ch(dve.scalar_tensor_tensor(den[:], num[:, 4:8, HD], -1.0, num[:, 4:8, HD], ALU.mult, ALU.max))
                    ch(dve.tensor_tensor(den[:], den[:], sm[:, 1, :], ALU.max))
                    ch(dve.reciprocal(den[:], den[:]))
                    ch(dve.tensor_tensor(num[:, 4:8, 0:HD], num[:, 4:8, 0:HD], bc(den[:], 2, HD), ALU.mult))
                    for i, o in enumerate((0, 768)):
                        yt = Y[:, ds(tiles[d], 1), o:o + 256].rearrange("p a (h n) -> p (a h) n", h=4)
                        ch.inc(dve.tensor_tensor(yt, yt, num[:, 4 * i:4 * i + 4, 0:HD], ALU.add))
                    dve.wait_ge(S("u_ready"), d + 1)
                    ch(dve.tensor_tensor(state[:, d], state[:, d], bc(cs[:], 2, HD + 1), ALU.mult))
                    for j in range(4):
                        for x in range(2):
                            q = slice(64 * x, 64 * x + 64)
                            o = (j % 3) * 130 + 65 * x
                            ch.inc(dve.tensor_tensor(state[q, d, j, :], state[q, d, j, :], PS[q, 2 + j // 3, o:o + 65], ALU.add))
                    ch.sync()
                    dve.engine_nop().then_inc(S("chunk_done"), 1)
                    dve.wait_ge(S("chunk_done"), d + 1)

            @block.tensor
            def _(pe):
                for d in range(2):
                    pe.wait_ge(S("cur_ready"), 4 * d + 4)
                    pe.matmul(PS[:, 0, 0:4], W["cum"][:, d, :], gc[:, 8 * d + 4:8 * d + 8], start=True, stop=True)
                    pe.matmul(PS[:, 0, 4:8], ones[:], gc[:, 8 * d + 4:8 * d + 8], start=True, stop=True).then_inc(S("b_ready"), 1)
                    for i in range(4):
                        pe.transpose(PS[:, 4, i * P:(i + 1) * P], qk[:, i * P:(i + 1) * P], ident[:])
                    for i in range(2):
                        mm = pe.transpose(PS[:, 5, i * P:(i + 1) * P], kT[:, 2 + i, :], ident[:])
                    mm.then_inc(S("qk_turned"), 1)
                    pe.wait_ge(S("diag_ready"), d + 1)
                    pe.matmul(PS[:, 1, :], ones[:], diag[:].rearrange("p h n -> p (h n)"), start=True, stop=True).then_inc(S("cb_ready"), 1)
                    pe.wait_ge(S("qk_ready"), 2 * d + 2)
                    for h in range(8):
                        j, q = h // 2, slice(64 * (h % 2), 64 * (h % 2) + 64)
                        mm = pe.matmul(PS[:, 2 + h % 2, j * P:(j + 1) * P], qT[q, j, :], kT[q, j, :], start=True, stop=True)
                    mm.then_inc(S("s_ready"), 1)
                    pe.wait_ge(S("sc_ready"), d + 1)
                    for h in range(8):
                        mm = pe.transpose(PS[:, 4 + h // 4, (h % 4) * P:(h % 4 + 1) * P], SC[:, h, :], ident[:])
                    mm.then_inc(S("sct_turned"), 1)
                    for h in range(8):
                        j, q, o = h // 2, slice(64 * (h % 2), 64 * (h % 2) + 64), (h // 2) * 65
                        pe.matmul(PS[:, h % 2, o:o + 65], qT[q, j, :], state[q, d, j, :], start=True, stop=True)
                    pe.wait_ge(S("sct_ready"), d + 1)
                    pe.wait_ge(S("v_ready"), 2 * d + 2)
                    for h in range(8):
                        o = (h // 2) * 65
                        mm = pe.matmul(PS[:, 6 + h % 2, o:o + 65], SCT[:, h, :], va[:, h, :], start=True, stop=True)
                    mm.then_inc(S("o_ready"), 1)
                    for j in range(4):
                        o = (j % 3) * 130
                        mm = pe.matmul(PS[:, 2 + j // 3, o:o + 130], ku[:, 2 * j:2 * j + 2, :].rearrange("p h n -> p (h n)"),
                                       va[:, 2 * j:2 * j + 2, :].rearrange("p h n -> p (h n)"), start=True, stop=True)
                    mm.then_inc(S("u_ready"), 1)
                    pe.wait_ge(S("chunk_done"), d + 1)
        ph.meet()


def mix_out(nc, D, layer, B, X, grow, selc, PS, ident):
    chan, tokm, prm, Y = B["chan"], B["tokm"], B["prm"], B["Y"]
    SEMS = ("x_loaded w_loaded rk_step rk_ready sil_ready og_ready gb_made gbs_ready heads_ready centred squared hvar_ready hroot_ready "
            "mix_ready turned T_ready out_ready out_read var_ready root_ready norm_ready gain_done row_ready stored dve_step")
    with Phase(nc, SEMS) as ph:
        S = ph.sem
        W = {n: ph.sb("m_" + n, s) for n, s in {
            "wo": [P, KC, D_MODEL], "gup": [P, 512], "gn": [P, 2, D_MODEL], "ln": [P, 2, D_MODEL], "hsel": [P, 2],
            "gb": [P, 2, D_MODEL], "x": [P, D_MODEL], "y": [P, 2, D_MODEL], "sq": [P, D_MODEL], "T": [P, KC, P],
            "rk": [P, 4, P], "sil": [P, 256], "og": [P, 256], "bon": [P, 8],
            "mean": [P, 16], "var": [P, 2, 16], "st": [P, 2, 6], "mv": [P, 2, 4]}.items()}
        loads = [(W["gup"][:], of_layer(D["g_up"], layer)), (W["gn"][:], row_bc(D["gn"], layer)), (W["ln"][:], row_bc(D["ln1"], layer)),
                 (W["hsel"][:], D["c_hsel"]), (W["wo"][:], of_layer(D["w_out"], layer).rearrange("(k p) n -> p k n", p=P))]
        x, sq = W["x"], W["sq"]
        with nc.Block() as block:
            @block.sync
            def _(sp):
                for dst, src in loads:
                    sp.dma_start(dst, src).then_inc(S("w_loaded"), 16)
                for t in range(NT):
                    if t:
                        sp.wait_ge(S("var_ready"), t)
                    sp.dma_start(x[:], X[t]).then_inc(S("x_loaded"), 16)
                    if t:
                        sp.wait_ge(S("row_ready"), t)
                        sp.dma_start(X[t - 1], W["y"][:, (t - 1) % 2, :]).then_inc(S("stored"), 16)
                sp.wait_ge(S("row_ready"), NT)
                sp.dma_start(X[NT - 1], W["y"][:, (NT - 1) % 2, :]).then_inc(S("stored"), 16)
                sp.wait_ge(S("stored"), 16 * NT)

            @block.gpsimd
            def _(pool):
                def bonus_products(t):
                    c = slice(tile_cols(t), tile_cols(t) + P)
                    if t:
                        pool.wait_ge(S("heads_ready"), t)
                    pool.tensor_tensor(W["rk"][:], chan[:, 0:4, c], chan[:, 4:8, c], ALU.mult).then_inc(S("rk_step"), 1)
                    pool.wait_ge(S("rk_step"), t + 1)
                    pool.tensor_tensor(W["rk"][:], W["rk"][:], bc(prm[:, 30:34], 2, P), ALU.mult).then_inc(S("rk_ready"), 1)

                bonus_products(0)
                for t in range(NT):
                    if t + 1 < NT:
                        bonus_products(t + 1)
                    y = W["y"][:, t % 2, :]
                    pool.wait_ge(S("norm_ready"), t + 1)
                    pool.tensor_tensor(y, y, W["ln"][:, 0, :], ALU.mult).then_inc(S("gain_done"), 1)
                    pool.wait_ge(S("gain_done"), t + 1)
                    pool.tensor_tensor(y, y, W["ln"][:, 1, :], ALU.add).then_inc(S("row_ready"), 1)

            @block.scalar
            def _(act):
                def gates(t):
                    if t:
                        act.wait_ge(S("mix_ready"), t)
                    act.activation(W["sil"][:], tokm[:, t, 768:1024], ACT.Silu).then_inc(S("sil_ready"), 1)
                    act.activation(W["og"][:], tokm[:, t, ML_O:ML_O + 256], ACT.Sigmoid).then_inc(S("og_ready"), 1)

                def first(t):
                    act.wait_ge(S("centred"), t + 1)
                    act.activation(sq[:], W["y"][:, t % 2, :], ACT.Square).then_inc(S("squared"), 1)
                    act.wait_ge(S("hvar_ready"), t + 1)
                    act.activation(W["var"][:, 0, :], W["var"][:, 0, :], ACT.Sqrt).then_inc(S("hroot_ready"), 1)
                    act.wait_ge(S("turned"), t + 1)
                    act.activation(W["T"][:], PS[:, 6:8, :].rearrange("p b (k n) -> p (b k) n", n=P), ACT.Copy).then_inc(S("T_ready"), 1)

                def second(t):
                    act.wait_ge(S("var_ready"), t + 1)
                    act.activation(W["mv"][:, t % 2, 2:3], W["mv"][:, t % 2, 2:3], ACT.Sqrt).then_inc(S("root_ready"), 1)

                for cond in range(2):
                    act.wait_ge(S("gb_made"), cond + 1)
                    act.activation(W["gb"][:, cond, :], PS[:, 4 + 2 * cond:6 + 2 * cond, :].rearrange("p b n -> p (b n)"), ACT.Copy).then_inc(S("gbs_ready"), 1)
                gates(0)
                first(0)
                for t in range(1, NT):
                    gates(t)
                    first(t)
                    second(t - 1)
                second(NT - 1)

            @block.tensor
            def _(pe):
                def heads(t):
                    c = tile_cols(t)
                    if t:
                        pe.wait_ge(S("mix_ready"), t)
                    pe.matmul(PS[:, 1, :], chan[:, 13, c:c + P], W["gup"][:], start=True, stop=True)
                    for k in range(4):
                        pe.transpose(PS[:, 2, k * P:(k + 1) * P], chan[:, 8 + k, c:c + P], ident[:])
                    pe.wait_ge(S("rk_ready"), t + 1)
                    for k in range(4):
                        mm = pe.matmul(PS[:, 3, 2 * k:2 * k + 2], W["rk"][:, k, :], W["hsel"][:], start=True, stop=True)
                    mm.then_inc(S("heads_ready"), 1)

                def turn(t):
                    pe.wait_ge(S("mix_ready"), t + 1)
                    for k in range(KC):
                        mm = pe.transpose(PS[:, 6 + k // 4, (k % 4) * P:(k % 4 + 1) * P], W["y"][:, t % 2, k * P:(k + 1) * P], ident[:])
                    mm.then_inc(S("turned"), 1)

                def project(t):
                    pe.wait_ge(S("T_ready"), t + 1)
                    if t:
                        pe.wait_ge(S("out_read"), t)
                    for i in range(2):
                        for k in range(KC):
                            mm = pe.matmul(PS[:, 4 + i, :], W["T"][:, k, :], W["wo"][:, k, i * 512:(i + 1) * 512], start=(k == 0), stop=(k == KC - 1))
                    mm.then_inc(S("out_ready"), 1)

                for cond in range(2):
                    for i in range(2):
                        mm = pe.matmul(PS[:, 4 + 2 * cond + i, :], selc[:, cond, :], grow[:, 0, i * 512:(i + 1) * 512], start=True, stop=True)
                    mm.then_inc(S("gb_made"), 1)
                pe.wait_ge(S("w_loaded"), 16 * len(loads))
                heads(0)
                pe.wait_ge(S("gbs_ready"), 2)
                for t in range(NT):
                    turn(t)
                    if t + 1 < NT:
                        heads(t + 1)
                    project(t)

            @block.vector
            def _(dve):
                ch = Chain(dve, S("dve_step"))
                var, mean = W["var"], W["mean"]

                def first(t):
                    y = W["y"][:, t % 2, :]
                    yt = Y[:, t, :].rearrange("p (h n) -> p h n", n=HD)
                    y3, s3 = y.rearrange("p (h n) -> p h n", n=HD), sq[:].rearrange("p (h n) -> p h n", n=HD)
                    ch(dve.tensor_reduce(mean[:], yt, AX, ALU.add))
                    ch(dve.tensor_scalar(mean[:], mean[:], 1.0 / HD, None, ALU.mult))
                    if t >= 2:
                        dve.wait_ge(S("stored"), 16 * (t - 1))
                    dve.tensor_tensor(y3, yt, bc(mean[:], 2, HD), ALU.subtract).then_inc(S("centred"), 1)
                    dve.wait_ge(S("squared"), t + 1)
                    ch(dve.tensor_reduce(var[:, 0, :], s3, AX, ALU.add))
                    dve.tensor_scalar(var[:, 0, :], var[:, 0, :], 1.0 / HD, EPS, ALU.mult, ALU.add).then_inc(S("hvar_ready"), 1)
                    dve.wait_ge(S("hroot_ready"), t + 1)
                    ch(dve.reciprocal(var[:, 1, :], var[:, 0, :]))
                    ch(dve.tensor_tensor(y3, y3, bc(var[:, 1, :], 2, HD), ALU.mult))
                    ch(dve.tensor_tensor(y, y, W["gn"][:, 0, :], ALU.mult))
                    ch(dve.tensor_tensor(y, y, W["gn"][:, 1, :], ALU.add))
                    dve.wait_ge(S("sil_ready"), t + 1)
                    dve.wait_ge(S("og_ready"), t + 1)
                    ch.inc(dve.tensor_tensor(y[:, 0:256], y[:, 0:256], W["sil"][:], ALU.mult))
                    ch.inc(dve.tensor_tensor(y[:, 768:1024], y[:, 768:1024], W["og"][:], ALU.mult))
                    dve.wait_ge(S("heads_ready"), t + 1)
                    ch(dve.tensor_copy(W["bon"][:], PS[:, 3, 0:8]))
                    ch(dve.tensor_tensor(s3[:, 0:8, :], PS[:, 2, :].rearrange("p (h n) -> p h n", n=HD), bc(W["bon"][:], 2, HD), ALU.mult))
                    ch(dve.tensor_tensor(y[:, 256:768], y[:, 256:768], sq[:, 0:512], ALU.add))
                    dve.tensor_tensor(y[:, 256:768], y[:, 256:768], PS[:, 1, :], ALU.mult).then_inc(S("mix_ready"), 1)

                def second(t):
                    y, mv = W["y"][:, t % 2, :], W["mv"][:, t % 2]
                    dve.wait_ge(S("out_ready"), t + 1)
                    if t == 0:
                        dve.wait_ge(S("gbs_ready"), 2)
                    dve.tensor_tensor(y, PS[:, 4:6, :].rearrange("p b n -> p (b n)"), W["gb"][:, min(t, 1), :], ALU.mult).then_inc(S("out_read"), 1)
                    dve.wait_ge(S("out_read"), t + 1)
                    dve.wait_ge(S("x_loaded"), 16 * t + 16)
                    ch(dve.scalar_tensor_tensor(y, x[:], ALPHA, y, ALU.mult, ALU.add))
                    norm_rows(dve, S, ch, y, W["st"], mv, t)

                dve.wait_ge(S("w_loaded"), 16 * len(loads))
                first(0)
                for t in range(1, NT):
                    first(t)
                    second(t - 1)
                second(NT - 1)
        ph.meet()


def norm_rows(dve, S, ch, y, st, mv, t):
    ch.inc(dve.bn_stats(st[:, 0, :], y[:, 0:512]))
    ch.inc(dve.bn_stats(st[:, 1, :], y[:, 512:1024]))
    ch.sync()
    ch(dve.bn_aggr(mv[:, 0:2], st[:, :, :]))
    dve.tensor_scalar(mv[:, 2:3], mv[:, 1:2], EPS, None, ALU.add).then_inc(S("var_ready"), 1)
    dve.wait_ge(S("root_ready"), t + 1)
    ch(dve.reciprocal(mv[:, 3:4], mv[:, 2:3]))
    dve.tensor_scalar(y, y, mv[:, 0:1], mv[:, 3:4], ALU.subtract, ALU.mult).then_inc(S("norm_ready"), 1)


def route(nc, D, layer, h2T, PS, ident):
    with ExitStack() as ctx:
        def sb(name, shape, dt=F32):
            return tile(nc, ctx, name, shape, dt)

        slots = sb("slots", [P, 3, TOK])
        iota = sb("iota", [P, P])
        with ExitStack() as c2:
            scores = c2.enter_context(nc.sbuf_tensor("scores", [P, NT, 16, P], F32))
            queries(nc, D, layer, h2T, scores, iota, PS)
            with Phase(nc, "cur_ready e_ready exp_ready slots_ready turned done dve_step") as ph:
                bufs = {n: ph.sb("k_" + n, s, dt) for n, s, dt in (
                    ("s", [P, 16, P], F32), ("s2", [P, 16, P], F32), ("v", [P, 16, TOPK], F32), ("i", [P, 16, TOPK], U32), ("if", [P, 16, TOPK], F32),
                    ("cand", [P, 8, 256], F32), ("cand2", [P, 8, 256], F32), ("tv", [P, 8, TOPK], F32), ("ti", [P, 8, TOPK], U32), ("hi", [P, 8, TOPK], U32),
                    ("lo", [P, 8, TOPK], U32), ("hl", [P, 2, 8, TOPK], F32), ("one", [P, P, TOPK], F32), ("sl", [P, 3, P], F32), ("sum", [P, 8], F32))}
                with nc.Fori(0, NT) as t:
                    top_tile(nc, ph, bufs, scores, slots, iota, PS, ident, t)
        spread(nc, D, slots, iota, PS)


def queries(nc, D, layer, h2T, scores, iota, PS):
    with Phase(nc, "k_loaded wa_loaded wb_loaded acc_ready q_ready s_ready s_read") as ph:
        S = ph.sem
        wt = ph.sb("wt", [P, 2, KC, P])
        keys = ph.sb("keys", [P, 16, P])
        qT = ph.sb("pqT", [P, 2, TOK])
        WL = ["wa_loaded", "wb_loaded"]
        with nc.Block() as block:
            @block.sync
            def _(sp):
                sp.dma_start(keys[:], of_layer(D["keys"], layer)).then_inc(S("k_loaded"), 16)
                sp.dma_start(iota[:], D["c_iota"]).then_inc(S("k_loaded"), 16)
                with sp.Fori(0, 8) as i:
                    for b in range(2):
                        sp.wait_ge(S("acc_ready"), i * 2 + b + 1)
                        sp.dma_start(wt[:, b], of_layer(of_layer(D["wq"], layer), i * 2 + b)).then_inc(S(WL[b]), 16)

            @block.tensor
            def _(pe):
                pe.sem_inc(S("acc_ready"), 2)
                pe.wait_ge(S("k_loaded"), 32)
                with pe.Fori(0, 8) as i:
                    for b in range(2):
                        pe.wait_ge(S(WL[b]), i * 16 + 16)
                        pe.wait_ge(S("q_ready"), i * 4 + 2 * b + 2)
                        for k in range(KC):
                            for z in range(2):
                                mm = pe.matmul(PS[:, 2 * b + z, 0:HT], wt[:, b, k, :], h2T[:, k, z * HT:(z + 1) * HT],
                                               start=(k == 0), stop=(k == KC - 1))
                        mm.then_inc(S("acc_ready"), 1)
                        pe.wait_ge(S("q_ready"), i * 4 + 2 * b + 6)
                        pe.wait_ge(S("s_read"), i * 4 + 2 * b + 2)
                        for t in range(NT):
                            mm = pe.matmul(PS[:, 4 + 2 * b + t // 4, (t % 4) * P:(t % 4 + 1) * P], qT[:, b, t * P:(t + 1) * P],
                                           keys[:, ds(i * 2 + b, 1), :].rearrange("p a n -> p (a n)"), start=True, stop=True)
                        mm.then_inc(S("s_ready"), 1)

            @block.scalar
            def _(act):
                act.sem_inc(S("q_ready"), 4)
                with act.Fori(0, 8) as i:
                    for b in range(2):
                        act.wait_ge(S("acc_ready"), i * 2 + b + 3)
                        act.wait_ge(S("s_ready"), i * 2 + b + 1)
                        for z in range(2):
                            act.activation(qT[:, b, z * HT:(z + 1) * HT], PS[:, 2 * b + z, 0:HT], ACT.Copy).then_inc(S("q_ready"), 1)

            @block.vector
            def _(dve):
                dve.sem_inc(S("s_read"), 4)
                dve.sem_inc(S("s_ready"), 2)
                with dve.Fori(0, 8) as i:
                    for b in range(2):
                        dve.wait_ge(S("s_ready"), i * 2 + b + 3)
                        dst = scores[:, :, ds(i * 2 + b, 1), :].rearrange("p t a n -> p t (a n)")
                        dve.tensor_copy(dst[:, 0:4, :], PS[:, 4 + 2 * b, :].rearrange("p (t n) -> p t n", t=4)).then_inc(S("s_read"), 1)
                        dve.tensor_copy(dst[:, 4, :], PS[:, 5 + 2 * b, 0:P]).then_inc(S("s_read"), 1)
                dve.wait_ge(S("s_read"), 4 + 32)
        ph.meet()


def top_tile(nc, ph, K, scores, slots, iota, PS, ident, t):
    S = ph.sem
    NEG = -3.0e38
    with nc.Block() as block:
        @block.scalar
        def _(act):
            act.activation(K["s"][:], scores[:, ds(t, 1), :, :].rearrange("p a g n -> p (a g) n"), ACT.Copy).then_inc(S("cur_ready"), 1)
            act.wait_ge(S("e_ready"), 1)
            act.activation(K["tv"][:], K["tv"][:], ACT.Exp).then_inc(S("exp_ready"), 1)
            act.wait_ge(S("turned"), 1)
            act.activation(slots[:, :, ds(t * P, P)], PS[:, 0, 0:3 * P].rearrange("p (a n) -> p a n", a=3), ACT.Copy).then_inc(S("done"), 1)
            act.wait_ge(S("done"), 1)

        @block.vector
        def _(dve):
            ch = Chain(dve, S("dve_step"))

            def top16(src, work, val, idx, n):
                for g in range(n):
                    ch.inc(dve.max(val[:, g, 0:8], src[:, g, :]))
                ch.sync()
                for g in range(n):
                    ch.inc(dve.max_index(idx[:, g, 0:8], val[:, g, 0:8], src[:, g, :]))
                for g in range(n):
                    ch.inc(dve.match_replace(work[:, g, :], val[:, g, 0:8], src[:, g, :], NEG))
                ch.sync()
                for g in range(n):
                    ch.inc(dve.max(val[:, g, 8:16], work[:, g, :]))
                ch.sync()
                for g in range(n):
                    ch.inc(dve.max_index(idx[:, g, 8:16], val[:, g, 8:16], work[:, g, :]))
                ch.sync()

            dve.wait_ge(S("cur_ready"), 1)
            top16(K["s"], K["s2"], K["v"], K["i"], 16)
            ch.inc(dve.tensor_copy(K["if"][:], K["i"][:]))
            v2 = K["v"][:].rearrange("p (h x) k -> p h x k", x=2)
            ch(dve.tensor_tensor(K["cand"][:].rearrange("p h (i j) -> p h i j", i=TOPK),
                                 bc(v2[:, :, 0, :], 3, TOPK), bc(v2[:, :, 1, :], 2, TOPK), ALU.add))
            top16(K["cand"], K["cand2"], K["tv"], K["ti"], 8)
            ch.inc(dve.tensor_copy(K["sum"][:], K["tv"][:, :, 0]))
            ch.inc(dve.tensor_scalar(K["hi"][:], K["ti"][:], 4, None, ALU.logical_shift_right))
            ch(dve.tensor_scalar(K["lo"][:], K["ti"][:], 15, None, ALU.bitwise_and))
            dve.tensor_tensor(K["tv"][:], K["tv"][:], bc(K["sum"][:], 2, TOPK), ALU.subtract).then_inc(S("e_ready"), 1)
            ch.inc(dve.tensor_copy(K["hl"][:, 0], K["hi"][:]))
            ch(dve.tensor_copy(K["hl"][:, 1], K["lo"][:]))
            i2 = K["if"][:].rearrange("p (h x) k -> p h x k", x=2)
            one4 = K["one"][:].rearrange("p (h k) r -> p h k r", h=8)
            for x in range(2):
                ch(dve.tensor_tensor(K["one"][:], bc(K["hl"][:, x].rearrange("p h k -> p (h k)"), 2, TOPK), bc(iota[:, 0:TOPK], 1, P), ALU.is_equal))
                ch(dve.tensor_tensor(one4, one4, bc(i2[:, :, x, :], 2, TOPK), ALU.mult))
                ch(dve.tensor_reduce(K["sl"][:, x, :], K["one"][:], AX, ALU.add))
            dve.wait_ge(S("exp_ready"), 1)
            ch(dve.tensor_reduce(K["sum"][:], K["tv"][:], AX, ALU.add))
            ch(dve.reciprocal(K["sum"][:], K["sum"][:]))
            dve.tensor_tensor(K["sl"][:, 2, :].rearrange("p (h k) -> p h k", h=8), K["tv"][:], bc(K["sum"][:], 2, TOPK), ALU.mult).then_inc(S("slots_ready"), 1)

        @block.tensor
        def _(pe):
            pe.wait_ge(S("slots_ready"), 1)
            for i in range(3):
                mm = pe.transpose(PS[:, 0, i * P:(i + 1) * P], K["sl"][:, i, :], ident[:])
            mm.then_inc(S("turned"), 1)
    ph.meet()


def spread(nc, D, slots, iota, PS):
    OCT = 8
    SLOTS = 4
    SETS = NB // OCT
    QB = NB // 4
    with Phase(nc, "cur_ready eq_ready a_ready b_ready w_ready w_read s0_stored s1_stored") as ph:
        S = ph.sem
        cur = ph.sb("cur", [P, 2, 3, NB])
        A, Bh = ph.sb("A", [P, SLOTS, OCT, P]), ph.sb("Bh", [P, SLOTS, OCT, P])
        Wt = ph.sb("Wt", [P, 2, P, NB])
        with nc.Block() as block:
            @block.scalar
            def _(act):
                for b in range(2):
                    act.sem_inc(S(f"s{b}_stored"), 16)
                with act.Fori(0, NBATCH // 2) as i:
                    for b in range(2):
                        act.activation(cur[:, b], slots[:, :, ds(i * 2 * NB + b * NB, NB)], ACT.Copy).then_inc(S("cur_ready"), 1)
                        act.wait_ge(S(f"s{b}_stored"), i * 16 + 16)
                        for q in range(QB):
                            act.wait_ge(S("w_ready"), i * 2 * QB + b * QB + q + 2 * SLOTS + 1)
                            act.activation(Wt[:, b, :, 4 * q:4 * q + 4], PS[:, q % 8, :].rearrange("p (t e) -> p e t", t=4), ACT.Copy).then_inc(S("w_read"), 1)

            @block.vector
            def _(dve):
                dve.sem_inc(S("w_ready"), 2 * SLOTS)
                with dve.Fori(0, NBATCH // 2) as i:
                    for b in range(2):
                        dve.wait_ge(S("cur_ready"), i * 2 + b + 1)
                        for n in range(SETS):
                            s = (b * SETS + n) % SLOTS
                            rows = slice(n * OCT, (n + 1) * OCT)
                            dve.wait_ge(S("w_ready"), i * 2 * QB + b * QB + 2 * n + 2)
                            dve.tensor_tensor(A[:, s], bc(cur[:, b, 0, rows], 2, P), bc(iota[:], 1, OCT), ALU.is_equal).then_inc(S("eq_ready"), 1)
                            dve.tensor_tensor(Bh[:, s], bc(cur[:, b, 1, rows], 2, P), bc(iota[:], 1, OCT), ALU.is_equal).then_inc(S("b_ready"), 1)

            @block.gpsimd
            def _(pool):
                with pool.Fori(0, NBATCH // 2) as i:
                    for b in range(2):
                        for n in range(SETS):
                            s = (b * SETS + n) % SLOTS
                            pool.wait_ge(S("eq_ready"), i * 2 * SETS + b * SETS + n + 1)
                            pool.tensor_tensor(A[:, s], A[:, s], bc(cur[:, b, 2, n * OCT:(n + 1) * OCT], 2, P), ALU.mult).then_inc(S("a_ready"), 1)

            @block.tensor
            def _(pe):
                pe.sem_inc(S("w_read"), 8)
                with pe.Fori(0, NBATCH // 2) as i:
                    for b in range(2):
                        for n in range(SETS):
                            s = (b * SETS + n) % SLOTS
                            pe.wait_ge(S("a_ready"), i * 2 * SETS + b * SETS + n + 1)
                            pe.wait_ge(S("b_ready"), i * 2 * SETS + b * SETS + n + 1)
                            for q in range(OCT // 4):
                                bank = (n * OCT // 4 + q) % 8
                                pe.wait_ge(S("w_read"), i * 2 * QB + b * QB + n * OCT // 4 + q + 1)
                                for t in range(4):
                                    mm = pe.matmul(PS[:, bank, t * P:(t + 1) * P], A[:, s, q * 4 + t, :], Bh[:, s, q * 4 + t, :], start=True, stop=True)
                                mm.then_inc(S("w_ready"), 1)

            @block.sync
            def _(sp):
                with sp.Fori(0, NBATCH // 2) as i:
                    for b in range(2):
                        sp.wait_ge(S("w_read"), i * 2 * QB + (b + 1) * QB + 8)
                        sp.dma_start(of_layer(D["wts"], i * 2 + b), Wt[:, b]).then_inc(S(f"s{b}_stored"), 16)
                for b in range(2):
                    sp.wait_ge(S(f"s{b}_stored"), 16 * (NBATCH // 2) + 16)
        ph.meet()


def split_rows(nc, src, hi, lo, PS):
    with Phase(nc, "hi_ready lo_ready") as ph:
        with nc.Block() as block:
            @block.scalar
            def _(act):
                for k in range(KC):
                    act.activation(hi[:, k, :], src[:, k, :], ACT.Copy).then_inc(ph.sem("hi_ready"), 1)

            @block.vector
            def _(dve):
                for k in range(KC):
                    dve.wait_ge(ph.sem("hi_ready"), k + 1)
                    dve.tensor_tensor(lo[:, k, :], src[:, k, :], hi[:, k, :].bitcast(F32), ALU.subtract).then_inc(ph.sem("lo_ready"), 1)
                dve.wait_ge(ph.sem("lo_ready"), KC)
        ph.meet()


def experts(nc, D, layer, hh, hl, ffn, PS):
    SEMS = ("u0_loaded u1_loaded v0_loaded v1_loaded g_loaded uhi_ready u_split vhi_ready v_split h_ready gelu_ready "
            "wf_ready whi_ready w_split o_ready o_read")
    with Phase(nc, SEMS) as ph:
        S = ph.sem
        u = ph.sb("u", [P, 2, KC * P])
        uh, ul = ph.sb("uh", [P, 2, KC, P], F32R), ph.sb("ul", [P, 2, KC, P], F32R)
        v = ph.sb("v", [P, 2, D_MODEL])
        vh, vl = ph.sb("vh", [P, GRP, D_MODEL], F32R), ph.sb("vl", [P, GRP, D_MODEL], F32R)
        g = ph.sb("g", [P, NBATCH, GRP, NB])
        ge, wf = ph.sb("ge", [P, 2, TOK]), ph.sb("wf", [P, 2, TOK])
        wh, wl = ph.sb("wh", [P, GRP, TOK], F32R), ph.sb("wl", [P, GRP, TOK], F32R)
        ut, pv, wts = of_layer(D["ut"], layer), of_layer(D["pv"], layer), D["wts"]
        OT = 2 * NT

        with nc.Block() as block:
            @block.sync
            def _(sp):
                with sp.Fori(0, NGRP) as i:
                    for e in range(GRP):
                        sp.wait_ge(S("u_split"), i * GRP + e + 1)
                        sp.dma_start(u[:, e % 2, :], of_layer(ut, i)[:, e, :]).then_inc(S(f"u{e % 2}_loaded"), 16)
                        sp.wait_ge(S("v_split"), i * GRP + e + 1)
                        sp.dma_start(v[:, e % 2, :], pv[:, ds(i * GRP + e, 1), :].rearrange("p a n -> p (a n)")).then_inc(S(f"v{e % 2}_loaded"), 16)
                        if e == 0:
                            sp.wait_ge(S("wf_ready"), i * GRP + 2)
                            sp.dma_start(g[:], wts[:, :, ds(i * GRP, GRP), :].rearrange("n p e t -> p n e t")).then_inc(S("g_loaded"), 16)

            @block.tensor
            def _(pe):
                def hidden(i, e):
                    pe.wait_ge(S("u_split"), i * GRP + e + 3)
                    pe.wait_ge(S("gelu_ready"), i * GRP + e + 1)
                    b, n = e % 2, 0
                    for k in range(KC):
                        for wt, x in ((uh, hh), (uh, hl), (ul, hh)):
                            for z in range(2):
                                mm = pe.matmul(PS[:, 2 * b + z, 0:HT], wt[:, b, k, :], x[:, k, z * HT:(z + 1) * HT],
                                               start=(n == 0), stop=(n == 3 * KC - 1))
                            n += 1
                    mm.then_inc(S("h_ready"), 1)

                def outputs(i):
                    pe.wait_ge(S("w_split"), i * GRP + GRP + 2)
                    pe.wait_ge(S("v_split"), i * GRP + GRP + 2)
                    for o in range(OT):
                        pe.wait_ge(S("o_read"), i * OT + 1 + (o - 3 if o >= 4 else 0))
                        n, cols = 0, slice((o % 2) * 512, (o % 2 + 1) * 512)
                        for e in range(GRP):
                            toks = slice((o // 2) * P, (o // 2 + 1) * P)
                            for wt, x in ((wh, vh), (wh, vl), (wl, vh)):
                                mm = pe.matmul(PS[:, 4 + o % 4, :], wt[:, e, toks], x[:, e, cols], start=(n == 0), stop=(n == 3 * GRP - 1))
                                n += 1
                        mm.then_inc(S("o_ready"), 1)

                hidden(0, 0)
                with pe.Fori(0, NGRP - 1) as i:
                    for e in range(1, GRP):
                        hidden(i, e)
                    hidden(i + 1, 0)
                    outputs(i)
                for e in range(1, GRP):
                    hidden(NGRP - 1, e)
                outputs(NGRP - 1)

            @block.scalar
            def _(act):
                def u_hi(i, e):
                    act.wait_ge(S(f"u{e % 2}_loaded"), i * 32 + 16 * (e // 2) + 16)
                    act.wait_ge(S("h_ready"), i * GRP + e + 1)
                    act.activation(uh[:, e % 2].rearrange("p k n -> p (k n)"), u[:, e % 2, :], ACT.Copy).then_inc(S("uhi_ready"), 1)

                def step(i, e, last=False):
                    if not last:
                        u_hi(i + (e + 1) // GRP, (e + 1) % GRP)
                    act.wait_ge(S("h_ready"), i * GRP + e + 3)
                    act.wait_ge(S("wf_ready"), i * GRP + e + 1)
                    b = e % 2
                    act.activation(ge[:, b, :].rearrange("p (z n) -> p z n", z=2), PS[:, 2 * b:2 * b + 2, 0:HT], ACT.Gelu).then_inc(S("gelu_ready"), 1)
                    act.wait_ge(S(f"v{b}_loaded"), i * 32 + 16 * (e // 2) + 16)
                    act.wait_ge(S("o_ready"), i * OT + 1)
                    act.activation(vh[:, e, :], v[:, b, :], ACT.Copy).then_inc(S("vhi_ready"), 1)
                    act.wait_ge(S("wf_ready"), i * GRP + e + 3)
                    act.activation(wh[:, e, :], wf[:, b, :], ACT.Copy).then_inc(S("whi_ready"), 1)

                act.sem_inc(S("gelu_ready"), 2)
                u_hi(0, 0)
                step(0, 0)
                with act.Fori(0, NGRP - 1) as i:
                    for e in range(1, GRP):
                        step(i, e)
                    step(i + 1, 0)
                for e in range(1, GRP):
                    step(NGRP - 1, e, last=(e == GRP - 1))

            @block.gpsimd
            def _(pool):
                pool.memset(ffn[:], 0.0).then_inc(S("o_read"), 1)
                pool.sem_inc(S("h_ready"), 2)
                pool.sem_inc(S("o_ready"), 1)

            @block.vector
            def _(dve):
                def u_lo(i, e):
                    dve.wait_ge(S("uhi_ready"), i * GRP + e + 1)
                    b = e % 2
                    dve.tensor_tensor(ul[:, b].rearrange("p k n -> p (k n)"), u[:, b, :], uh[:, b].rearrange("p k n -> p (k n)").bitcast(F32),
                                      ALU.subtract).then_inc(S("u_split"), 1)

                def add_outputs(i):
                    dve.wait_ge(S("o_read"), i * OT + 1)
                    for o in range(OT):
                        dve.wait_ge(S("o_ready"), i * OT + o + 2)
                        acc = ffn[:, o // 2, (o % 2) * 512:(o % 2 + 1) * 512]
                        dve.tensor_tensor(acc, acc, PS[:, 4 + o % 4, :], ALU.add).then_inc(S("o_read"), 1)

                def step(i, e, last=False):
                    b = e % 2
                    if not last:
                        u_lo(i + (e + 1) // GRP, (e + 1) % GRP)
                    if e == 0 and not isinstance(i, int):
                        add_outputs(i - 1)
                    dve.wait_ge(S("gelu_ready"), i * GRP + e + 3)
                    dve.wait_ge(S("g_loaded"), i * 16 + 16)
                    dve.wait_ge(S("w_split"), i * GRP + e + 1)
                    dve.tensor_tensor(wf[:, b, :].rearrange("p (n t) -> p n t", t=NB), ge[:, b, :].rearrange("p (n t) -> p n t", t=NB),
                                      g[:, :, e, :], ALU.mult).then_inc(S("wf_ready"), 1)
                    dve.wait_ge(S("vhi_ready"), i * GRP + e + 1)
                    dve.tensor_tensor(vl[:, e, :], v[:, b, :], vh[:, e, :].bitcast(F32), ALU.subtract).then_inc(S("v_split"), 1)
                    dve.wait_ge(S("whi_ready"), i * GRP + e + 1)
                    dve.tensor_tensor(wl[:, e, :], wf[:, b, :], wh[:, e, :].bitcast(F32), ALU.subtract).then_inc(S("w_split"), 1)

                for name in ("u_split", "v_split", "wf_ready", "w_split"):
                    dve.sem_inc(S(name), 2)
                u_lo(0, 0)
                step(0, 0)
                with dve.Fori(0, NGRP - 1) as i:
                    for e in range(1, GRP):
                        step(i, e)
                    step(i + 1, 0)
                for e in range(1, GRP):
                    step(NGRP - 1, e, last=(e == GRP - 1))
                add_outputs(NGRP - 1)
                dve.wait_ge(S("o_read"), NGRP * OT + 1)
        ph.meet()


def finish(nc, D, layer, ffn, X, grow, selc, PS):
    with Phase(nc, "x_loaded w_loaded gb_made gbs_ready scaled var_ready root_ready norm_ready gain_done row_ready stored dve_step") as ph:
        S = ph.sem
        W = {n: ph.sb("f_" + n, s) for n, s in {"x": [P, NT, D_MODEL], "ln": [P, 2, D_MODEL], "st": [P, 2, 6], "mv": [P, NT, 4],
                                                 "gb": [P, 2, D_MODEL]}.items()}
        with nc.Block() as block:
            @block.sync
            def _(sp):
                for t in range(NT):
                    sp.dma_start(W["x"][:, t, :], X[t]).then_inc(S("x_loaded"), 16)
                sp.dma_start(W["ln"][:], row_bc(D["ln2"], layer)).then_inc(S("w_loaded"), 16)
                for t in range(NT):
                    sp.wait_ge(S("row_ready"), t + 1)
                    sp.dma_start(X[t], ffn[:, t, :]).then_inc(S("stored"), 16)
                sp.wait_ge(S("stored"), 16 * NT)

            @block.tensor
            def _(pe):
                for cond in range(2):
                    for i in range(2):
                        mm = pe.matmul(PS[:, 2 * cond + i, :], selc[:, cond, :], grow[:, 1, i * 512:(i + 1) * 512], start=True, stop=True)
                    mm.then_inc(S("gb_made"), 1)

            @block.scalar
            def _(act):
                for cond in range(2):
                    act.wait_ge(S("gb_made"), cond + 1)
                    act.activation(W["gb"][:, cond, :], PS[:, 2 * cond:2 * cond + 2, :].rearrange("p b n -> p (b n)"), ACT.Copy).then_inc(S("gbs_ready"), 1)
                for t in range(NT):
                    act.wait_ge(S("var_ready"), t + 1)
                    act.activation(W["mv"][:, t, 2:3], W["mv"][:, t, 2:3], ACT.Sqrt).then_inc(S("root_ready"), 1)

            @block.gpsimd
            def _(pool):
                for t in range(NT):
                    pool.wait_ge(S("gbs_ready"), min(t, 1) + 1)
                    pool.tensor_tensor(ffn[:, t, :], ffn[:, t, :], W["gb"][:, min(t, 1), :], ALU.mult).then_inc(S("scaled"), 1)
                pool.wait_ge(S("w_loaded"), 16)
                for t in range(NT):
                    pool.wait_ge(S("norm_ready"), t + 1)
                    pool.tensor_tensor(ffn[:, t, :], ffn[:, t, :], W["ln"][:, 0, :], ALU.mult).then_inc(S("gain_done"), 1)
                    pool.wait_ge(S("gain_done"), t + 1)
                    pool.tensor_tensor(ffn[:, t, :], ffn[:, t, :], W["ln"][:, 1, :], ALU.add).then_inc(S("row_ready"), 1)

            @block.vector
            def _(dve):
                ch = Chain(dve, S("dve_step"))
                dve.wait_ge(S("x_loaded"), 16 * NT)
                for t in range(NT):
                    dve.wait_ge(S("scaled"), t + 1)
                    ch(dve.scalar_tensor_tensor(ffn[:, t, :], W["x"][:, t, :], ALPHA, ffn[:, t, :], ALU.mult, ALU.add))
                    norm_rows(dve, S, ch, ffn[:, t, :], W["st"], W["mv"][:, t], t)
        ph.meet()


def constants(np):
    i = np.arange(P)
    s, t = i[:, None], i[None, :]
    C = {"c_ident": np.eye(P), "c_ones": np.ones((P, P)), "c_iota": np.tile(i, (P, 1))}
    C["c_selc"] = np.stack([np.stack([np.full(P, float(r == c)) for c in range(2)]) for r in range(2)])
    C["c_blk"] = (s // HD == t // HD)
    C["c_hsel"] = (s // HD == np.arange(2)[None, :])
    r = np.exp(-0.5)
    mid = [(i < HD).astype(float), (i >= HD).astype(float)]
    inc = [(s <= t).astype(float), (s >= t).astype(float)]
    exc = [(s < t).astype(float), (s > t).astype(float)]
    C["c_tri"] = np.stack([-r * np.concatenate([inc[d] - mid[d][:, None], exc[d] - mid[d][:, None], mid[d][:, None]], 1) for d in range(2)], 1)
    C["c_strict"] = np.stack(exc, 1)
    C["c_incl"] = np.stack(inc, 1)
    C["c_strictT"] = np.stack([e.T for e in exc], 1)
    same = [(s // n == t // n).astype(float) for n in (16, 32, 64, 128)]
    C["c_lvl"] = np.stack([same[0]] + [same[k] - same[k - 1] for k in (1, 2, 3)], 1)
    C["c_cum"] = np.stack(inc, 1)
    C["c_negm"] = np.stack([(1 - e.T) * -1e30 for e in inc], 1)
    C["c_dist"] = np.stack([np.maximum(s - t, 0), np.maximum(t - s, 0)], 1)
    C["c_pos"] = np.stack([np.stack([i + 1, P - 1 - i, np.full(P, P)], 1), np.stack([P - i, i, np.full(P, P)], 1)], 1)
    nf = HD // 4
    inv = np.float32(10000.0) ** (-np.arange(nf, dtype=np.float32) / np.float32(nf))
    pos = np.arange(LAT, dtype=np.float32)
    ang = np.concatenate([(pos // 64)[:, None] * inv, (pos % 64)[:, None] * inv], -1).astype(np.float32)
    C["c_cos"] = np.cos(ang).reshape(NT - 1, P, 32).transpose(1, 0, 2)
    C["c_sin"] = np.sin(ang).reshape(NT - 1, P, 32).transpose(1, 0, 2)
    return {n: np.ascontiguousarray(a, dtype=np.float32) for n, a in C.items()}


def layouts(np, I):
    L = DEPTH

    def cols(a, n):
        return a.reshape(L, n, P).transpose(0, 2, 1)

    A = {}
    A["x"] = np.concatenate([I["x_prompt"].reshape(1, P, D_MODEL), I["x_sample"].reshape(NT - 1, P, D_MODEL)])
    A["cond"] = np.stack([I["c_ctx"].reshape(KC, P), I["c"].reshape(KC, P)], -1).transpose(1, 0, 2)
    A["b_mod"] = np.stack([I["b_mod"], I["b_mod"]], 1)
    A["w_mod"] = I["w_mod"]
    w = I["w_in"].reshape(L, KC, P, -1)
    ch = np.concatenate([w[..., 1024:2816], w[..., 2816:3328]], -1).reshape(L, KC, P, CT, P)
    A["w_ch"] = ch.transpose(0, 3, 2, 1, 4)
    A["w_tm"] = np.concatenate([w[..., 0:1024], w[..., 3328:3856]], -1).transpose(0, 2, 1, 3)
    A["prm"] = np.concatenate([
        cols(I["rwkv_mu"], 14), I["rwkv_a0"].reshape(L, 2, 4, P).transpose(0, 3, 1, 2).reshape(L, P, 8),
        cols(I["rwkv_kk"], 4), cols(I["rwkv_ka"], 4), cols(I["rwkv_rk"], 4),
        I["mlstm_conv"].reshape(L, 3, 4, P).transpose(0, 3, 2, 1).reshape(L, P, 12)], -1)
    A["gbias"] = np.repeat(I["mlstm_gate_bias"].reshape(L, 1, 16), P, 1)
    A["lora"] = np.concatenate([I["rwkv_w_up"], I["rwkv_a_up"]], 2).transpose(0, 2, 1, 3)
    A["w0"] = I["rwkv_w0"].reshape(L, 1, 2, 512)
    A["s_rwkv"] = I["state_rwkv"][0].reshape(L, 2, 4, 2, HD, HD).transpose(0, 3, 5, 1, 2, 4).reshape(L, P, 2, 4, HD)
    ret, mc, mn = I["state_ret"][0], I["state_mlstm_c"][0], I["state_mlstm_n"][0]
    c65 = np.concatenate([np.concatenate([ret, np.zeros_like(ret[..., :1])], -1), np.concatenate([mc, mn[..., None]], -1)], 2)
    A["s_la"] = c65.reshape(L, 2, 4, 2, HD, HD + 1).transpose(0, 3, 4, 1, 2, 5).reshape(L, P, 2, 4, HD + 1)
    A["s_m"] = I["state_mlstm_m"][0].reshape(L, 8)
    A["ret_decay"] = I["ret_decay"].reshape(L, 8)
    A["w_out"] = I["w_out"]
    A["g_up"] = I["rwkv_g_up"]
    A["gn"] = np.concatenate([I["ret_gn"], I["rwkv_gn"], I["mlstm_gn"]], -1)
    A["ln1"], A["ln2"] = I["ln1"], I["ln2"]
    A["wq"] = I["peer_wq"].reshape(L, KC, P, 16, P).transpose(0, 3, 2, 1, 4)
    A["keys"] = I["peer_keys"].reshape(L, 16, P, P).transpose(0, 3, 1, 2)
    A["ut"] = I["peer_u"].reshape(L, P, NGRP, GRP, KC, P).transpose(0, 2, 5, 3, 4, 1)
    A["pv"] = I["peer_v"].reshape(L, P, P, D_MODEL)
    return {n: np.ascontiguousarray(a) for n, a in A.items()}


OUTS = {"y": (NT, P, D_MODEL), "o_rwkv": (DEPTH, P, 2, 4, HD), "o_la": (DEPTH, P, 2, 4, HD + 1), "o_m": (DEPTH, 8)}
SCRATCH = {"x_work": (NT, P, D_MODEL), "wts": (NBATCH, P, P, NB)}


def kernel(**inputs):
    import numpy as np
    import concourse.bacc as bacc
    from concourse.bass_utils import run_bass_kernel_spmd as run

    I = {n: np.asarray(a) for n, a in inputs.items()}
    arrays = {**layouts(np, I), **constants(np)}
    nc = bacc.Bacc("TRN2", target_bir_lowering=False, num_devices=1)
    D = {n: nc.dram_tensor(n, a.shape, F32, kind="ExternalInput").ap() for n, a in arrays.items()}
    D |= {n: nc.dram_tensor(n, s, F32).ap() for n, s in SCRATCH.items()}
    D |= {n: nc.dram_tensor(n, s, F32, kind="ExternalOutput").ap() for n, s in OUTS.items()}
    build(nc, D)
    out = run(nc, [arrays], core_ids=[0]).results[0]
    y = out["y"]
    rwkv_s = out["o_rwkv"].reshape(DEPTH, 2, HD, 2, 4, HD).transpose(0, 3, 4, 1, 5, 2).reshape(1, DEPTH, 2, 8, HD, HD)
    la = out["o_la"].reshape(DEPTH, 2, HD, 2, 4, HD + 1).transpose(0, 3, 4, 1, 2, 5).reshape(1, DEPTH, 2, 8, HD, HD + 1)
    c = np.ascontiguousarray
    return (c(y[0:1]), c(y[1:].reshape(1, LAT, D_MODEL)), c(la[:, :, :, 0:4, :, 0:HD]), c(rwkv_s),
            c(la[:, :, :, 4:8, :, 0:HD]), c(la[:, :, :, 4:8, :, HD]), c(out["o_m"].reshape(1, DEPTH, 2, 4)))
```

```python
from contextlib import ExitStack

import concourse.bass as bass
from concourse import mybir

P = 128
D_MODEL = 1024
KC = D_MODEL // P
NT = 5
TOK = NT * P
LAT = TOK - P
HT = TOK // 2
DEPTH = 2
HD = 64
CT_RW = 14
CT = CT_RW + 4
COLS = 1 + P + 1 + LAT + 1
IN = COLS - 2
TM = 1552
ML_V, ML_O, GATES = 1024, 1280, 1536
TOPK = 16
NB = 64
NBATCH = TOK // NB
GRP = 4
NGRP = P // GRP
NPRM = 46
EPS = 1e-5
ALPHA = (2 * DEPTH) ** 0.25

F32 = mybir.dt.float32
U32 = mybir.dt.uint32
F32R = mybir.dt.float32r
ALU = mybir.AluOpType
ACT = mybir.ActivationFunctionType
AX = mybir.AxisListType.X
ds = bass.ds


def tile(nc, ctx, name, shape, dt=F32):
    return ctx.enter_context(nc.sbuf_tensor(f"{name}_{nc.next_id()}", shape, dt))


class Chain:

    def __init__(self, eng, sem, before=0):
        self.eng, self.sem, self.before, self.n = eng, sem, before, 0

    def inc(self, ins):
        self.n += 1
        ins.then_inc(self.sem, 1)

    def sync(self):
        self.eng.wait_ge(self.sem, self.before + self.n)

    def __call__(self, ins):
        self.inc(ins)
        self.sync()


class Phase:

    def __init__(self, nc, sems):
        self.nc, self.names, self.ctx = nc, sems.split(), ExitStack()

    def __enter__(self):
        self.s = {n: self.ctx.enter_context(self.nc.semaphore(f"{n}_{self.nc.next_id()}")) for n in self.names}
        return self

    def __exit__(self, *a):
        self.ctx.close()

    def sem(self, n):
        return self.s[n]

    def sb(self, name, shape, dt=F32):
        return tile(self.nc, self.ctx, name, shape, dt)

    def meet(self):
        nums = [h.num for h in self.s.values()]
        self.nc.gpsimd.sem_clear(range(min(nums), max(nums) + 1))
        self.nc.all_engine_barrier()


def bc(ap, axis, n):
    v = ap.unsqueeze(axis)
    shape = list(v.shape)
    shape[axis] = n
    return v.to_broadcast(shape)


def of_layer(ap, layer):
    names = " ".join("abcdefg"[:len(ap.shape) - 1])
    rest = names.split()
    return ap[ds(layer, 1)].rearrange(f"l {names} -> (l {rest[0]}) {' '.join(rest[1:])}")


def tile_cols(t):
    return 1 if isinstance(t, int) and t == 0 else t * P + 2


def load_all(nc, loads):
    with Phase(nc, "loaded") as ph:
        with nc.Block() as block:
            @block.sync
            def _(sp):
                for dst, src in loads:
                    sp.dma_start(dst, src).then_inc(ph.sem("loaded"), 16)
                sp.wait_ge(ph.sem("loaded"), 16 * len(loads))
        ph.meet()


def build(nc, D):
    with ExitStack() as ctx:
        def sb(name, shape, dt=F32):
            return tile(nc, ctx, name, shape, dt)

        PS = ctx.enter_context(nc.psum_tensor("PS", [P, 8, 512], F32))
        ident = sb("ident", [P, P])
        ones = sb("ones", [P, P])
        modT = sb("modT", [P, NT, 32])
        scond = sb("scond", [P, KC, 2])
        grow = sb("grow", [2, 2, D_MODEL])
        selc = sb("selc", [2, 2, P])
        X = D["x_work"]

        load_all(nc, [(ident[:], D["c_ident"]), (ones[:], D["c_ones"]), (selc[:], D["c_selc"]), (X, D["x"])])

        with nc.Fori(0, DEPTH) as layer:
            modulation(nc, D, layer, modT, scond, PS, ident, ones)
            with ExitStack() as mixer:
                def mb(name, shape, dt=F32):
                    return tile(nc, mixer, name, shape, dt)

                B = {"chan": mb("chan", [P, CT, COLS]),
                     "tokm": mb("tokm", [P, NT, TM]),
                     "prm": mb("prm", [P, NPRM])}
                with ExitStack() as part:
                    hh, hl = tile(nc, part, "h_hi", [P, KC, TOK], F32R), tile(nc, part, "h_lo", [P, KC, TOK], F32R)
                    with nc.sbuf_tensor("hT", [P, KC, TOK], F32) as hT:
                        normalise(nc, X, hT, modT, 0, PS, ident)
                        split_rows(nc, hT, hh, hl, PS)
                    project_in(nc, D, layer, hh, hl, B, PS)
                B["kkn"] = mb("kkn", [P, 4, IN])
                B["gates"] = mb("gates", [P, NT, 16])
                prepare(nc, D, layer, B, modT, scond, grow, PS, ident, ones)
                B["Y"] = mb("Y", [P, NT, D_MODEL])
                rwkv(nc, D, layer, B, PS, ident, ones)
                linear(nc, D, layer, B, PS, ident, ones)
                mix_out(nc, D, layer, B, X, grow, selc, PS, ident)
            with ExitStack() as ex:
                hh, hl = tile(nc, ex, "hh", [P, KC, TOK], F32R), tile(nc, ex, "hl", [P, KC, TOK], F32R)
                with nc.sbuf_tensor("h2T", [P, KC, TOK], F32) as h2T:
                    normalise(nc, X, h2T, modT, 16, PS, ident)
                    split_rows(nc, h2T, hh, hl, PS)
                route(nc, D, layer, hh, hl, PS, ident)
                ffn = tile(nc, ex, "ffn", [P, NT, D_MODEL])
                experts(nc, D, layer, hh, hl, ffn, PS)
                finish(nc, D, layer, ffn, X, grow, selc, PS)
        load_all(nc, [(D["y"], X)])


MOD_W = 2 * D_MODEL


def load_mod(sp, S, D, layer, wm, parts):
    for n in range(KC * len(parts)):
        part, kc = parts[n // KC], n % KC
        if n >= 3:
            sp.wait_ge(S("w_used"), n - 2)
        sp.dma_start(wm[:, n % 3, :], of_layer(D["w_mod"], layer)[kc * P:(kc + 1) * P, part * MOD_W:(part + 1) * MOD_W]).then_inc(S(f"w{n % 3}_loaded"), 16)


def mod_rows(pe, S, PS, scond, ones, bmod, wm, n, bank):
    pe.wait_ge(S(f"w{n % 3}_loaded"), 16 * (n // 3 + 1))
    for c in range(4):
        mm = pe.matmul(PS[0:2, bank + c, :], scond[:, n % KC, :], wm[:, n % 3, c * 512:(c + 1) * 512], start=(n % KC == 0), stop=False)
    mm.then_inc(S("w_used"), 1)
    if n % KC == KC - 1:
        for c in range(4):
            o = (n // KC) * MOD_W + c * 512
            mm = pe.matmul(PS[0:2, bank + c, :], ones[0:1, 0:2], bmod[0:1, o:o + 512], start=False, stop=True)
        mm.then_inc(S("rows_ready"), 1)


def modulation(nc, D, layer, modT, scond, PS, ident, ones):
    with Phase(nc, "cond_loaded bias_loaded w0_loaded w1_loaded w2_loaded silu_ready w_used rows_ready rows_kept cols_ready mod_ready") as ph:
        S = ph.sem
        cond = ph.sb("cond", [P, KC, 2])
        bmod = ph.sb("bmod", [1, MOD_W])
        mrow = ph.sb("mrow", [2, MOD_W])
        wm = ph.sb("wm", [P, 3, MOD_W])
        with nc.Block() as block:
            @block.sync
            def _(sp):
                sp.dma_start(cond[:], D["cond"]).then_inc(S("cond_loaded"), 16)
                sp.dma_start(bmod[:], of_layer(D["b_mod"], layer)[0:1, 0:MOD_W]).then_inc(S("bias_loaded"), 16)
                load_mod(sp, S, D, layer, wm, (0,))

            @block.scalar
            def _(act):
                act.wait_ge(S("cond_loaded"), 16)
                act.activation(scond[:], cond[:], ACT.Silu).then_inc(S("silu_ready"), 1)

            @block.tensor
            def _(pe):
                pe.wait_ge(S("silu_ready"), 1)
                pe.wait_ge(S("bias_loaded"), 16)
                for n in range(KC):
                    mod_rows(pe, S, PS, scond, ones, bmod, wm, n, 0)
                pe.wait_ge(S("rows_kept"), 1)
                for j in range(2 * KC):
                    mm = pe.transpose(PS[:, 4, 2 * j:2 * j + 2], mrow[:, j * P:(j + 1) * P], ident[0:2, 0:2])
                mm.then_inc(S("cols_ready"), 1)

            @block.vector
            def _(dve):
                dve.wait_ge(S("rows_ready"), 1)
                dve.tensor_copy(mrow[:], PS[0:2, 0:4, :].rearrange("p b n -> p (b n)")).then_inc(S("rows_kept"), 1)
                keep_columns(dve, S, PS[:, 4, 0:32], modT, 0)
        ph.meet()


def keep_columns(dve, S, cols, modT, first):
    cols = cols.rearrange("p (j c) -> p c j", c=2)
    dve.wait_ge(S("cols_ready"), 1)
    dve.tensor_copy(modT[:, 0, first:first + 16], cols[:, 0, :]).then_inc(S("mod_ready"), 1)
    dve.tensor_copy(modT[:, 1:NT, first:first + 16], bc(cols[:, 1, :], 1, NT - 1)).then_inc(S("mod_ready"), 1)
    dve.wait_ge(S("mod_ready"), 2)
    scale = modT[:, :, first + 8:first + 16]
    dve.tensor_scalar(scale, scale, 1.0, None, ALU.add).then_inc(S("mod_ready"), 1)
    dve.wait_ge(S("mod_ready"), 3)


def normalise(nc, X, hT, modT, first, PS, ident):
    with Phase(nc, "x_loaded stats_ready var_ready root_ready inv_ready norm_ready turned columns_ready") as ph:
        S = ph.sem
        x = ph.sb("nx", [P, NT, D_MODEL])
        xn = ph.sb("nxn", [P, 2, D_MODEL])
        st = ph.sb("nst", [P, NT, 2, 6])
        mv = ph.sb("nmv", [P, NT, 2])
        rs = ph.sb("nrs", [P, 2, NT])
        with nc.Block() as block:
            @block.sync
            def _(sp):
                for t in range(NT):
                    sp.dma_start(x[:, t, :], X[t]).then_inc(S("x_loaded"), 16)

            @block.vector
            def _(dve):
                dve.wait_ge(S("x_loaded"), 16 * NT)
                for t in range(NT):
                    for z in range(2):
                        dve.bn_stats(st[:, t, z, :], x[:, t, z * 512:(z + 1) * 512]).then_inc(S("stats_ready"), 1)
                for t in range(NT):
                    dve.wait_ge(S("stats_ready"), 2 * t + 2)
                    dve.bn_aggr(mv[:, t, :], st[:, t, :, :]).then_inc(S("stats_ready"), 1)
                dve.wait_ge(S("stats_ready"), 3 * NT)
                dve.tensor_scalar(rs[:, 0, :], mv[:, :, 1], EPS, None, ALU.add).then_inc(S("var_ready"), 1)
                dve.wait_ge(S("root_ready"), 1)
                dve.reciprocal(rs[:, 1, :], rs[:, 0, :]).then_inc(S("inv_ready"), 1)
                dve.wait_ge(S("inv_ready"), 1)
                for t in range(NT):
                    if t >= 2:
                        dve.wait_ge(S("turned"), t - 1)
                    dve.tensor_scalar(xn[:, t % 2, :], x[:, t, :], mv[:, t, 0:1], rs[:, 1, t:t + 1], ALU.subtract, ALU.mult).then_inc(S("norm_ready"), 1)

            @block.scalar
            def _(act):
                act.wait_ge(S("var_ready"), 1)
                act.activation(rs[:, 0, :], rs[:, 0, :], ACT.Sqrt).then_inc(S("root_ready"), 1)
                for t in range(NT):
                    act.wait_ge(S("turned"), t + 1)
                    for k in range(KC):
                        act.activation(hT[:, k, t * P:(t + 1) * P], PS[:, 2 * (t % 4) + k // 4, (k % 4) * P:(k % 4 + 1) * P], ACT.Identity,
                                       scale=modT[:, t, first + 8 + k:first + 9 + k], bias=modT[:, t, first + k:first + k + 1]).then_inc(S("columns_ready"), 1)
                act.wait_ge(S("columns_ready"), KC * NT)

            @block.tensor
            def _(pe):
                for t in range(NT):
                    if t >= 4:
                        pe.wait_ge(S("columns_ready"), KC * (t - 3))
                    pe.wait_ge(S("norm_ready"), t + 1)
                    for k in range(KC):
                        mm = pe.transpose(PS[:, 2 * (t % 4) + k // 4, (k % 4) * P:(k % 4 + 1) * P], xn[:, t % 2, k * P:(k + 1) * P], ident[:])
                    mm.then_inc(S("turned"), 1)
        ph.meet()


def project_in(nc, D, layer, hh, hl, B, PS):
    chan, tokm, prm = B["chan"], B["tokm"], B["prm"]
    NCH, TW = 8, TM // 8
    with Phase(nc, "prm_loaded pads_zero wa_loaded wb_loaded ta_loaded tb_loaded hi_ready split acc_ready acc_read tacc_ready tacc_read") as ph:
        S = ph.sem
        wt = ph.sb("wt", [P, 2, KC, P])
        wth, wtl = ph.sb("wth", [P, 2, KC, P], F32R), ph.sb("wtl", [P, 2, KC, P], F32R)
        wk = ph.sb("wk", [P, 2, KC, TW])
        wkh, wkl = ph.sb("wkh", [P, 2, KC, TW], F32R), ph.sb("wkl", [P, 2, KC, TW], F32R)
        WL = ["wa_loaded", "wb_loaded"]
        TL = ["ta_loaded", "tb_loaded"]
        with nc.Block() as block:
            @block.sync
            def _(sp):
                with sp.Fori(0, CT // 2) as i:
                    for b in range(2):
                        sp.wait_ge(S("split"), i * 2 + b + 1)
                        sp.dma_start(wt[:, b], of_layer(of_layer(D["w_ch"], layer), i * 2 + b)).then_inc(S(WL[b]), 16)
                w_tm = of_layer(D["w_tm"], layer)
                for i in range(NCH):
                    if i >= 2:
                        sp.wait_ge(S("split"), CT + 1 + i)
                    sp.dma_start(wk[:, i % 2], w_tm[:, :, i * TW:(i + 1) * TW]).then_inc(S(TL[i % 2]), 16)
                sp.dma_start(prm[:], of_layer(D["prm"], layer)).then_inc(S("prm_loaded"), 16)
                sp.wait_ge(S("prm_loaded"), 16)

            @block.scalar
            def _(act):
                act.sem_inc(S("acc_ready"), 2)
                with act.Fori(0, CT // 2) as i:
                    for b in range(2):
                        act.wait_ge(S(WL[b]), i * 16 + 16)
                        act.wait_ge(S("acc_ready"), i * 2 + b + 1)
                        act.activation(wth[:, b], wt[:, b], ACT.Copy).then_inc(S("hi_ready"), 1)
                for i in range(NCH):
                    act.wait_ge(S(TL[i % 2]), 16 * (i // 2 + 1))
                    if i >= 2:
                        act.wait_ge(S("tacc_ready"), NT * (i - 1))
                    act.activation(wkh[:, i % 2], wk[:, i % 2], ACT.Copy).then_inc(S("hi_ready"), 1)

            @block.gpsimd
            def _(pool):
                pool.sem_inc(S("split"), 2)
                for c in (0, 1 + P, COLS - 1):
                    pool.memset(chan[:, :, c:c + 1], 0.0).then_inc(S("pads_zero"), 1)
                with pool.Fori(0, CT // 2) as i:
                    for b in range(2):
                        pool.wait_ge(S("hi_ready"), i * 2 + b + 1)
                        pool.tensor_tensor(wtl[:, b], wt[:, b], wth[:, b].bitcast(F32), ALU.subtract).then_inc(S("split"), 1)
                for i in range(NCH):
                    pool.wait_ge(S("hi_ready"), CT + i + 1)
                    pool.tensor_tensor(wkl[:, i % 2], wk[:, i % 2], wkh[:, i % 2].bitcast(F32), ALU.subtract).then_inc(S("split"), 1)
                pool.wait_ge(S("pads_zero"), 3)

            @block.tensor
            def _(pe):
                with pe.Fori(0, CT // 2) as i:
                    for b in range(2):
                        pe.wait_ge(S("split"), i * 2 + b + 3)
                        pe.wait_ge(S("acc_read"), i * 6 + 3 * b + 3)
                        n = 0
                        for k in range(KC):
                            for w, x in ((wth, hh), (wth, hl), (wtl, hh)):
                                for z in range(2):
                                    mm = pe.matmul(PS[:, 2 * b + z, 0:HT], w[:, b, k, :], x[:, k, z * HT:(z + 1) * HT], start=(n == 0), stop=(n == 3 * KC - 1))
                                n += 1
                        mm.then_inc(S("acc_ready"), 1)
                o = 0
                for i in range(NCH):
                    pe.wait_ge(S("split"), CT + i + 3)
                    for t in range(NT):
                        if o >= 4:
                            pe.wait_ge(S("tacc_read"), o - 3)
                        n = 0
                        for k in range(KC):
                            for x, w in ((hh, wkh), (hh, wkl), (hl, wkh)):
                                mm = pe.matmul(PS[:, 4 + o % 4, 0:TW], x[:, k, t * P:(t + 1) * P], w[:, i % 2, k, :], start=(n == 0), stop=(n == 3 * KC - 1))
                                n += 1
                        mm.then_inc(S("tacc_ready"), 1)
                        o += 1

            @block.vector
            def _(dve):
                dve.sem_inc(S("acc_read"), 6)
                with dve.Fori(0, CT // 2) as i:
                    for b in range(2):
                        dve.wait_ge(S("acc_ready"), i * 2 + b + 3)
                        row = chan[:, ds(i * 2 + b, 1), :].rearrange("p a n -> p (a n)")
                        dve.tensor_copy(row[:, 1:P + 1], PS[:, 2 * b, 0:P]).then_inc(S("acc_read"), 1)
                        dve.tensor_copy(row[:, P + 2:HT + 2], PS[:, 2 * b, P:HT]).then_inc(S("acc_read"), 1)
                        dve.tensor_copy(row[:, HT + 2:COLS - 1], PS[:, 2 * b + 1, 0:HT]).then_inc(S("acc_read"), 1)
                for o in range(NCH * NT):
                    i, t = o // NT, o % NT
                    dve.wait_ge(S("tacc_ready"), o + 1)
                    dve.tensor_copy(tokm[:, t, i * TW:(i + 1) * TW], PS[:, 4 + o % 4, 0:TW]).then_inc(S("tacc_read"), 1)
                dve.wait_ge(S("acc_read"), 6 + 3 * CT)
                dve.wait_ge(S("tacc_read"), NCH * NT)
        ph.meet()


def prepare(nc, D, layer, B, modT, scond, grow, PS, ident, ones):
    chan, tokm, prm, kkn, gates = B["chan"], B["tokm"], B["prm"], B["kkn"], B["gates"]
    with Phase(nc, "c_loaded shifted conv_ready silu_done low_done key_ready square_ready sums_ready root_ready z_ready ln_ready "
                   "bias_loaded w0_loaded w1_loaded w2_loaded w_used rows_ready rows_kept cols_ready mod_ready dve_step act_step") as ph:
        S = ph.sem
        tmp = ph.sb("tmp", [P, CT_RW, IN])
        blk = ph.sb("blk", [P, P])
        cos = ph.sb("cos", [P, NT - 1, 32])
        sin = ph.sb("sin", [P, NT - 1, 32])
        gbias = ph.sb("gbias", [P, 16])
        lz = ph.sb("lz", [P, NT, 2, 4])
        bmod = ph.sb("bmod", [1, 2 * MOD_W])
        mrow = ph.sb("mrow", [2, MOD_W])
        wm = ph.sb("wm", [P, 3, MOD_W])
        loads = [(blk[:], D["c_blk"]), (cos[:], D["c_cos"]), (sin[:], D["c_sin"]),
                 (gbias[:], of_layer(D["gbias"], layer))]
        rw, ml = chan[:, 0:CT_RW, :], chan[:, CT_RW:CT, :]
        conv = prm[:, 34:46].rearrange("p (c j) -> p j c", j=3)
        g4 = gates[:].rearrange("p t (d x h) -> p t d x h", d=2, x=2)
        logf = [g4[:, :, d, 1, :] for d in range(2)]
        t2, t3 = tmp[:, 0:4, :], tmp[:, 4:8, :]
        with nc.Block() as block:
            @block.sync
            def _(sp):
                for dst, src in loads:
                    sp.dma_start(dst, src).then_inc(S("c_loaded"), 16)
                sp.dma_start(bmod[:], of_layer(D["b_mod"], layer)[0:1, MOD_W:3 * MOD_W]).then_inc(S("bias_loaded"), 16)
                load_mod(sp, S, D, layer, wm, (1, 2))

            @block.vector
            def _(dve):
                ch = Chain(dve, S("dve_step"))
                ch(dve.tensor_tensor(tmp[:], rw[:, :, 0:IN], rw[:, :, 2:IN + 2], ALU.add))
                ch(dve.scalar_tensor_tensor(tmp[:], tmp[:], 0.5, rw[:, :, 1:IN + 1], ALU.mult, ALU.subtract))
                ch(dve.tensor_tensor(tmp[:], tmp[:], bc(prm[:, 0:CT_RW], 2, IN), ALU.mult))
                dve.tensor_tensor(rw[:, :, 1:IN + 1], rw[:, :, 1:IN + 1], tmp[:], ALU.add).then_inc(S("shifted"), 1)
                dve.wait_ge(S("shifted"), 1)
                dve.tensor_tensor(kkn[:], rw[:, 4:8, 1:IN + 1], bc(prm[:, 22:26], 2, IN), ALU.mult).then_inc(S("key_ready"), 1)
                t0, t1 = tmp[:, 4:8, :], tmp[:, 8:12, :]
                ch(dve.tensor_tensor(t0, ml[:, :, 0:IN], bc(conv[:, 0, :], 2, IN), ALU.mult))
                ch(dve.tensor_tensor(t1, ml[:, :, 1:IN + 1], bc(conv[:, 1, :], 2, IN), ALU.mult))
                ch(dve.tensor_tensor(t0, t0, t1, ALU.add))
                ch(dve.tensor_tensor(t1, ml[:, :, 2:IN + 2], bc(conv[:, 2, :], 2, IN), ALU.mult))
                dve.tensor_tensor(t0, t0, t1, ALU.add).then_inc(S("conv_ready"), 1)
                dve.wait_ge(S("c_loaded"), 16 * len(loads))
                dve.tensor_tensor(gates[:], tokm[:, :, GATES:TM], bc(gbias[:], 1, NT), ALU.add).then_inc(S("z_ready"), 1)
                qk = tokm[:, 1:NT, 0:512].rearrange("p t (h z i) -> p t h z i", h=8, z=2)
                x1, x2 = qk[:, :, :, 0, :], qk[:, :, :, 1, :]
                cb, sbb = bc(cos[:], 2, 8), bc(sin[:], 2, 8)
                r = [tmp[:, 8:14, :].rearrange("p a n -> p (a n)")[:, i * 1024:(i + 1) * 1024].rearrange("p (t h i) -> p t h i", t=4, h=8) for i in range(3)]
                dve.wait_ge(S("conv_ready"), 1)
                ch.inc(dve.tensor_tensor(r[0], x1, cb, ALU.mult))
                ch.inc(dve.tensor_tensor(r[1], x2, sbb, ALU.mult))
                ch(dve.tensor_tensor(r[2], x1, sbb, ALU.mult))
                ch(dve.tensor_tensor(x1, r[0], r[1], ALU.subtract))
                ch(dve.tensor_tensor(r[0], x2, cb, ALU.mult))
                ch(dve.tensor_tensor(x2, r[0], r[2], ALU.add))
                ch(dve.tensor_scalar(tokm[:, :, 256:512], tokm[:, :, 256:512], HD ** -0.5, None, ALU.mult))
                dve.wait_ge(S("silu_done"), 1)
                ch(dve.tensor_scalar(ml[:, 2:4, 1:IN + 1], ml[:, 2:4, 1:IN + 1], HD ** -0.5, None, ALU.mult))
                for i in range(8):
                    dve.wait_ge(S("sums_ready"), i + 1)
                    a = (0, 321)[i % 2]
                    n = (321, IN - 321)[i % 2]
                    dve.tensor_scalar(t3[:, i // 2, a:a + n], PS[:, i, 0:n], 1e-24, None, ALU.max).then_inc(S("ln_ready"), 1)
                dve.wait_ge(S("root_ready"), 1)
                ch(dve.tensor_scalar(t3, t3, 1e-12, None, ALU.max))
                ch(dve.reciprocal(t3, t3))
                ch(dve.tensor_tensor(kkn[:], kkn[:], t3, ALU.mult))
                keep_columns(dve, S, PS[:, 7, 384:416], modT, 16)
                dve.wait_ge(S("act_step"), 4)
                for d in range(2):
                    ch(dve.tensor_scalar(logf[d], logf[d], 0.0, None, ALU.min))
                    ch(dve.tensor_tensor(logf[d], logf[d], lz[:, :, d, :], ALU.subtract))

            @block.scalar
            def _(act):
                act.wait_ge(S("shifted"), 1)
                act.activation(chan[0:64, 12, 1:IN + 1], chan[0:64, 12, 1:IN + 1], ACT.Tanh).then_inc(S("low_done"), 1)
                act.activation(chan[:, 13, 1:IN + 1], chan[:, 13, 1:IN + 1], ACT.Sigmoid).then_inc(S("low_done"), 1)
                act.wait_ge(S("key_ready"), 1)
                act.activation(t2, kkn[:], ACT.Square).then_inc(S("square_ready"), 1)
                act.wait_ge(S("conv_ready"), 1)
                act.activation(ml[:, :, 1:IN + 1], tmp[:, 4:8, :], ACT.Silu).then_inc(S("silu_done"), 1)
                for part in range(2):
                    act.wait_ge(S("rows_ready"), part + 1)
                    rows = PS[0:2, 4 * part:4 * part + 4, :].rearrange("p b n -> p (b n)")
                    g, m = part * D_MODEL, (1 - part) * D_MODEL
                    act.activation(grow[:, part, :], rows[:, g:g + D_MODEL], ACT.Copy).then_inc(S("rows_kept"), 1)
                    act.activation(mrow[:, part * D_MODEL:(part + 1) * D_MODEL], rows[:, m:m + D_MODEL], ACT.Copy).then_inc(S("rows_kept"), 1)
                act.wait_ge(S("z_ready"), 1)
                for d in range(2):
                    act.activation(lz[:, :, d, :], logf[d], ACT.Abs).then_inc(S("act_step"), 1)
                act.wait_ge(S("act_step"), 2)
                act.activation(lz[:], lz[:], ACT.Exp, scale=-1.0).then_inc(S("act_step"), 1)
                act.wait_ge(S("act_step"), 3)
                act.activation(lz[:], lz[:], ACT.Ln, bias=1.0).then_inc(S("act_step"), 1)
                act.wait_ge(S("ln_ready"), 8)
                act.activation(t3, t3, ACT.Sqrt).then_inc(S("root_ready"), 1)
                act.wait_ge(S("low_done"), 2)

            @block.tensor
            def _(pe):
                pe.wait_ge(S("bias_loaded"), 16)
                for n in range(2 * KC):
                    mod_rows(pe, S, PS, scond, ones, bmod, wm, n, 4 * (n // KC))
                pe.wait_ge(S("rows_kept"), 4)
                for j in range(2 * KC):
                    mm = pe.transpose(PS[:, 7, 384 + 2 * j:384 + 2 * j + 2], mrow[:, j * P:(j + 1) * P], ident[0:2, 0:2])
                mm.then_inc(S("cols_ready"), 1)
                pe.wait_ge(S("square_ready"), 1)
                pe.wait_ge(S("c_loaded"), 16 * len(loads))
                for i in range(8):
                    a = (0, 321)[i % 2]
                    n = (321, IN - 321)[i % 2]
                    pe.matmul(PS[:, i, 0:n], blk[:], t2[:, i // 2, a:a + n], start=True, stop=True).then_inc(S("sums_ready"), 1)
        ph.meet()


def rwkv(nc, D, layer, B, PS, ident, ones):
    with ExitStack() as ctx:
        W = {n: tile(nc, ctx, "r_" + n, s) for n, s in {
            "tri": [P, 2, 257],
            "strict": [P, 2, P], "near": [P, 2, P],
            "incl": [P, 2, P], "strictT": [P, 2, P],
            "lvl": [P, 4, P],
            "lora": [P, 2, 512],
            "w0": [1, 2, 512],
            "state": [P, 2, 4, HD]}.items()}
        for n, s in {"s0": [P, 4, HD], "low": [P, P], "vt": [P, 512], "eM": [P, 4], "ePC": [P, 4],
                     "bt": [P, 4, P], "kt": [P, 4, P], "KR": [P, 4, 2, P], "btk": [P, 512], "ktk": [P, 512],
                     "G": [P, 4, 3, P], "L": [P, 4, P], "T": [P, 4, HD], "E": [P, 4, P], "ET": [P, 4, P], "Z": [P, 4, P], "ZT": [P, 4, P]}.items():
            W[n] = [tile(nc, ctx, f"r_{n}{d}", s) for d in range(2)]
        W["sg"], W["a"], W["eN"], W["v"] = W["E"], W["Z"], W["ET"], W["ZT"]
        load_all(nc, [(W["tri"][:], D["c_tri"]), (W["strict"][:], D["c_strict"]), (W["incl"][:], D["c_incl"]), (W["near"][:], D["c_near"]),
                      (W["strictT"][:], D["c_strictT"]), (W["lvl"][:], D["c_lvl"]),
                      (W["lora"][:], of_layer(D["lora"], layer)), (W["w0"][:], of_layer(D["w0"], layer))])
        with Phase(nc, "zeroed") as ph:
            with nc.Block() as block:
                @block.gpsimd
                def _(pool):
                    pool.memset(W["state"][:], 0.0).then_inc(ph.sem("zeroed"), 1)
                    pool.memset(B["Y"][:], 0.0).then_inc(ph.sem("zeroed"), 1)
                    pool.wait_ge(ph.sem("zeroed"), 2)
            ph.meet()
        rwkv_tiles(nc, B, W, PS, ident, ones, (0, 0))
        load_all(nc, [(of_layer(D["o_rwkv"], layer), W["state"][:])])
        load_all(nc, [(W["state"][:], of_layer(D["s_rwkv"], layer))])
        with nc.Fori(0, NT - 1) as j:
            rwkv_tiles(nc, B, W, PS, ident, ones, (j + 1, 4 - j))


def rwkv_tiles(nc, B, W, PS, ident, ones, tiles):
    chan, prm, kkn, Y, state = B["chan"], B["prm"], B["kkn"], B["Y"], W["state"]
    names = ("cur_ready z_ready a_ready vt_turned sg_ready rate_ready vt_ready cum_ready exp_ready feat_ready tok_turned tok_ready "
             "g_ready g_read l_ready inv_start zp_ready pow_ready pow_dve pow_act lm_ready merge_ready zt_turned merge_act zt_ready merge_dve "
             "rh_ready rhn_ready sa_ready sas_ready y_ready half_done")
    HEADS = [(h, h // 2, slice(64 * (h % 2), 64 * (h % 2) + 64), 2 * (h % 2) + h // 2) for h in range(4)]

    with Phase(nc, "dve_step " + " ".join(f"{n}{d}" for n in names.split() for d in range(2))) as ph:
        def S(name, d):
            return ph.sem(f"{name}{d}")

        def four(d, b, n=P):
            return PS[:, 4 * d + b, 0:4 * n].rearrange("p (h n) -> p h n", n=n)

        def parity(d, b, n):
            return PS[:, 4 * d + b:4 * d + b + 2, 0:2 * n].rearrange("p x (j n) -> p x j n", n=n)

        def paired(ap, d, k):
            return ap.rearrange("p s (a x n) -> p s x a n", x=2, n=16 << k)[:, :, 1 - d]

        with nc.Block() as block:
            @block.scalar
            def _(act):
                for d in range(2):
                    c0 = tile_cols(tiles[d])
                    act.activation(W["low"][d][:], chan[:, 12, ds(c0, P)], ACT.Copy).then_inc(S("cur_ready", d), 1)
                    act.activation(W["v"][d][:], chan[:, 8:12, ds(c0, P)], ACT.Copy).then_inc(S("cur_ready", d), 1)
                for d in range(2):
                    act.wait_ge(S("z_ready", d), 1)
                    act.activation(W["sg"][d][:].rearrange("p h n -> p (h n)"), PS[:, 4 * d, :], ACT.Sigmoid).then_inc(S("sg_ready", d), 1)
                    act.wait_ge(S("a_ready", d), 1)
                    for c in range(4):
                        act.activation(W["a"][d][:, c, :], four(d, 1)[:, c, :], ACT.Sigmoid,
                                       bias=prm[:, 14 + 4 * d + c:15 + 4 * d + c]).then_inc(S("rate_ready", d), 1)
                    act.wait_ge(S("vt_turned", d), 1)
                    act.activation(W["vt"][d][:], PS[:, 4 * d + 2, :], ACT.Copy).then_inc(S("vt_ready", d), 1)
                for d in range(2):
                    act.wait_ge(S("cum_ready", d), 1)
                    act.activation(W["eN"][d][:], four(d, 3), ACT.Exp, scale=-1.0).then_inc(S("exp_ready", d), 1)
                    act.activation(W["KR"][d][:, :, 1, :], four(d, 3), ACT.Exp).then_inc(S("exp_ready", d), 1)
                    act.activation(W["KR"][d][:, :, 0, :], four(d, 0), ACT.Exp).then_inc(S("exp_ready", d), 1)
                    act.activation(W["eM"][d][:], PS[:, 4 * d + 1, 0:4], ACT.Exp).then_inc(S("exp_ready", d), 1)
                for d in range(2):
                    act.wait_ge(S("tok_turned", d), 1)
                    act.activation(W["btk"][d][:], PS[:, 4 * d + 2, :], ACT.Copy).then_inc(S("tok_ready", d), 1)
                    act.activation(W["ktk"][d][:], PS[:, 4 * d + 1, :], ACT.Copy).then_inc(S("tok_ready", d), 1)
                for half in range(2):
                    for k in range(3):
                        for d in range(2):
                            act.wait_ge(S("pow_ready", d), 3 * half + k + 1)
                            if k < 2:
                                act.activation(W["E"][d][:], four(d, 0), ACT.Copy).then_inc(S("pow_act", d), 1)
                            act.activation(W["ET"][d][:], four(d, 1), ACT.Copy).then_inc(S("pow_act", d), 1)
                    for k in range(3):
                        for d in range(2):
                            act.wait_ge(S("merge_ready", d), 6 * half + 2 * k + 1)
                            act.activation(W["T"][d][:], four(d, 0, HD), ACT.Copy).then_inc(S("merge_act", d), 1)
                            act.wait_ge(S("zt_turned", d), 3 * half + k + 1)
                            act.activation(W["ZT"][d][:], four(d, 1), ACT.Copy).then_inc(S("zt_ready", d), 1)
                    for d in range(2):
                        act.wait_ge(S("rh_ready", d), half + 1)
                        act.activation(W["L"][d][:, 0:2, :].rearrange("p j (x n) -> p x j n", x=2), parity(d, 0, HD), ACT.Copy,
                                       scale=-1.0).then_inc(S("rhn_ready", d), 1)
                    for d in range(2):
                        act.wait_ge(S("sa_ready", d), half + 1)
                        act.activation(W["L"][d][:, 2:4, :].rearrange("p j n -> p (j n)"), PS[:, 4 * d + 2, 0:4 * HD], ACT.Copy).then_inc(S("sas_ready", d), 1)

            @block.vector
            def _(dve):
                ch = Chain(dve, ph.sem("dve_step"))
                for d in range(2):
                    c0 = tile_cols(tiles[d])
                    r, k = chan[:, 0:4, ds(c0, P)], chan[:, 4:8, ds(c0, P)]
                    kk = kkn[:, :, ds(c0 - 1, P)]
                    kt, bt, KR, a, eN = (W[n][d] for n in ("kt", "bt", "KR", "a", "eN"))
                    dve.wait_ge(S("rate_ready", d), 4)
                    for c in range(4):
                        ch.inc(dve.tensor_scalar(kt[:, c, :], a[:, c, :], 1.0, prm[:, 26 + c:27 + c], ALU.subtract, ALU.mult))
                    ch(dve.tensor_tensor(bt[:], kk, a[:], ALU.mult))
                    ch(dve.scalar_tensor_tensor(kt[:], kt[:], 1.0, k, ALU.add, ALU.mult))
                    dve.wait_ge(S("exp_ready", d), 4)
                    ch.inc(dve.tensor_copy(W["ePC"][d][:], KR[:, :, 1, P - 1 if d == 0 else 0]))
                    ch.sync()
                    dve.tensor_tensor(bt[:], bt[:], eN[:], ALU.mult).then_inc(S("feat_ready", d), 1)
                    dve.tensor_tensor(kt[:], kt[:], eN[:], ALU.mult).then_inc(S("feat_ready", d), 1)
                    dve.tensor_tensor(KR[:, :, 0, :], KR[:, :, 0, :], kk, ALU.mult).then_inc(S("feat_ready", d), 1)
                    dve.tensor_tensor(KR[:, :, 1, :], KR[:, :, 1, :], r, ALU.mult).then_inc(S("feat_ready", d), 1)
                    dve.tensor_tensor(W["s0"][d][:], state[:, d], bc(W["eM"][d][:], 2, HD), ALU.mult).then_inc(S("feat_ready", d), 1)
                for half in range(2):
                    for d in range(2):
                        E, G = W["E"][d], W["G"][d]
                        for h, j, q, s in HEADS:
                            dve.wait_ge(S("g_ready", d), 4 * half + h + 1)
                            g = PS[:, 4 * d + h, :].rearrange("p (x y n) -> p x y n", x=2, y=2)
                            dve.tensor_tensor(E[:, s, :], g[:, 0, 0, :], W["near"][:, d, :], ALU.mult).then_inc(S("g_read", d), 1)
                            dve.tensor_tensor(G[:, h, 0, :], g[:, 1, 0, :], W["strict"][:, d, :], ALU.mult).then_inc(S("g_read", d), 1)
                            dve.tensor_tensor(G[:, h, 1:3, :], g[:, :, 1, :], bc(W["incl"][:, d, :], 1, 2), ALU.mult).then_inc(S("g_read", d), 1)
                    for d in range(2):
                        L, E, ET = W["L"][d], W["E"][d], W["ET"][d]
                        dve.wait_ge(S("l_ready", d), half + 1)
                        strictT = bc(bc(W["strictT"][:, d, :], 1, 2), 1, 2)
                        ch.inc(dve.tensor_tensor(L[:].rearrange("p (x j) n -> p x j n", x=2), parity(d, 0, P), strictT, ALU.mult))
                        dve.wait_ge(S("g_read", d), 12 * half + 12)
                        dve.tensor_tensor(W["Z"][d][:], bc(ident[:], 1, 4), E[:], ALU.subtract).then_inc(S("inv_start", d), 1)
                        ch.sync()
                        dve.tensor_tensor(ET[:], L[:], bc(W["lvl"][:, 0, :], 1, 4), ALU.mult).then_inc(S("inv_start", d), 1)
                    for k in range(1, 4):
                        for d in range(2):
                            Z = W["Z"][d]
                            dve.wait_ge(S("zp_ready", d), 3 * half + k)
                            if k > 1:
                                dve.wait_ge(S("pow_dve", d), 3 * half + k - 1)
                            else:
                                dve.wait_ge(S("inv_start", d), 2 * half + 2)
                            dve.tensor_tensor(Z[:], Z[:], four(d, 2), ALU.add).then_inc(S("pow_dve", d), 1)
                    for k in range(3):
                        for d in range(2):
                            dve.wait_ge(S("merge_ready", d), 6 * half + 2 * k + 2)
                            if k:
                                dve.wait_ge(S("merge_dve", d), 3 * half + k)
                            else:
                                dve.wait_ge(S("pow_dve", d), 3 * half + 3)
                            Zc = paired(W["Z"][d][:], d, k)
                            new = four(d, 2, HD).rearrange("p s (a n) -> p s a n", n=16 << k)
                            dve.tensor_tensor(Zc, Zc, new, ALU.subtract).then_inc(S("merge_dve", d), 1)
                    for d in range(2):
                        dve.wait_ge(S("y_ready", d), 2 * half + 1)
                        yt = Y[:, ds(tiles[d], 1), 256 + 256 * half:512 + 256 * half].rearrange("p a (j x n) -> p (a x) j n", x=2, n=HD)
                        ch.inc(dve.tensor_tensor(yt, yt, parity(d, 0, HD), ALU.add))
                        dve.wait_ge(S("y_ready", d), 2 * half + 2)
                        pairs = PS[:, 4 * d + 3, 0:256].rearrange("p (j x n) -> p j x n", j=2, x=2)
                        js = slice(2 * half, 2 * half + 2)
                        for x in range(2):
                            q = slice(64 * x, 64 * x + 64)
                            ch.inc(dve.tensor_tensor(state[q, d, js, :], W["s0"][d][q, js, :], pairs[q, :, x, :], ALU.add))
                        ch.sync()
                        dve.tensor_tensor(state[:, d, js, :], state[:, d, js, :], bc(W["ePC"][d][:, js], 2, HD), ALU.mult).then_inc(S("half_done", d), 1)
                for d in range(2):
                    dve.wait_ge(S("half_done", d), 2)

            @block.gpsimd
            def _(pool):
                for half in range(2):
                    for k, out in enumerate(("E", "ET", "E")):
                        for d in range(2):
                            last = (S("pow_ready", d), 3 * half + 3), (S("zp_ready", d), 3 * half + 3), (S("merge_ready", d), 6 * half + 1)
                            pool.wait_ge(*last[k])
                            pool.tensor_tensor(W[out][d][:], W["L"][d][:], bc(W["lvl"][:, k + 1, :], 1, 4), ALU.mult).then_inc(S("lm_ready", d), 1)

            @block.tensor
            def _(pe):
                for d in range(2):
                    b, low = 4 * d, W["low"][d]
                    pe.wait_ge(S("cur_ready", d), 2)
                    pe.matmul(PS[:, b, :], low[0:64, :], W["lora"][0:64, d, :], start=True, stop=False)
                    pe.matmul(PS[:, b, :], ones[0:1, :], W["w0"][0:1, d, :], start=False, stop=True).then_inc(S("z_ready", d), 1)
                    for c in range(4):
                        mm = pe.matmul(PS[:, b + 1, c * P:(c + 1) * P], W["lora"][64:128, d, c * P:(c + 1) * P], low[64:128, :], start=True, stop=True)
                    mm.then_inc(S("a_ready", d), 1)
                    for c in range(4):
                        mm = pe.transpose(PS[:, b + 2, c * P:(c + 1) * P], W["v"][d][:, c, :], ident[:])
                    mm.then_inc(S("vt_turned", d), 1)
                for d in range(2):
                    b = 4 * d
                    pe.wait_ge(S("sg_ready", d), 1)
                    pe.wait_ge(S("rate_ready", d), 4)
                    for c in range(4):
                        w = W["sg"][d][:, c, :]
                        pe.matmul(PS[:, b + 3, c * P:(c + 1) * P], w, W["tri"][:, d, 0:P], start=True, stop=True)
                        pe.matmul(PS[:, b, c * P:(c + 1) * P], w, W["tri"][:, d, P:2 * P], start=True, stop=True)
                        mm = pe.matmul(PS[:, b + 1, c:c + 1], w, W["tri"][:, d, 2 * P:2 * P + 1], start=True, stop=True)
                    mm.then_inc(S("cum_ready", d), 1)
                for d in range(2):
                    b = 4 * d
                    pe.wait_ge(S("vt_ready", d), 1)
                    pe.wait_ge(S("feat_ready", d), 2)
                    for c in range(4):
                        pe.transpose(PS[:, b + 2, c * P:(c + 1) * P], W["bt"][d][:, c, :], ident[:])
                        mm = pe.transpose(PS[:, b + 1, c * P:(c + 1) * P], W["kt"][d][:, c, :], ident[:])
                    mm.then_inc(S("tok_turned", d), 1)
                for half in range(2):
                    for d in range(2):
                        bt, kt, KR = W["bt"][d], W["kt"][d], W["KR"][d]
                        if half:
                            pe.wait_ge(S("half_done", d), 1)
                        else:
                            pe.wait_ge(S("feat_ready", d), 5)
                            pe.wait_ge(S("tok_ready", d), 2)
                        for h, j, q, s in HEADS:
                            kr = KR[q, 2 * half + j].rearrange("p x n -> p (x n)")
                            pe.matmul(PS[:, 4 * d + h, 0:256], bt[q, 2 * half + j, :], kr, start=True, stop=True)
                            pe.matmul(PS[:, 4 * d + h, 256:512], kt[q, 2 * half + j, :], kr, start=True, stop=True).then_inc(S("g_ready", d), 1)
                    for d in range(2):
                        pe.wait_ge(S("g_read", d), 12 * half + 6)
                        for h, j, q, s in HEADS:
                            mm = pe.matmul(PS[:, 4 * d + h % 2, j * P:(j + 1) * P], W["KR"][d][q, 2 * half + j, 0, :],
                                           W["bt"][d][q, 2 * half + j, :], start=True, stop=True)
                        mm.then_inc(S("l_ready", d), 1)
                    for k in range(4):
                        for d in range(2):
                            E, ET, Z = (W[n][d] for n in ("E", "ET", "Z"))
                            if k:
                                pe.wait_ge(S("pow_act", d), 5 * half + (2, 4, 5)[k - 1])
                            else:
                                pe.wait_ge(S("inv_start", d), 2 * half + 2)
                            if k > 1:
                                pe.wait_ge(S("pow_dve", d), 3 * half + k - 1)
                            if k:
                                for s in range(4):
                                    mm = pe.matmul(PS[:, 4 * d + 2, s * P:s * P + P], ET[:, s, :], Z[:, s, :], start=True, stop=True)
                                mm.then_inc(S("zp_ready", d), 1)
                            if k < 3:
                                for s in range(4):
                                    o = slice(s * P, s * P + P)
                                    if k < 2:
                                        pe.matmul(PS[:, 4 * d, o], ET[:, s, :], E[:, s, :], start=True, stop=True)
                                    mm = pe.matmul(PS[:, 4 * d + 1, o], E[:, s, :], ET[:, s, :], start=True, stop=True)
                                mm.then_inc(S("pow_ready", d), 1)
                    for k in range(3):
                        for d in range(2):
                            O, Z = W["ET" if k == 1 else "E"][d], W["Z"][d]
                            pe.wait_ge(S("lm_ready", d), 3 * half + k + 1)
                            if k:
                                pe.wait_ge(S("merge_dve", d), 3 * half + k)
                            else:
                                pe.wait_ge(S("pow_dve", d), 3 * half + 3)
                            Zc = paired(Z[:], d, k)
                            for s in range(4):
                                mm = pe.matmul(PS[:, 4 * d, s * HD:(s + 1) * HD].rearrange("p (a n) -> p a n", n=16 << k), O[:, s, :], Zc[:, s], start=True, stop=True)
                            mm.then_inc(S("merge_ready", d), 1)
                            for s in range(4):
                                mm = pe.transpose(PS[:, 4 * d + 1, s * P:s * P + P], Z[:, s, :], ident[:])
                            mm.then_inc(S("zt_turned", d), 1)
                        for d in range(2):
                            pe.wait_ge(S("merge_act", d), 3 * half + k + 1)
                            pe.wait_ge(S("zt_ready", d), 3 * half + k + 1)
                            for s in range(4):
                                mm = pe.matmul(PS[:, 4 * d + 2, s * HD:(s + 1) * HD], W["ZT"][d][:, s, :], W["T"][d][:, s, :], start=True, stop=True)
                            mm.then_inc(S("merge_ready", d), 1)
                    for d in range(2):
                        KR, G, s0, vt = (W[n][d] for n in ("KR", "G", "s0", "vt"))
                        for h, j, q, s in HEADS:
                            o, J = slice(j * HD, (j + 1) * HD), 2 * half + j
                            pe.matmul(PS[:, 4 * d + h % 2, o], KR[q, J, 0, :], s0[q, J, :], start=True, stop=False)
                            mm = pe.matmul(PS[:, 4 * d + h % 2, o], G[:, h, 0, :], vt[:, (4 * half + h) * HD:(4 * half + h + 1) * HD], start=False, stop=True)
                        mm.then_inc(S("rh_ready", d), 1)
                    for d in range(2):
                        pe.wait_ge(S("rhn_ready", d), half + 1)
                        pe.wait_ge(S("merge_dve", d), 3 * half + 3)
                        for h, j, q, s in HEADS:
                            mm = pe.matmul(PS[:, 4 * d + 2, h * HD:(h + 1) * HD], W["Z"][d][:, s, :], W["L"][d][:, j, (h % 2) * HD:(h % 2 + 1) * HD],
                                           start=True, stop=True)
                        mm.then_inc(S("sa_ready", d), 1)
                    for d in range(2):
                        KR, G, s0, vt, L = (W[n][d] for n in ("KR", "G", "s0", "vt", "L"))
                        pe.wait_ge(S("sas_ready", d), half + 1)
                        for h, j, q, s in HEADS:
                            o, J, vc = slice(j * HD, (j + 1) * HD), 2 * half + j, slice((4 * half + h) * HD, (4 * half + h + 1) * HD)
                            sa = L[:, 2 + j, (h % 2) * HD:(h % 2 + 1) * HD]
                            pe.matmul(PS[:, 4 * d + h % 2, o], KR[q, J, 1, :], s0[q, J, :], start=True, stop=False)
                            pe.matmul(PS[:, 4 * d + h % 2, o], G[:, h, 1, :], sa, start=False, stop=False)
                            mm = pe.matmul(PS[:, 4 * d + h % 2, o], G[:, h, 2, :], vt[:, vc], start=False, stop=True)
                        mm.then_inc(S("y_ready", d), 1)
                        for j in range(2):
                            o, c = slice(j * P, (j + 1) * P), slice((2 * half + j) * P, (2 * half + j + 1) * P)
                            pe.matmul(PS[:, 4 * d + 3, o], W["btk"][d][:, c], L[:, 2 + j, :], start=True, stop=False)
                            mm = pe.matmul(PS[:, 4 * d + 3, o], W["ktk"][d][:, c], vt[:, c], start=False, stop=True)
                        mm.then_inc(S("y_ready", d), 1)
        ph.meet()


def row_bc(ap, layer):
    v = ap[ds(layer, 1)].partition_broadcast(P)
    names = " ".join("bcdefg"[:len(v.shape) - 2])
    return v.rearrange(f"p a {names} -> p (a {names.split()[0]}) {' '.join(names.split()[1:])}")


def linear(nc, D, layer, B, PS, ident, ones):
    with ExitStack() as ctx:
        def sb(name, shape, dt=F32):
            return tile(nc, ctx, name, shape, dt)

        W = {n: sb("l_" + n, s) for n, s in {
            "cum": [P, 2, P], "negm": [P, 2, P], "dist": [P, 2, P], "pos": [P, 2, 3],
            "rdec": [P, 8], "wret": [P, 2, 4, P], "fret": [P, 2, 3, 4],
            "state": [P, 2, 4, HD + 1],
            "m": [P, 2, 4]}.items()}
        for n, s in {
            "qk": [P, 512], "qT": [P, 4, P], "kT": [P, 4, P], "va": [P, 8, HD + 1], "gc": [P, 16],
            "b": [P, 8], "c": [P, 4], "diag": [P, 4, P], "Dm": [P, 4, P], "gl": [P, 4], "g": [P, 4], "mn": [P, 4],
            "sm": [P, 4, 4], "f": [P, 3, 8], "cs": [P, 4], "SC": [P, 8, P], "SCT": [P, 8, P], "ku": [P, 8, HD],
            "num": [P, 8, HD + 1], "den": [P, 4]}.items():
            W[n] = [sb(f"l_{n}{d}", s) for d in range(2)]
        load_all(nc, [(W["cum"][:], D["c_cum"]), (W["negm"][:], D["c_negm"]), (W["dist"][:], D["c_dist"]),
                      (W["pos"][:], D["c_pos"]), (W["rdec"][:], row_bc(D["ret_decay"], layer))])
        with Phase(nc, "zeroed lg_ready dist_ready w_ready dve_step") as ph:
            S = ph.sem
            with nc.Block() as block:
                @block.gpsimd
                def _(pool):
                    pool.memset(W["state"][:], 0.0).then_inc(S("zeroed"), 1)
                    pool.memset(W["m"][:], 0.0).then_inc(S("zeroed"), 1)
                    for d in range(2):
                        pool.memset(W["va"][d][:], 1.0).then_inc(S("zeroed"), 1)
                    pool.wait_ge(S("zeroed"), 4)

                @block.scalar
                def _(act):
                    act.activation(W["rdec"][:], W["rdec"][:], ACT.Exp).then_inc(S("lg_ready"), 1)
                    act.wait_ge(S("dist_ready"), 1)
                    act.activation(W["wret"][:], W["wret"][:], ACT.Exp).then_inc(S("w_ready"), 1)
                    act.activation(W["fret"][:], W["fret"][:], ACT.Exp).then_inc(S("w_ready"), 1)
                    act.wait_ge(S("w_ready"), 2)

                @block.vector
                def _(dve):
                    ch = Chain(dve, S("dve_step"))
                    dve.wait_ge(S("lg_ready"), 1)
                    ch(dve.tensor_scalar(W["rdec"][:], W["rdec"][:], -1.0, None, ALU.mult))
                    for d in range(2):
                        for h in range(4):
                            lg = W["rdec"][:, 4 * d + h:4 * d + h + 1]
                            ch.inc(dve.scalar_tensor_tensor(W["wret"][:, d, h, :], W["dist"][:, d, :], lg, W["negm"][:, d, :], ALU.mult, ALU.add))
                            ch.inc(dve.tensor_scalar(W["fret"][:, d, :, h], W["pos"][:, d, :], lg, None, ALU.mult))
                    ch.sync()
                    dve.engine_nop().then_inc(S("dist_ready"), 1)
            ph.meet()
        linear_tiles(nc, B, W, PS, ident, ones, (0, 0))
        load_all(nc, [(of_layer(D["o_la"], layer), W["state"][:]), (D["o_m"][ds(layer, 1), :], W["m"][0:1].rearrange("p d h -> p (d h)"))])
        load_all(nc, [(W["state"][:], of_layer(D["s_la"], layer)), (W["m"][:].rearrange("p d h -> p (d h)"), row_bc(D["s_m"], layer))])
        with nc.Fori(0, NT - 1) as j:
            linear_tiles(nc, B, W, PS, ident, ones, (j + 1, 4 - j))


def linear_tiles(nc, B, W, PS, ident, ones, tiles):
    chan, tokm, gates, Y = B["chan"], B["tokm"], B["gates"], B["Y"]
    state, m = W["state"], W["m"]
    KV = 4 * (HD + 1)

    def work(names, d):
        return [W[n][d] for n in names.split()]

    def by_parity(ap):
        return ap.rearrange("p (j x) n -> p x j n", x=2)

    def halves(d, b, n):
        return PS[:, 4 * d + b:4 * d + b + 2, 0:4 * n].rearrange("p x (j n) -> p x j n", n=n)

    def heads(d, b, n):
        return PS[:, 4 * d + b, 0:4 * n].rearrange("p (h n) -> p h n", n=n)

    with Phase(nc, "cur_ready v_ready qk_turned qk_ready b_ready diag_ready cb_ready logs_ready w_ready s_ready sc_ready "
                   "sct_turned sct_ready out_ready dve_step") as ph:
        S = ph.sem
        with nc.Block() as block:
            @block.gpsimd
            def _(pool):
                for d in range(2):
                    for i, c0 in enumerate((512, ML_V)):
                        pool.tensor_copy(W["va"][d][:, 4 * i:4 * i + 4, 0:HD], tokm[:, ds(tiles[d], 1), c0:c0 + 256].rearrange("p a (h n) -> p (a h) n", h=4)).then_inc(S("v_ready"), 1)

            @block.scalar
            def _(act):
                for d in range(2):
                    t, c0 = tiles[d], tile_cols(tiles[d])
                    qk, gc, qT, kT = work("qk gc qT kT", d)
                    act.activation(qk[:], tokm[:, ds(t, 1), 0:512].rearrange("p a n -> p (a n)"), ACT.Copy).then_inc(S("cur_ready"), 1)
                    act.activation(gc[:], gates[:, ds(t, 1), :].rearrange("p a n -> p (a n)"), ACT.Copy).then_inc(S("cur_ready"), 1)
                    act.activation(qT[:, 2:4, :], chan[:, 14:16, ds(c0, P)], ACT.Copy).then_inc(S("cur_ready"), 1)
                    act.activation(kT[:, 2:4, :], chan[:, 16:18, ds(c0, P)], ACT.Copy).then_inc(S("cur_ready"), 1)
                for d in range(2):
                    qT, kT = work("qT kT", d)
                    act.wait_ge(S("qk_turned"), d + 1)
                    act.activation(qT[:, 0:2, :], heads(d, 2, P)[:, 0:2, :], ACT.Copy).then_inc(S("qk_ready"), 1)
                    act.activation(kT[:, 0:2, :], heads(d, 2, P)[:, 2:4, :], ACT.Copy).then_inc(S("qk_ready"), 1)
                for d in range(2):
                    Dm, sm = work("Dm sm", d)
                    act.wait_ge(S("logs_ready"), d + 1)
                    act.activation(Dm[:], Dm[:], ACT.Exp).then_inc(S("w_ready"), 1)
                    act.activation(sm[:], sm[:], ACT.Exp).then_inc(S("w_ready"), 1)
                for d in range(2):
                    act.wait_ge(S("sct_turned"), d + 1)
                    act.activation(W["SCT"][d][:], PS[:, 4 * d:4 * d + 2, :].rearrange("p b (h n) -> p (b h) n", n=P), ACT.Copy).then_inc(S("sct_ready"), 1)

            @block.vector
            def _(dve):
                ch = Chain(dve, S("dve_step"))
                for d in range(2):
                    b, c, gc, diag = work("b c gc diag", d)
                    dve.wait_ge(S("b_ready"), d + 1)
                    ch(dve.tensor_copy(b[:], PS[:, 4 * d + 1, 0:8]))
                    ch(dve.tensor_tensor(c[:], gc[:, 8 * d:8 * d + 4], b[:, 0:4], ALU.subtract))
                    dve.tensor_tensor(diag[:], bc(ident[:], 1, 4), bc(c[:], 2, P), ALU.mult).then_inc(S("diag_ready"), 1)
                for d in range(2):
                    b, c, gl, g, mn, Dm, sm = work("b c gl g mn Dm sm", d)
                    cb = heads(d, 1, P)
                    dve.wait_ge(S("cb_ready"), d + 1)
                    ch.inc(dve.tensor_reduce(gl[:], cb, AX, ALU.max))
                    ch(dve.tensor_tensor(Dm[:], cb, bc(W["negm"][:, d, :], 1, 4), ALU.add))
                    ch(dve.tensor_reduce(g[:], Dm[:], AX, ALU.max))
                    ch.inc(dve.tensor_tensor(g[:], g[:], m[:, d, :], ALU.max))
                    ch(dve.tensor_tensor(gl[:], gl[:], m[:, d, :], ALU.max))
                    ch.inc(dve.tensor_tensor(Dm[:], Dm[:], bc(g[:], 2, P), ALU.subtract))
                    ch.inc(dve.tensor_tensor(sm[:, 0, :], m[:, d, :], g[:], ALU.subtract))
                    ch.inc(dve.scalar_tensor_tensor(sm[:, 1, :], b[:, 0:4], -1.0, g[:], ALU.mult, ALU.subtract))
                    ch.inc(dve.tensor_tensor(sm[:, 2, :], c[:], gl[:], ALU.subtract))
                    ch.inc(dve.tensor_tensor(sm[:, 3, :], m[:, d, :], gl[:], ALU.subtract))
                    ch(dve.tensor_tensor(mn[:], b[:, 4:8], gl[:], ALU.add))
                    dve.tensor_copy(m[:, d, :], mn[:]).then_inc(S("logs_ready"), 1)
                for d in range(2):
                    f, sm, ku, qk, cs, SC, Dm = work("f sm ku qk cs SC Dm", d)
                    dve.wait_ge(S("w_ready"), 2 * d + 2)
                    ch.inc(dve.tensor_copy(f[:, :, 0:4], W["fret"][:, d]))
                    ch.inc(dve.tensor_copy(f[:, 0, 4:8], sm[:, 0, :]))
                    ch(dve.tensor_copy(f[:, 1:3, 4:8], sm[:, 2:4, :]))
                    ch.inc(dve.tensor_tensor(ku[:, 0:4, :], qk[:, 256:512].rearrange("p (h n) -> p h n", h=4), bc(f[:, 1, 0:4], 2, HD), ALU.mult))
                    ch.inc(dve.tensor_tensor(ku[:, 4:8, :], heads(d, 0, HD), bc(f[:, 1, 4:8], 2, HD), ALU.mult))
                    for x in range(2):
                        q = slice(64 * x, 64 * x + 64)
                        ch.inc(dve.tensor_copy(cs[q, :], f[q, 2, x:8:2]))
                    dve.wait_ge(S("s_ready"), d + 1)
                    ch.inc(dve.tensor_tensor(by_parity(SC[:, 0:4, :]), halves(d, 2, P)[:, :, 0:2, :], by_parity(W["wret"][:, d]), ALU.mult))
                    ch.inc(dve.tensor_tensor(by_parity(SC[:, 4:8, :]), halves(d, 2, P)[:, :, 2:4, :], by_parity(Dm[:]), ALU.mult))
                    ch.sync()
                    dve.engine_nop().then_inc(S("sc_ready"), 1)
                for d in range(2):
                    f, num, den, sm, cs = work("f num den sm cs", d)
                    dve.wait_ge(S("out_ready"), d + 1)
                    ws = bc(f[:, 0, :].rearrange("p (j x) -> p x j", x=2), 3, HD + 1)
                    ch(dve.tensor_tensor(by_parity(num[:]), halves(d, 2, HD + 1), ws, ALU.mult))
                    ch(dve.tensor_tensor(by_parity(num[:]), by_parity(num[:]), halves(d, 0, HD + 1), ALU.add))
                    ch(dve.scalar_tensor_tensor(den[:], num[:, 4:8, HD], -1.0, num[:, 4:8, HD], ALU.mult, ALU.max))
                    ch(dve.tensor_tensor(den[:], den[:], sm[:, 1, :], ALU.max))
                    ch(dve.reciprocal(den[:], den[:]))
                    ch.inc(dve.tensor_tensor(num[:, 4:8, 0:HD], num[:, 4:8, 0:HD], bc(den[:], 2, HD), ALU.mult))
                    ch(dve.tensor_tensor(state[:, d], state[:, d], bc(cs[:], 2, HD + 1), ALU.mult))
                    for x in range(2):
                        q = slice(64 * x, 64 * x + 64)
                        o = KV + (HD + 1) * x
                        ch.inc(dve.tensor_tensor(state[q, d], state[q, d], PS[q, 4 * d:4 * d + 4, o:o + HD + 1], ALU.add))
                    for i, o in enumerate((0, 768)):
                        yt = Y[:, ds(tiles[d], 1), o:o + 256].rearrange("p a (h n) -> p (a h) n", h=4)
                        ch.inc(dve.tensor_tensor(yt, yt, num[:, 4 * i:4 * i + 4, 0:HD], ALU.add))
                    ch.sync()

            @block.tensor
            def _(pe):
                for d in range(2):
                    gc, qk, kT = work("gc qk kT", d)
                    pe.wait_ge(S("cur_ready"), 4 * d + 4)
                    pe.matmul(PS[:, 4 * d + 1, 0:4], W["cum"][:, d, :], gc[:, 8 * d + 4:8 * d + 8], start=True, stop=True)
                    pe.matmul(PS[:, 4 * d + 1, 4:8], ones[:], gc[:, 8 * d + 4:8 * d + 8], start=True, stop=True).then_inc(S("b_ready"), 1)
                    for i in range(4):
                        pe.transpose(PS[:, 4 * d + 2, i * P:(i + 1) * P], qk[:, i * P:(i + 1) * P], ident[:])
                    for i in range(2):
                        mm = pe.transpose(PS[:, 4 * d, i * P:(i + 1) * P], kT[:, 2 + i, :], ident[:])
                    mm.then_inc(S("qk_turned"), 1)
                for d in range(2):
                    qT, kT = work("qT kT", d)
                    pe.wait_ge(S("diag_ready"), d + 1)
                    pe.matmul(PS[:, 4 * d + 1, :], ones[:], W["diag"][d][:].rearrange("p h n -> p (h n)"), start=True, stop=True).then_inc(S("cb_ready"), 1)
                    pe.wait_ge(S("qk_ready"), 2 * d + 2)
                    for h in range(8):
                        j, q = h // 2, slice(64 * (h % 2), 64 * (h % 2) + 64)
                        mm = pe.matmul(PS[:, 4 * d + 2 + h % 2, j * P:(j + 1) * P], qT[q, j, :], kT[q, j, :], start=True, stop=True)
                    mm.then_inc(S("s_ready"), 1)
                for d in range(2):
                    pe.wait_ge(S("sc_ready"), d + 1)
                    for h in range(8):
                        mm = pe.transpose(PS[:, 4 * d + h // 4, (h % 4) * P:(h % 4 + 1) * P], W["SC"][d][:, h, :], ident[:])
                    mm.then_inc(S("sct_turned"), 1)
                    for h in range(8):
                        j, q, o = h // 2, slice(64 * (h % 2), 64 * (h % 2) + 64), (h // 2) * (HD + 1)
                        pe.matmul(PS[:, 4 * d + 2 + h % 2, o:o + HD + 1], W["qT"][d][q, j, :], state[q, d, j, :], start=True, stop=True)
                for d in range(2):
                    SCT, va, ku = work("SCT va ku", d)
                    pe.wait_ge(S("sct_ready"), d + 1)
                    pe.wait_ge(S("v_ready"), 2 * d + 2)
                    for h in range(8):
                        o = (h // 2) * (HD + 1)
                        pe.matmul(PS[:, 4 * d + h % 2, o:o + HD + 1], SCT[:, h, :], va[:, h, :], start=True, stop=True)
                    for j in range(4):
                        mm = pe.matmul(PS[:, 4 * d + j, KV:KV + 2 * (HD + 1)], ku[:, 2 * j:2 * j + 2, :].rearrange("p h n -> p (h n)"),
                                       va[:, 2 * j:2 * j + 2, :].rearrange("p h n -> p (h n)"), start=True, stop=True)
                    mm.then_inc(S("out_ready"), 1)
        ph.meet()


def mix_out(nc, D, layer, B, X, grow, selc, PS, ident):
    chan, tokm, prm, Y = B["chan"], B["tokm"], B["prm"], B["Y"]
    SEMS = ("x_loaded w_loaded wo_loaded rk_step rk_ready sil_ready og_ready gb_made gbs_ready heads_ready centred squared hvar_ready hroot_ready "
            "mix_ready turned T_ready out_ready out_read var_ready root_ready norm_ready gain_done row_ready stored dve_step")
    with Phase(nc, SEMS) as ph:
        S = ph.sem
        W = {n: ph.sb("m_" + n, s) for n, s in {
            "wo": [P, KC, D_MODEL], "gup": [P, 512], "gn": [P, 2, D_MODEL], "ln": [P, 2, D_MODEL], "hsel": [P, 2],
            "gb": [P, 2, D_MODEL], "x": [P, D_MODEL], "y": [P, 2, D_MODEL], "sq": [P, D_MODEL], "T": [P, KC, P],
            "rk": [P, 4, P], "sil": [P, 256], "og": [P, 256], "bon": [P, 8],
            "mean": [P, 16], "var": [P, 2, 16], "st": [P, 2, 6], "mv": [P, 2, 4]}.items()}
        loads = [(W["gup"][:], of_layer(D["g_up"], layer)), (W["gn"][:], row_bc(D["gn"], layer)), (W["ln"][:], row_bc(D["ln1"], layer)),
                 (W["hsel"][:], D["c_hsel"])]
        x, sq = W["x"], W["sq"]
        with nc.Block() as block:
            @block.sync
            def _(sp):
                for dst, src in loads:
                    sp.dma_start(dst, src).then_inc(S("w_loaded"), 16)
                sp.dma_start(W["wo"][:], of_layer(D["w_out"], layer).rearrange("(k p) n -> p k n", p=P)).then_inc(S("wo_loaded"), 16)
                for t in range(NT):
                    if t:
                        sp.wait_ge(S("var_ready"), t)
                    sp.dma_start(x[:], X[t]).then_inc(S("x_loaded"), 16)
                    if t:
                        sp.wait_ge(S("row_ready"), t)
                        sp.dma_start(X[t - 1], W["y"][:, (t - 1) % 2, :]).then_inc(S("stored"), 16)
                sp.wait_ge(S("row_ready"), NT)
                sp.dma_start(X[NT - 1], W["y"][:, (NT - 1) % 2, :]).then_inc(S("stored"), 16)
                sp.wait_ge(S("stored"), 16 * NT)

            @block.gpsimd
            def _(pool):
                def bonus_products(t):
                    c = slice(tile_cols(t), tile_cols(t) + P)
                    if t:
                        pool.wait_ge(S("heads_ready"), t)
                    pool.tensor_tensor(W["rk"][:], chan[:, 0:4, c], chan[:, 4:8, c], ALU.mult).then_inc(S("rk_step"), 1)
                    pool.wait_ge(S("rk_step"), t + 1)
                    pool.tensor_tensor(W["rk"][:], W["rk"][:], bc(prm[:, 30:34], 2, P), ALU.mult).then_inc(S("rk_ready"), 1)

                bonus_products(0)
                for t in range(NT):
                    if t + 1 < NT:
                        bonus_products(t + 1)
                    y = W["y"][:, t % 2, :]
                    pool.wait_ge(S("norm_ready"), t + 1)
                    pool.tensor_tensor(y, y, W["ln"][:, 0, :], ALU.mult).then_inc(S("gain_done"), 1)
                    pool.wait_ge(S("gain_done"), t + 1)
                    pool.tensor_tensor(y, y, W["ln"][:, 1, :], ALU.add).then_inc(S("row_ready"), 1)

            @block.scalar
            def _(act):
                def gates(t):
                    if t:
                        act.wait_ge(S("mix_ready"), t)
                    act.activation(W["sil"][:], tokm[:, t, 768:1024], ACT.Silu).then_inc(S("sil_ready"), 1)
                    act.activation(W["og"][:], tokm[:, t, ML_O:ML_O + 256], ACT.Sigmoid).then_inc(S("og_ready"), 1)

                def first(t):
                    act.wait_ge(S("centred"), t + 1)
                    act.activation(sq[:], W["y"][:, t % 2, :], ACT.Square).then_inc(S("squared"), 1)
                    act.wait_ge(S("hvar_ready"), t + 1)
                    act.activation(W["var"][:, 0, :], W["var"][:, 0, :], ACT.Sqrt).then_inc(S("hroot_ready"), 1)
                    act.wait_ge(S("turned"), t + 1)
                    act.activation(W["T"][:], PS[:, 6:8, :].rearrange("p b (k n) -> p (b k) n", n=P), ACT.Copy).then_inc(S("T_ready"), 1)

                def second(t):
                    act.wait_ge(S("var_ready"), t + 1)
                    act.activation(W["mv"][:, t % 2, 2:3], W["mv"][:, t % 2, 2:3], ACT.Sqrt).then_inc(S("root_ready"), 1)

                for cond in range(2):
                    act.wait_ge(S("gb_made"), cond + 1)
                    act.activation(W["gb"][:, cond, :], PS[:, 4 + 2 * cond:6 + 2 * cond, :].rearrange("p b n -> p (b n)"), ACT.Copy).then_inc(S("gbs_ready"), 1)
                gates(0)
                first(0)
                for t in range(1, NT):
                    gates(t)
                    first(t)
                    second(t - 1)
                second(NT - 1)

            @block.tensor
            def _(pe):
                def heads(t):
                    c = tile_cols(t)
                    if t:
                        pe.wait_ge(S("mix_ready"), t)
                    pe.matmul(PS[:, 1, :], chan[:, 13, c:c + P], W["gup"][:], start=True, stop=True)
                    for k in range(4):
                        pe.transpose(PS[:, 2, k * P:(k + 1) * P], chan[:, 8 + k, c:c + P], ident[:])
                    pe.wait_ge(S("rk_ready"), t + 1)
                    for k in range(4):
                        mm = pe.matmul(PS[:, 3, 2 * k:2 * k + 2], W["rk"][:, k, :], W["hsel"][:], start=True, stop=True)
                    mm.then_inc(S("heads_ready"), 1)

                def turn(t):
                    pe.wait_ge(S("mix_ready"), t + 1)
                    for k in range(KC):
                        mm = pe.transpose(PS[:, 6 + k // 4, (k % 4) * P:(k % 4 + 1) * P], W["y"][:, t % 2, k * P:(k + 1) * P], ident[:])
                    mm.then_inc(S("turned"), 1)

                def project(t):
                    pe.wait_ge(S("T_ready"), t + 1)
                    if t:
                        pe.wait_ge(S("out_read"), t)
                    else:
                        pe.wait_ge(S("wo_loaded"), 16)
                    for i in range(2):
                        for k in range(KC):
                            mm = pe.matmul(PS[:, 4 + i, :], W["T"][:, k, :], W["wo"][:, k, i * 512:(i + 1) * 512], start=(k == 0), stop=(k == KC - 1))
                    mm.then_inc(S("out_ready"), 1)

                for cond in range(2):
                    for i in range(2):
                        mm = pe.matmul(PS[:, 4 + 2 * cond + i, :], selc[:, cond, :], grow[:, 0, i * 512:(i + 1) * 512], start=True, stop=True)
                    mm.then_inc(S("gb_made"), 1)
                pe.wait_ge(S("w_loaded"), 16 * len(loads))
                heads(0)
                pe.wait_ge(S("gbs_ready"), 2)
                for t in range(NT):
                    turn(t)
                    if t + 1 < NT:
                        heads(t + 1)
                    project(t)

            @block.vector
            def _(dve):
                ch = Chain(dve, S("dve_step"))
                var, mean = W["var"], W["mean"]

                def first(t):
                    y = W["y"][:, t % 2, :]
                    yt = Y[:, t, :].rearrange("p (h n) -> p h n", n=HD)
                    y3, s3 = y.rearrange("p (h n) -> p h n", n=HD), sq[:].rearrange("p (h n) -> p h n", n=HD)
                    ch(dve.tensor_reduce(mean[:], yt, AX, ALU.add))
                    ch(dve.tensor_scalar(mean[:], mean[:], 1.0 / HD, None, ALU.mult))
                    if t >= 2:
                        dve.wait_ge(S("stored"), 16 * (t - 1))
                    dve.tensor_tensor(y3, yt, bc(mean[:], 2, HD), ALU.subtract).then_inc(S("centred"), 1)
                    dve.wait_ge(S("squared"), t + 1)
                    ch(dve.tensor_reduce(var[:, 0, :], s3, AX, ALU.add))
                    dve.tensor_scalar(var[:, 0, :], var[:, 0, :], 1.0 / HD, EPS, ALU.mult, ALU.add).then_inc(S("hvar_ready"), 1)
                    dve.wait_ge(S("hroot_ready"), t + 1)
                    ch(dve.reciprocal(var[:, 1, :], var[:, 0, :]))
                    ch(dve.tensor_tensor(y3, y3, bc(var[:, 1, :], 2, HD), ALU.mult))
                    ch(dve.tensor_tensor(y, y, W["gn"][:, 0, :], ALU.mult))
                    ch(dve.tensor_tensor(y, y, W["gn"][:, 1, :], ALU.add))
                    dve.wait_ge(S("sil_ready"), t + 1)
                    dve.wait_ge(S("og_ready"), t + 1)
                    ch.inc(dve.tensor_tensor(y[:, 0:256], y[:, 0:256], W["sil"][:], ALU.mult))
                    ch.inc(dve.tensor_tensor(y[:, 768:1024], y[:, 768:1024], W["og"][:], ALU.mult))
                    dve.wait_ge(S("heads_ready"), t + 1)
                    ch(dve.tensor_copy(W["bon"][:], PS[:, 3, 0:8]))
                    ch(dve.tensor_tensor(s3[:, 0:8, :], PS[:, 2, :].rearrange("p (h n) -> p h n", n=HD), bc(W["bon"][:], 2, HD), ALU.mult))
                    ch(dve.tensor_tensor(y[:, 256:768], y[:, 256:768], sq[:, 0:512], ALU.add))
                    dve.tensor_tensor(y[:, 256:768], y[:, 256:768], PS[:, 1, :], ALU.mult).then_inc(S("mix_ready"), 1)

                def second(t):
                    y, mv = W["y"][:, t % 2, :], W["mv"][:, t % 2]
                    dve.wait_ge(S("out_ready"), t + 1)
                    if t == 0:
                        dve.wait_ge(S("gbs_ready"), 2)
                    dve.tensor_tensor(y, PS[:, 4:6, :].rearrange("p b n -> p (b n)"), W["gb"][:, min(t, 1), :], ALU.mult).then_inc(S("out_read"), 1)
                    dve.wait_ge(S("out_read"), t + 1)
                    dve.wait_ge(S("x_loaded"), 16 * t + 16)
                    ch(dve.scalar_tensor_tensor(y, x[:], ALPHA, y, ALU.mult, ALU.add))
                    norm_rows(dve, S, ch, y, W["st"], mv, t)

                dve.wait_ge(S("w_loaded"), 16 * len(loads))
                first(0)
                for t in range(1, NT):
                    first(t)
                    second(t - 1)
                second(NT - 1)
        ph.meet()


def norm_rows(dve, S, ch, y, st, mv, t):
    ch.inc(dve.bn_stats(st[:, 0, :], y[:, 0:512]))
    ch.inc(dve.bn_stats(st[:, 1, :], y[:, 512:1024]))
    ch.sync()
    ch(dve.bn_aggr(mv[:, 0:2], st[:, :, :]))
    dve.tensor_scalar(mv[:, 2:3], mv[:, 1:2], EPS, None, ALU.add).then_inc(S("var_ready"), 1)
    dve.wait_ge(S("root_ready"), t + 1)
    ch(dve.reciprocal(mv[:, 3:4], mv[:, 2:3]))
    dve.tensor_scalar(y, y, mv[:, 0:1], mv[:, 3:4], ALU.subtract, ALU.mult).then_inc(S("norm_ready"), 1)


def route(nc, D, layer, hh, hl, PS, ident):
    with ExitStack() as ctx:
        def sb(name, shape, dt=F32):
            return tile(nc, ctx, name, shape, dt)

        slots = sb("slots", [P, 3, TOK])
        iota = sb("iota", [P, P])
        with ExitStack() as c2:
            scores = c2.enter_context(nc.sbuf_tensor("scores", [P, NT, 16, P], F32))
            queries(nc, D, layer, hh, hl, scores, iota, PS)
            with Phase(nc, "cur_ready cur_used e_ready exp_ready slots_ready turned done dve_step") as ph:
                bufs = {n: ph.sb("k_" + n, s, dt) for n, s, dt in (
                    ("s", [P, 16, P], F32), ("s2", [P, 16, P], F32), ("v", [P, 16, TOPK], F32), ("i", [P, 16, TOPK], U32), ("if", [P, 16, TOPK], F32),
                    ("cand", [P, 8, 256], F32), ("cand2", [P, 8, 256], F32), ("tv", [P, 8, TOPK], F32), ("ti", [P, 8, TOPK], U32), ("hi", [P, 8, TOPK], U32),
                    ("lo", [P, 8, TOPK], U32), ("hl", [P, 2, 8, TOPK], F32), ("one", [P, P, TOPK], F32), ("sl", [P, 3, P], F32), ("sum", [P, 8], F32), ("mark", [P, 1], F32))}
                top_pairs(nc, ph, bufs, scores, slots, iota, PS, ident)
        spread(nc, D, slots, iota, PS)


def queries(nc, D, layer, hh, hl, scores, iota, PS):
    with Phase(nc, "k_loaded wa_loaded wb_loaded hi_ready split acc_ready q_ready s_ready s_read") as ph:
        S = ph.sem
        wt = ph.sb("wt", [P, 2, KC, P])
        wh, wl = ph.sb("wqh", [P, 2, KC, P], F32R), ph.sb("wql", [P, 2, KC, P], F32R)
        keys = ph.sb("keys", [P, 16, P])
        qT = ph.sb("pqT", [P, 2, TOK])
        WL = ["wa_loaded", "wb_loaded"]
        with nc.Block() as block:
            @block.sync
            def _(sp):
                sp.dma_start(keys[:], of_layer(D["keys"], layer)).then_inc(S("k_loaded"), 16)
                sp.dma_start(iota[:], D["c_iota"]).then_inc(S("k_loaded"), 16)
                with sp.Fori(0, 8) as i:
                    for b in range(2):
                        sp.wait_ge(S("split"), i * 2 + b + 1)
                        sp.dma_start(wt[:, b], of_layer(of_layer(D["wq"], layer), i * 2 + b)).then_inc(S(WL[b]), 16)

            @block.tensor
            def _(pe):
                pe.sem_inc(S("acc_ready"), 2)
                pe.sem_inc(S("s_ready"), 2)
                pe.wait_ge(S("k_loaded"), 32)

                def queries_of(i, b):
                    pe.wait_ge(S("split"), i * 2 + b + 3)
                    pe.wait_ge(S("q_ready"), i * 4 + 2 * b + 2)
                    n = 0
                    for k in range(KC):
                        for w, x in ((wh, hh), (wh, hl), (wl, hh)):
                            for z in range(2):
                                mm = pe.matmul(PS[:, 2 * b + z, 0:HT], w[:, b, k, :], x[:, k, z * HT:(z + 1) * HT],
                                               start=(n == 0), stop=(n == 3 * KC - 1))
                            n += 1
                    mm.then_inc(S("acc_ready"), 1)

                def scores_of(i, b):
                    pe.wait_ge(S("q_ready"), i * 4 + 2 * b + 6)
                    pe.wait_ge(S("s_read"), i * 4 + 2 * b + 2)
                    for t in range(NT):
                        mm = pe.matmul(PS[:, 4 + 2 * b + t // 4, (t % 4) * P:(t % 4 + 1) * P], qT[:, b, t * P:(t + 1) * P],
                                       keys[:, ds(i * 2 + b, 1), :].rearrange("p a n -> p (a n)"), start=True, stop=True)
                    mm.then_inc(S("s_ready"), 1)

                queries_of(0, 0)
                with pe.Fori(0, 7) as i:
                    queries_of(i, 1)
                    scores_of(i, 0)
                    queries_of(i + 1, 0)
                    scores_of(i, 1)
                queries_of(7, 1)
                scores_of(7, 0)
                scores_of(7, 1)

            @block.gpsimd
            def _(pool):
                pool.sem_inc(S("split"), 2)
                with pool.Fori(0, 8) as i:
                    for b in range(2):
                        pool.wait_ge(S("hi_ready"), i * 2 + b + 1)
                        pool.tensor_tensor(wl[:, b], wt[:, b], wh[:, b].bitcast(F32), ALU.subtract).then_inc(S("split"), 1)

            @block.scalar
            def _(act):
                with act.Fori(0, 8) as i:
                    for b in range(2):
                        act.wait_ge(S(WL[b]), i * 16 + 16)
                        act.wait_ge(S("acc_ready"), i * 2 + b + 1)
                        act.activation(wh[:, b], wt[:, b], ACT.Copy).then_inc(S("hi_ready"), 1)

            @block.vector
            def _(dve):
                dve.sem_inc(S("q_ready"), 4)
                dve.sem_inc(S("s_read"), 4)

                def evacuate(i, b):
                    dve.wait_ge(S("acc_ready"), i * 2 + b + 3)
                    dve.wait_ge(S("s_ready"), i * 2 + b + 1)
                    for z in range(2):
                        dve.tensor_copy(qT[:, b, z * HT:(z + 1) * HT], PS[:, 2 * b + z, 0:HT]).then_inc(S("q_ready"), 1)

                def keep(i, b):
                    dve.wait_ge(S("s_ready"), i * 2 + b + 3)
                    dst = scores[:, :, ds(i * 2 + b, 1), :].rearrange("p t a n -> p t (a n)")
                    dve.tensor_copy(dst[:, 0:4, :], PS[:, 4 + 2 * b, :].rearrange("p (t n) -> p t n", t=4)).then_inc(S("s_read"), 1)
                    dve.tensor_copy(dst[:, 4, :], PS[:, 5 + 2 * b, 0:P]).then_inc(S("s_read"), 1)

                evacuate(0, 0)
                with dve.Fori(0, 7) as i:
                    evacuate(i, 1)
                    keep(i, 0)
                    evacuate(i + 1, 0)
                    keep(i, 1)
                evacuate(7, 1)
                keep(7, 0)
                keep(7, 1)
                dve.wait_ge(S("s_read"), 4 + 32)
        ph.meet()


def top_pairs(nc, ph, K, scores, slots, iota, PS, ident):
    S = ph.sem
    NEG = -3.0e38
    TOP_STEPS = 135
    with nc.Block() as block:
        @block.scalar
        def _(act):
            def load(t):
                act.activation(K["s"][:], scores[:, ds(t, 1), :, :].rearrange("p a g n -> p (a g) n"), ACT.Copy).then_inc(S("cur_ready"), 1)

            def finish(t):
                act.wait_ge(S("e_ready"), t + 1)
                act.activation(K["tv"][:], K["tv"][:], ACT.Exp).then_inc(S("exp_ready"), 1)
                act.wait_ge(S("turned"), t + 2)
                act.activation(slots[:, :, ds(t * P, P)], PS[:, 0, 0:3 * P].rearrange("p (a n) -> p a n", a=3), ACT.Copy).then_inc(S("done"), 1)

            load(0)
            with act.Fori(0, NT - 1) as t:
                act.wait_ge(S("cur_used"), t + 1)
                load(t + 1)
                finish(t)
            finish(NT - 1)
            act.wait_ge(S("done"), NT + 1)

        @block.vector
        def _(dve):
            dve.sem_inc(S("turned"), 1)

            def settle():
                dve.tensor_copy(K["mark"][:], iota[:, 0:1])

            def top16(ch, src, work, val, idx, n):
                settle()
                for g in range(n):
                    ch.inc(dve.max(val[:, g, 0:8], src[:, g, :]))
                ch.sync()
                settle()
                for g in range(n):
                    ch.inc(dve.max_index(idx[:, g, 0:8], val[:, g, 0:8], src[:, g, :]))
                for g in range(n):
                    ch.inc(dve.match_replace(work[:, g, :], val[:, g, 0:8], src[:, g, :], NEG))
                ch.sync()
                settle()
                for g in range(n):
                    ch.inc(dve.max(val[:, g, 8:16], work[:, g, :]))
                ch.sync()
                settle()
                for g in range(n):
                    ch.inc(dve.max_index(idx[:, g, 8:16], val[:, g, 8:16], work[:, g, :]))
                ch.sync()

            with dve.Fori(0, NT) as t:
                ch = Chain(dve, S("dve_step"), t * TOP_STEPS)
                dve.wait_ge(S("cur_ready"), t + 1)
                top16(ch, K["s"], K["s2"], K["v"], K["i"], 16)
                dve.sem_inc(S("cur_used"), 1)
                ch.inc(dve.tensor_copy(K["if"][:], K["i"][:]))
                v2 = K["v"][:].rearrange("p (h x) k -> p h x k", x=2)
                ch(dve.tensor_tensor(K["cand"][:].rearrange("p h (i j) -> p h i j", i=TOPK),
                                     bc(v2[:, :, 0, :], 3, TOPK), bc(v2[:, :, 1, :], 2, TOPK), ALU.add))
                top16(ch, K["cand"], K["cand2"], K["tv"], K["ti"], 8)
                ch.inc(dve.tensor_copy(K["sum"][:], K["tv"][:, :, 0]))
                ch.inc(dve.tensor_scalar(K["hi"][:], K["ti"][:], 4, None, ALU.logical_shift_right))
                ch(dve.tensor_scalar(K["lo"][:], K["ti"][:], 15, None, ALU.bitwise_and))
                dve.tensor_tensor(K["tv"][:], K["tv"][:], bc(K["sum"][:], 2, TOPK), ALU.subtract).then_inc(S("e_ready"), 1)
                ch.inc(dve.tensor_copy(K["hl"][:, 0], K["hi"][:]))
                ch(dve.tensor_copy(K["hl"][:, 1], K["lo"][:]))
                i2 = K["if"][:].rearrange("p (h x) k -> p h x k", x=2)
                one4 = K["one"][:].rearrange("p (h k) r -> p h k r", h=8)
                dve.wait_ge(S("turned"), t + 1)
                for x in range(2):
                    ch(dve.tensor_tensor(K["one"][:], bc(K["hl"][:, x].rearrange("p h k -> p (h k)"), 2, TOPK), bc(iota[:, 0:TOPK], 1, P), ALU.is_equal))
                    ch(dve.tensor_tensor(one4, one4, bc(i2[:, :, x, :], 2, TOPK), ALU.mult))
                    ch(dve.tensor_reduce(K["sl"][:, x, :], K["one"][:], AX, ALU.add))
                dve.wait_ge(S("exp_ready"), t + 1)
                ch(dve.tensor_reduce(K["sum"][:], K["tv"][:], AX, ALU.add))
                ch(dve.reciprocal(K["sum"][:], K["sum"][:]))
                dve.tensor_tensor(K["sl"][:, 2, :].rearrange("p (h k) -> p h k", h=8), K["tv"][:], bc(K["sum"][:], 2, TOPK), ALU.mult).then_inc(S("slots_ready"), 1)
                if ch.n != TOP_STEPS:
                    raise ValueError(f"TOP_STEPS is {ch.n}")

        @block.tensor
        def _(pe):
            pe.sem_inc(S("done"), 1)
            with pe.Fori(0, NT) as t:
                pe.wait_ge(S("slots_ready"), t + 1)
                pe.wait_ge(S("done"), t + 1)
                for i in range(3):
                    mm = pe.transpose(PS[:, 0, i * P:(i + 1) * P], K["sl"][:, i, :], ident[:])
                mm.then_inc(S("turned"), 1)
    ph.meet()


def spread(nc, D, slots, iota, PS):
    OCT = 8
    SLOTS = 4
    SETS = NB // OCT
    QB = NB // 4
    with Phase(nc, "cur_ready eq_ready a_ready b_ready w_ready w_read s0_stored s1_stored") as ph:
        S = ph.sem
        cur = ph.sb("cur", [P, 2, 3, NB])
        A, Bh = ph.sb("A", [P, SLOTS, OCT, P]), ph.sb("Bh", [P, SLOTS, OCT, P])
        Wt = ph.sb("Wt", [P, 2, P, NB])
        with nc.Block() as block:
            @block.scalar
            def _(act):
                for b in range(2):
                    act.sem_inc(S(f"s{b}_stored"), 16)

                def load(n, b):
                    act.activation(cur[:, b], slots[:, :, ds(n * NB, NB)], ACT.Copy).then_inc(S("cur_ready"), 1)

                def evacuate(i, b):
                    act.wait_ge(S(f"s{b}_stored"), i * 16 + 16)
                    for q in range(QB):
                        act.wait_ge(S("w_ready"), i * 2 * QB + b * QB + q + 2 * SLOTS + 1)
                        act.activation(Wt[:, b, :, 4 * q:4 * q + 4], PS[:, q % 8, :].rearrange("p (t e) -> p e t", t=4), ACT.Copy).then_inc(S("w_read"), 1)

                load(0, 0)
                with act.Fori(0, NBATCH // 2 - 1) as i:
                    load(i * 2 + 1, 1)
                    evacuate(i, 0)
                    load(i * 2 + 2, 0)
                    evacuate(i, 1)
                load(NBATCH - 1, 1)
                evacuate(NBATCH // 2 - 1, 0)
                evacuate(NBATCH // 2 - 1, 1)

            @block.vector
            def _(dve):
                dve.sem_inc(S("w_ready"), 2 * SLOTS)
                with dve.Fori(0, NBATCH // 2) as i:
                    for b in range(2):
                        dve.wait_ge(S("cur_ready"), i * 2 + b + 1)
                        for n in range(SETS):
                            s = (b * SETS + n) % SLOTS
                            rows = slice(n * OCT, (n + 1) * OCT)
                            dve.wait_ge(S("w_ready"), i * 2 * QB + b * QB + 2 * n + 2)
                            dve.tensor_tensor(A[:, s], bc(cur[:, b, 0, rows], 2, P), bc(iota[:], 1, OCT), ALU.is_equal).then_inc(S("eq_ready"), 1)
                            dve.tensor_tensor(Bh[:, s], bc(cur[:, b, 1, rows], 2, P), bc(iota[:], 1, OCT), ALU.is_equal).then_inc(S("b_ready"), 1)

            @block.gpsimd
            def _(pool):
                with pool.Fori(0, NBATCH // 2) as i:
                    for b in range(2):
                        for n in range(SETS):
                            s = (b * SETS + n) % SLOTS
                            pool.wait_ge(S("eq_ready"), i * 2 * SETS + b * SETS + n + 1)
                            pool.tensor_tensor(A[:, s], A[:, s], bc(cur[:, b, 2, n * OCT:(n + 1) * OCT], 2, P), ALU.mult).then_inc(S("a_ready"), 1)

            @block.tensor
            def _(pe):
                pe.sem_inc(S("w_read"), 8)
                with pe.Fori(0, NBATCH // 2) as i:
                    for b in range(2):
                        for n in range(SETS):
                            s = (b * SETS + n) % SLOTS
                            pe.wait_ge(S("a_ready"), i * 2 * SETS + b * SETS + n + 1)
                            pe.wait_ge(S("b_ready"), i * 2 * SETS + b * SETS + n + 1)
                            for q in range(OCT // 4):
                                bank = (n * OCT // 4 + q) % 8
                                pe.wait_ge(S("w_read"), i * 2 * QB + b * QB + n * OCT // 4 + q + 1)
                                for t in range(4):
                                    mm = pe.matmul(PS[:, bank, t * P:(t + 1) * P], A[:, s, q * 4 + t, :], Bh[:, s, q * 4 + t, :], start=True, stop=True)
                                mm.then_inc(S("w_ready"), 1)

            @block.sync
            def _(sp):
                with sp.Fori(0, NBATCH // 2) as i:
                    for b in range(2):
                        sp.wait_ge(S("w_read"), i * 2 * QB + (b + 1) * QB + 8)
                        sp.dma_start(of_layer(D["wts"], i * 2 + b), Wt[:, b]).then_inc(S(f"s{b}_stored"), 16)
                for b in range(2):
                    sp.wait_ge(S(f"s{b}_stored"), 16 * (NBATCH // 2) + 16)
        ph.meet()


def split_rows(nc, src, hi, lo, PS):
    with Phase(nc, "hi_ready lo_ready") as ph:
        with nc.Block() as block:
            @block.scalar
            def _(act):
                for k in range(KC):
                    act.activation(hi[:, k, :], src[:, k, :], ACT.Copy).then_inc(ph.sem("hi_ready"), 1)

            @block.vector
            def _(dve):
                for k in range(KC):
                    dve.wait_ge(ph.sem("hi_ready"), k + 1)
                    dve.tensor_tensor(lo[:, k, :], src[:, k, :], hi[:, k, :].bitcast(F32), ALU.subtract).then_inc(ph.sem("lo_ready"), 1)
                dve.wait_ge(ph.sem("lo_ready"), KC)
        ph.meet()


def experts(nc, D, layer, hh, hl, ffn, PS):
    SEMS = ("u0_loaded u1_loaded v0_loaded v1_loaded g_loaded uhi_ready u_split vhi_ready v_split h_ready gelu_ready "
            "wf_ready whi_ready w_split o_ready o_read")
    with Phase(nc, SEMS) as ph:
        S = ph.sem
        u = ph.sb("u", [P, 2, KC * P])
        uh, ul = ph.sb("uh", [P, 2, KC, P], F32R), ph.sb("ul", [P, 2, KC, P], F32R)
        v = ph.sb("v", [P, 2, D_MODEL])
        vh, vl = ph.sb("vh", [P, GRP, D_MODEL], F32R), ph.sb("vl", [P, GRP, D_MODEL], F32R)
        g = ph.sb("g", [P, NBATCH, GRP, NB])
        ge, wf = ph.sb("ge", [P, 2, TOK]), ph.sb("wf", [P, 2, TOK])
        wh, wl = ph.sb("wh", [P, GRP, TOK], F32R), ph.sb("wl", [P, GRP, TOK], F32R)
        ut, pv, wts = of_layer(D["ut"], layer), of_layer(D["pv"], layer), D["wts"]
        OT = 2 * NT

        with nc.Block() as block:
            @block.sync
            def _(sp):
                with sp.Fori(0, NGRP) as i:
                    for e in range(GRP):
                        sp.wait_ge(S("u_split"), i * GRP + e + 1)
                        sp.dma_start(u[:, e % 2, :], of_layer(ut, i)[:, e, :]).then_inc(S(f"u{e % 2}_loaded"), 16)
                        sp.wait_ge(S("v_split"), i * GRP + e + 1)
                        sp.dma_start(v[:, e % 2, :], pv[:, ds(i * GRP + e, 1), :].rearrange("p a n -> p (a n)")).then_inc(S(f"v{e % 2}_loaded"), 16)
                        if e == 0:
                            sp.wait_ge(S("wf_ready"), i * GRP + 2)
                            sp.dma_start(g[:], wts[:, :, ds(i * GRP, GRP), :].rearrange("n p e t -> p n e t")).then_inc(S("g_loaded"), 16)

            @block.tensor
            def _(pe):
                def hidden(i, e):
                    pe.wait_ge(S("u_split"), i * GRP + e + 3)
                    pe.wait_ge(S("gelu_ready"), i * GRP + e + 1)
                    b, n = e % 2, 0
                    for k in range(KC):
                        for wt, x in ((uh, hh), (uh, hl), (ul, hh)):
                            for z in range(2):
                                mm = pe.matmul(PS[:, 2 * b + z, 0:HT], wt[:, b, k, :], x[:, k, z * HT:(z + 1) * HT],
                                               start=(n == 0), stop=(n == 3 * KC - 1))
                            n += 1
                    mm.then_inc(S("h_ready"), 1)

                def outputs(i):
                    pe.wait_ge(S("w_split"), i * GRP + GRP + 2)
                    pe.wait_ge(S("v_split"), i * GRP + GRP + 2)
                    for o in range(OT):
                        pe.wait_ge(S("o_read"), i * OT + 1 + (o - 3 if o >= 4 else 0))
                        n, cols = 0, slice((o % 2) * 512, (o % 2 + 1) * 512)
                        for e in range(GRP):
                            toks = slice((o // 2) * P, (o // 2 + 1) * P)
                            for wt, x in ((wh, vh), (wh, vl), (wl, vh)):
                                mm = pe.matmul(PS[:, 4 + o % 4, :], wt[:, e, toks], x[:, e, cols], start=(n == 0), stop=(n == 3 * GRP - 1))
                                n += 1
                        mm.then_inc(S("o_ready"), 1)

                hidden(0, 0)
                with pe.Fori(0, NGRP - 1) as i:
                    for e in range(1, GRP):
                        hidden(i, e)
                    hidden(i + 1, 0)
                    outputs(i)
                for e in range(1, GRP):
                    hidden(NGRP - 1, e)
                outputs(NGRP - 1)

            @block.scalar
            def _(act):
                def u_hi(i, e):
                    act.wait_ge(S(f"u{e % 2}_loaded"), i * 32 + 16 * (e // 2) + 16)
                    act.wait_ge(S("h_ready"), i * GRP + e + 1)
                    act.activation(uh[:, e % 2].rearrange("p k n -> p (k n)"), u[:, e % 2, :], ACT.Copy).then_inc(S("uhi_ready"), 1)

                def step(i, e, last=False):
                    if not last:
                        u_hi(i + (e + 1) // GRP, (e + 1) % GRP)
                    act.wait_ge(S("h_ready"), i * GRP + e + 3)
                    act.wait_ge(S("wf_ready"), i * GRP + e + 1)
                    b = e % 2
                    act.activation(ge[:, b, :].rearrange("p (z n) -> p z n", z=2), PS[:, 2 * b:2 * b + 2, 0:HT], ACT.Gelu).then_inc(S("gelu_ready"), 1)
                    act.wait_ge(S(f"v{b}_loaded"), i * 32 + 16 * (e // 2) + 16)
                    act.wait_ge(S("o_ready"), i * OT + 1)
                    act.activation(vh[:, e, :], v[:, b, :], ACT.Copy).then_inc(S("vhi_ready"), 1)
                    act.wait_ge(S("wf_ready"), i * GRP + e + 3)
                    act.activation(wh[:, e, :], wf[:, b, :], ACT.Copy).then_inc(S("whi_ready"), 1)

                act.sem_inc(S("gelu_ready"), 2)
                u_hi(0, 0)
                step(0, 0)
                with act.Fori(0, NGRP - 1) as i:
                    for e in range(1, GRP):
                        step(i, e)
                    step(i + 1, 0)
                for e in range(1, GRP):
                    step(NGRP - 1, e, last=(e == GRP - 1))

            @block.gpsimd
            def _(pool):
                pool.memset(ffn[:], 0.0).then_inc(S("o_read"), 1)
                pool.sem_inc(S("h_ready"), 2)
                pool.sem_inc(S("o_ready"), 1)

            @block.vector
            def _(dve):
                def u_lo(i, e):
                    dve.wait_ge(S("uhi_ready"), i * GRP + e + 1)
                    b = e % 2
                    dve.tensor_tensor(ul[:, b].rearrange("p k n -> p (k n)"), u[:, b, :], uh[:, b].rearrange("p k n -> p (k n)").bitcast(F32),
                                      ALU.subtract).then_inc(S("u_split"), 1)

                def add_outputs(i):
                    dve.wait_ge(S("o_read"), i * OT + 1)
                    for o in range(OT):
                        dve.wait_ge(S("o_ready"), i * OT + o + 2)
                        acc = ffn[:, o // 2, (o % 2) * 512:(o % 2 + 1) * 512]
                        dve.tensor_tensor(acc, acc, PS[:, 4 + o % 4, :], ALU.add).then_inc(S("o_read"), 1)

                def step(i, e, last=False):
                    b = e % 2
                    if not last:
                        u_lo(i + (e + 1) // GRP, (e + 1) % GRP)
                    if e == 0 and not isinstance(i, int):
                        add_outputs(i - 1)
                    dve.wait_ge(S("gelu_ready"), i * GRP + e + 3)
                    dve.wait_ge(S("g_loaded"), i * 16 + 16)
                    dve.wait_ge(S("w_split"), i * GRP + e + 1)
                    dve.tensor_tensor(wf[:, b, :].rearrange("p (n t) -> p n t", t=NB), ge[:, b, :].rearrange("p (n t) -> p n t", t=NB),
                                      g[:, :, e, :], ALU.mult).then_inc(S("wf_ready"), 1)
                    dve.wait_ge(S("vhi_ready"), i * GRP + e + 1)
                    dve.tensor_tensor(vl[:, e, :], v[:, b, :], vh[:, e, :].bitcast(F32), ALU.subtract).then_inc(S("v_split"), 1)
                    dve.wait_ge(S("whi_ready"), i * GRP + e + 1)
                    dve.tensor_tensor(wl[:, e, :], wf[:, b, :], wh[:, e, :].bitcast(F32), ALU.subtract).then_inc(S("w_split"), 1)

                for name in ("u_split", "v_split", "wf_ready", "w_split"):
                    dve.sem_inc(S(name), 2)
                u_lo(0, 0)
                step(0, 0)
                with dve.Fori(0, NGRP - 1) as i:
                    for e in range(1, GRP):
                        step(i, e)
                    step(i + 1, 0)
                for e in range(1, GRP):
                    step(NGRP - 1, e, last=(e == GRP - 1))
                add_outputs(NGRP - 1)
                dve.wait_ge(S("o_read"), NGRP * OT + 1)
        ph.meet()


def finish(nc, D, layer, ffn, X, grow, selc, PS):
    with Phase(nc, "x_loaded w_loaded gb_made gbs_ready scaled var_ready root_ready norm_ready gain_done row_ready stored dve_step") as ph:
        S = ph.sem
        W = {n: ph.sb("f_" + n, s) for n, s in {"x": [P, NT, D_MODEL], "ln": [P, 2, D_MODEL], "st": [P, 2, 6], "mv": [P, NT, 4],
                                                 "gb": [P, 2, D_MODEL]}.items()}
        with nc.Block() as block:
            @block.sync
            def _(sp):
                for t in range(NT):
                    sp.dma_start(W["x"][:, t, :], X[t]).then_inc(S("x_loaded"), 16)
                sp.dma_start(W["ln"][:], row_bc(D["ln2"], layer)).then_inc(S("w_loaded"), 16)
                for t in range(NT):
                    sp.wait_ge(S("row_ready"), t + 1)
                    sp.dma_start(X[t], ffn[:, t, :]).then_inc(S("stored"), 16)
                sp.wait_ge(S("stored"), 16 * NT)

            @block.tensor
            def _(pe):
                for cond in range(2):
                    for i in range(2):
                        mm = pe.matmul(PS[:, 2 * cond + i, :], selc[:, cond, :], grow[:, 1, i * 512:(i + 1) * 512], start=True, stop=True)
                    mm.then_inc(S("gb_made"), 1)

            @block.scalar
            def _(act):
                for cond in range(2):
                    act.wait_ge(S("gb_made"), cond + 1)
                    act.activation(W["gb"][:, cond, :], PS[:, 2 * cond:2 * cond + 2, :].rearrange("p b n -> p (b n)"), ACT.Copy).then_inc(S("gbs_ready"), 1)
                for t in range(NT):
                    act.wait_ge(S("var_ready"), t + 1)
                    act.activation(W["mv"][:, t, 2:3], W["mv"][:, t, 2:3], ACT.Sqrt).then_inc(S("root_ready"), 1)

            @block.gpsimd
            def _(pool):
                for t in range(NT):
                    pool.wait_ge(S("gbs_ready"), min(t, 1) + 1)
                    pool.tensor_tensor(ffn[:, t, :], ffn[:, t, :], W["gb"][:, min(t, 1), :], ALU.mult).then_inc(S("scaled"), 1)
                pool.wait_ge(S("w_loaded"), 16)
                for t in range(NT):
                    pool.wait_ge(S("norm_ready"), t + 1)
                    pool.tensor_tensor(ffn[:, t, :], ffn[:, t, :], W["ln"][:, 0, :], ALU.mult).then_inc(S("gain_done"), 1)
                    pool.wait_ge(S("gain_done"), t + 1)
                    pool.tensor_tensor(ffn[:, t, :], ffn[:, t, :], W["ln"][:, 1, :], ALU.add).then_inc(S("row_ready"), 1)

            @block.vector
            def _(dve):
                ch = Chain(dve, S("dve_step"))
                dve.wait_ge(S("x_loaded"), 16 * NT)
                for t in range(NT):
                    dve.wait_ge(S("scaled"), t + 1)
                    ch(dve.scalar_tensor_tensor(ffn[:, t, :], W["x"][:, t, :], ALPHA, ffn[:, t, :], ALU.mult, ALU.add))
                    norm_rows(dve, S, ch, ffn[:, t, :], W["st"], W["mv"][:, t], t)
        ph.meet()


def constants(np):
    i = np.arange(P)
    s, t = i[:, None], i[None, :]
    C = {"c_ident": np.eye(P), "c_ones": np.ones((P, P)), "c_iota": np.tile(i, (P, 1))}
    C["c_selc"] = np.stack([np.stack([np.full(P, float(r == c)) for c in range(2)]) for r in range(2)])
    C["c_blk"] = (s // HD == t // HD)
    C["c_hsel"] = (s // HD == np.arange(2)[None, :])
    r = np.exp(-0.5)
    mid = [(i < HD).astype(float), (i >= HD).astype(float)]
    inc = [(s <= t).astype(float), (s >= t).astype(float)]
    exc = [(s < t).astype(float), (s > t).astype(float)]
    C["c_tri"] = np.stack([-r * np.concatenate([inc[d] - mid[d][:, None], exc[d] - mid[d][:, None], mid[d][:, None]], 1) for d in range(2)], 1)
    C["c_strict"] = np.stack(exc, 1)
    C["c_incl"] = np.stack(inc, 1)
    C["c_strictT"] = np.stack([e.T for e in exc], 1)
    same = [(s // n == t // n).astype(float) for n in (16, 32, 64, 128)]
    C["c_near"] = np.stack([e * same[0] for e in exc], 1)
    C["c_lvl"] = np.stack([same[0]] + [same[k] - same[k - 1] for k in (1, 2, 3)], 1)
    C["c_cum"] = np.stack(inc, 1)
    C["c_negm"] = np.stack([(1 - e.T) * -1e30 for e in inc], 1)
    C["c_dist"] = np.stack([np.maximum(s - t, 0), np.maximum(t - s, 0)], 1)
    C["c_pos"] = np.stack([np.stack([i + 1, P - 1 - i, np.full(P, P)], 1), np.stack([P - i, i, np.full(P, P)], 1)], 1)
    nf = HD // 4
    inv = np.float32(10000.0) ** (-np.arange(nf, dtype=np.float32) / np.float32(nf))
    pos = np.arange(LAT, dtype=np.float32)
    ang = np.concatenate([(pos // 64)[:, None] * inv, (pos % 64)[:, None] * inv], -1).astype(np.float32)
    C["c_cos"] = np.cos(ang).reshape(NT - 1, P, 32).transpose(1, 0, 2)
    C["c_sin"] = np.sin(ang).reshape(NT - 1, P, 32).transpose(1, 0, 2)
    return {n: np.ascontiguousarray(a, dtype=np.float32) for n, a in C.items()}


def layouts(np, I):
    L = DEPTH

    def cols(a, n):
        return a.reshape(L, n, P).transpose(0, 2, 1)

    A = {}
    A["x"] = np.concatenate([I["x_prompt"].reshape(1, P, D_MODEL), I["x_sample"].reshape(NT - 1, P, D_MODEL)])
    A["cond"] = np.stack([I["c_ctx"].reshape(KC, P), I["c"].reshape(KC, P)], -1).transpose(1, 0, 2)
    A["b_mod"] = np.stack([I["b_mod"], I["b_mod"]], 1)
    A["w_mod"] = I["w_mod"]
    w = I["w_in"].reshape(L, KC, P, -1)
    ch = np.concatenate([w[..., 1024:2816], w[..., 2816:3328]], -1).reshape(L, KC, P, CT, P)
    A["w_ch"] = ch.transpose(0, 3, 2, 1, 4)
    A["w_tm"] = np.concatenate([w[..., 0:1024], w[..., 3328:3856]], -1).transpose(0, 2, 1, 3)
    A["prm"] = np.concatenate([
        cols(I["rwkv_mu"], 14), I["rwkv_a0"].reshape(L, 2, 4, P).transpose(0, 3, 1, 2).reshape(L, P, 8),
        cols(I["rwkv_kk"], 4), cols(I["rwkv_ka"], 4), cols(I["rwkv_rk"], 4),
        I["mlstm_conv"].reshape(L, 3, 4, P).transpose(0, 3, 2, 1).reshape(L, P, 12)], -1)
    A["gbias"] = np.repeat(I["mlstm_gate_bias"].reshape(L, 1, 16), P, 1)
    A["lora"] = np.concatenate([I["rwkv_w_up"], I["rwkv_a_up"]], 2).transpose(0, 2, 1, 3)
    A["w0"] = I["rwkv_w0"].reshape(L, 1, 2, 512)
    A["s_rwkv"] = I["state_rwkv"][0].reshape(L, 2, 4, 2, HD, HD).transpose(0, 3, 5, 1, 2, 4).reshape(L, P, 2, 4, HD)
    ret, mc, mn = I["state_ret"][0], I["state_mlstm_c"][0], I["state_mlstm_n"][0]
    c65 = np.concatenate([np.concatenate([ret, np.zeros_like(ret[..., :1])], -1), np.concatenate([mc, mn[..., None]], -1)], 2)
    A["s_la"] = c65.reshape(L, 2, 4, 2, HD, HD + 1).transpose(0, 3, 4, 1, 2, 5).reshape(L, P, 2, 4, HD + 1)
    A["s_m"] = I["state_mlstm_m"][0].reshape(L, 8)
    A["ret_decay"] = I["ret_decay"].reshape(L, 8)
    A["w_out"] = I["w_out"]
    A["g_up"] = I["rwkv_g_up"]
    A["gn"] = np.concatenate([I["ret_gn"], I["rwkv_gn"], I["mlstm_gn"]], -1)
    A["ln1"], A["ln2"] = I["ln1"], I["ln2"]
    A["wq"] = I["peer_wq"].reshape(L, KC, P, 16, P).transpose(0, 3, 2, 1, 4)
    A["keys"] = I["peer_keys"].reshape(L, 16, P, P).transpose(0, 3, 1, 2)
    A["ut"] = I["peer_u"].reshape(L, P, NGRP, GRP, KC, P).transpose(0, 2, 5, 3, 4, 1)
    A["pv"] = I["peer_v"].reshape(L, P, P, D_MODEL)
    return {n: np.ascontiguousarray(a) for n, a in A.items()}


OUTS = {"y": (NT, P, D_MODEL), "o_rwkv": (DEPTH, P, 2, 4, HD), "o_la": (DEPTH, P, 2, 4, HD + 1), "o_m": (DEPTH, 8)}
SCRATCH = {"x_work": (NT, P, D_MODEL), "wts": (NBATCH, P, P, NB)}


def kernel(**inputs):
    import numpy as np
    import concourse.bacc as bacc
    from concourse.bass_utils import run_bass_kernel_spmd as run

    I = {n: np.asarray(a) for n, a in inputs.items()}
    arrays = {**layouts(np, I), **constants(np)}
    nc = bacc.Bacc("TRN2", target_bir_lowering=False, num_devices=1)
    D = {n: nc.dram_tensor(n, a.shape, F32, kind="ExternalInput").ap() for n, a in arrays.items()}
    D |= {n: nc.dram_tensor(n, s, F32).ap() for n, s in SCRATCH.items()}
    D |= {n: nc.dram_tensor(n, s, F32, kind="ExternalOutput").ap() for n, s in OUTS.items()}
    build(nc, D)
    out = run(nc, [arrays], core_ids=[0]).results[0]
    y = out["y"]
    rwkv_s = out["o_rwkv"].reshape(DEPTH, 2, HD, 2, 4, HD).transpose(0, 3, 4, 1, 5, 2).reshape(1, DEPTH, 2, 8, HD, HD)
    la = out["o_la"].reshape(DEPTH, 2, HD, 2, 4, HD + 1).transpose(0, 3, 4, 1, 2, 5).reshape(1, DEPTH, 2, 8, HD, HD + 1)
    c = np.ascontiguousarray
    return (c(y[0:1]), c(y[1:].reshape(1, LAT, D_MODEL)), c(la[:, :, :, 0:4, :, 0:HD]), c(rwkv_s),
            c(la[:, :, :, 4:8, :, 0:HD]), c(la[:, :, :, 4:8, :, HD]), c(out["o_m"].reshape(1, DEPTH, 2, 4)))
```
